# Optimizing a Trainium2 kernel written in Bass

```python
import math
import jax, jax.numpy as jnp
from jax import lax
import numpy as np

D_MODEL = 1024
BATCH = 1
SEQ = 512
DEPTH = 2

CHUNK = 64
D_MIX = D_MODEL
GDN_HEADS = 4
GDN_HEAD_DIM = 128
GDN_WIDTH = GDN_HEADS * GDN_HEAD_DIM
GDN_CONV = 4
CONV_WIDTH = D_MIX - GDN_WIDTH
CONV_KERNEL = 31
D_FF = 2816
NORM_EPS = 1e-6

Q0 = 0
K0 = Q0 + GDN_WIDTH
V0 = K0 + GDN_WIDTH
Z0 = V0 + GDN_WIDTH
A0 = Z0 + GDN_WIDTH
B0 = A0 + GDN_HEADS
G0 = B0 + GDN_HEADS
IN_COLS = G0 + 2 * CONV_WIDTH

kernel_name = "hybrid_gdn_conformer_conv_macaron"

def rms_norm(x, g):
    xf = x.astype(jnp.float32)
    y = xf * lax.rsqrt(jnp.mean(xf * xf, axis=-1, keepdims=True) + NORM_EPS)
    return (y * g.astype(jnp.float32)).astype(x.dtype)

def layer_norm(x, g, b):
    xf = x.astype(jnp.float32)
    mu = jnp.mean(xf, axis=-1, keepdims=True)
    xc = xf - mu
    y = xc * lax.rsqrt(jnp.mean(xc * xc, axis=-1, keepdims=True) + NORM_EPS)
    return (y * g.astype(jnp.float32) + b.astype(jnp.float32)).astype(x.dtype)

def causal_depthwise_conv(x, w):
    K, C = w.shape
    xp = jnp.pad(x, ((0, 0), (K - 1, 0), (0, 0)))
    return lax.conv_general_dilated(xp, w[:, None, :].astype(x.dtype), window_strides=(1,), padding='VALID',
                                    dimension_numbers=('NWC', 'WIO', 'NWC'), feature_group_count=C)

def swiglu_ffn(x, w_in, w_out):
    h = x @ w_in
    gate, up = h[..., :D_FF], h[..., D_FF:]
    return (jax.nn.silu(gate) * up) @ w_out

def l2_normalize(x):
    return x * lax.rsqrt(jnp.sum(x * x, axis=-1, keepdims=True) + 1e-6)

def chunk_gated_delta_rule(q, k, v, g, beta):
    Bsz, T, H, Dk = q.shape
    Dv = v.shape[-1]
    N = T // CHUNK

    def blocks(t):
        t = t.reshape((Bsz, N, CHUNK, H) + t.shape[3:])
        return jnp.moveaxis(t, 3, 1)

    q, k, v, g, beta = blocks(q), blocks(k), blocks(v), blocks(g), blocks(beta)
    gc = jnp.cumsum(g, axis=-1)
    idx = jnp.arange(CHUNK)
    lower = idx[:, None] >= idx[None, :]
    strict = idx[:, None] > idx[None, :]
    decay = jnp.exp(jnp.where(lower, gc[..., :, None] - gc[..., None, :], -jnp.inf))
    kb = k * beta[..., None]
    a_mat = jnp.where(strict, jnp.einsum('bhncd,bhnsd->bhncs', kb, k) * decay, 0.0)
    rhs = jnp.concatenate([v * beta[..., None], kb * jnp.exp(gc)[..., None]], axis=-1)
    sol = lax.linalg.triangular_solve(a_mat, rhs, left_side=True, lower=True, unit_diagonal=True)
    u, w = sol[..., :Dv], sol[..., Dv:]
    qk = jnp.einsum('bhncd,bhnsd->bhncs', q, k) * decay
    g_last = gc[..., -1]
    q_dec = q * jnp.exp(gc)[..., None]
    k_dec = k * jnp.exp(g_last[..., None] - gc)[..., None]
    xs = tuple(jnp.moveaxis(t, 2, 0) for t in (q_dec, k_dec, u, w, qk, jnp.exp(g_last)))

    def step(S, inp):
        qd, kd, uc, wc, qkc, eg = inp
        v_new = uc - jnp.einsum('bhcd,bhde->bhce', wc, S)
        o = jnp.einsum('bhcd,bhde->bhce', qd, S) + jnp.einsum('bhcs,bhse->bhce', qkc, v_new)
        S = S * eg[..., None, None] + jnp.einsum('bhcd,bhce->bhde', kd, v_new)
        return S, o

    S0 = jnp.zeros((Bsz, H, Dk, Dv), q.dtype)
    _, o = lax.scan(step, S0, xs)
    o = jnp.transpose(o, (1, 0, 3, 2, 4))
    return o.reshape(Bsz, T, H, Dv)

def gated_deltanet_group(h, conv_w, a_log, dt_bias, out_g):
    Bsz, T, _ = h.shape
    qkv = jax.nn.silu(causal_depthwise_conv(h[..., Q0:Z0], conv_w))
    qkv = qkv.astype(jnp.float32).reshape(Bsz, T, 3, GDN_HEADS, GDN_HEAD_DIM)
    q = l2_normalize(qkv[:, :, 0]) * (GDN_HEAD_DIM ** -0.5)
    k = l2_normalize(qkv[:, :, 1])
    v = qkv[:, :, 2]
    a = h[..., A0:B0].astype(jnp.float32)
    b = h[..., B0:G0].astype(jnp.float32)
    g = -jnp.exp(a_log.astype(jnp.float32)) * jax.nn.softplus(a + dt_bias.astype(jnp.float32))
    beta = jax.nn.sigmoid(b)
    o = chunk_gated_delta_rule(q, k, v, g, beta)
    z = h[..., Z0:A0].astype(jnp.float32).reshape(Bsz, T, GDN_HEADS, GDN_HEAD_DIM)
    o = o * lax.rsqrt(jnp.mean(o * o, axis=-1, keepdims=True) + NORM_EPS) * out_g.astype(jnp.float32)
    o = o * jax.nn.silu(z)
    return o.reshape(Bsz, T, GDN_WIDTH).astype(h.dtype)

def conformer_conv_group(h, dw_w, dw_b, ln_g, ln_b):
    glu = h[..., G0:G0 + CONV_WIDTH] * jax.nn.sigmoid(h[..., G0 + CONV_WIDTH:IN_COLS])
    u = causal_depthwise_conv(glu, dw_w) + dw_b
    return jax.nn.silu(layer_norm(u, ln_g, ln_b))

def setup_inputs(seed: int = 0) -> dict:
    key = jax.random.key(seed)
    ks = jax.random.split(key, 24)
    L, D = DEPTH, D_MODEL
    nrm = lambda k, s, fan: jax.random.normal(k, s, jnp.float32) * (fan ** -0.5)
    gain = lambda k, s: 1.0 + 0.05 * jax.random.normal(k, s, jnp.float32)
    dt = jnp.exp(jax.random.uniform(ks[9], (L, GDN_HEADS), jnp.float32, math.log(1e-3), math.log(1e-1)))
    return {
        "x": jax.random.normal(ks[0], (BATCH, SEQ, D), jnp.float32),
        "ffn1_norm_pre": gain(ks[1], (L, D)),
        "ffn1_w_in": nrm(ks[2], (L, D, 2 * D_FF), D),
        "ffn1_w_out": nrm(ks[3], (L, D_FF, D), D_FF),
        "ffn1_norm_post": gain(ks[4], (L, D)),
        "mix_norm_pre": gain(ks[5], (L, D)),
        "mix_w_in": nrm(ks[6], (L, D, IN_COLS), D),
        "gdn_conv_w": nrm(ks[7], (L, GDN_CONV, 3 * GDN_WIDTH), GDN_CONV),
        "gdn_a_log": jnp.log(jax.random.uniform(ks[8], (L, GDN_HEADS), jnp.float32, 1.0, 16.0)),
        "gdn_dt_bias": dt + jnp.log(-jnp.expm1(-dt)),
        "gdn_out_norm": gain(ks[10], (L, GDN_HEAD_DIM)),
        "cm_dw_w": nrm(ks[11], (L, CONV_KERNEL, CONV_WIDTH), CONV_KERNEL),
        "cm_dw_b": 0.02 * jax.random.normal(ks[12], (L, CONV_WIDTH), jnp.float32),
        "cm_ln_g": gain(ks[13], (L, CONV_WIDTH)),
        "cm_ln_b": 0.02 * jax.random.normal(ks[14], (L, CONV_WIDTH), jnp.float32),
        "mix_w_out": nrm(ks[15], (L, D_MIX, D), D_MIX),
        "mix_norm_post": gain(ks[16], (L, D)),
        "ffn2_norm_pre": gain(ks[17], (L, D)),
        "ffn2_w_in": nrm(ks[18], (L, D, 2 * D_FF), D),
        "ffn2_w_out": nrm(ks[19], (L, D_FF, D), D_FF),
        "ffn2_norm_post": gain(ks[20], (L, D)),
        "block_norm": gain(ks[21], (L, D)),
    }

def reference(x, ffn1_norm_pre, ffn1_w_in, ffn1_w_out, ffn1_norm_post, mix_norm_pre, mix_w_in,
              gdn_conv_w, gdn_a_log, gdn_dt_bias, gdn_out_norm, cm_dw_w, cm_dw_b, cm_ln_g, cm_ln_b,
              mix_w_out, mix_norm_post, ffn2_norm_pre, ffn2_w_in, ffn2_w_out, ffn2_norm_post, block_norm):
    for l in range(DEPTH):
        h = swiglu_ffn(rms_norm(x, ffn1_norm_pre[l]), ffn1_w_in[l], ffn1_w_out[l])
        x = x + 0.5 * rms_norm(h, ffn1_norm_post[l])
        h = rms_norm(x, mix_norm_pre[l]) @ mix_w_in[l]
        o_gdn = gated_deltanet_group(h, gdn_conv_w[l], gdn_a_log[l], gdn_dt_bias[l], gdn_out_norm[l])
        o_cm = conformer_conv_group(h, cm_dw_w[l], cm_dw_b[l], cm_ln_g[l], cm_ln_b[l])
        h = jnp.concatenate([o_gdn, o_cm], axis=-1) @ mix_w_out[l]
        x = x + rms_norm(h, mix_norm_post[l])
        h = swiglu_ffn(rms_norm(x, ffn2_norm_pre[l]), ffn2_w_in[l], ffn2_w_out[l])
        x = x + 0.5 * rms_norm(h, ffn2_norm_post[l])
        x = rms_norm(x, block_norm[l])
    return x


_drawn_inputs = setup_inputs


def setup_inputs(seed=0):
    import zlib

    import numpy as np

    out = dict(_drawn_inputs(seed))
    spreads = {}
    factors = {'cm_ln_b': 3.093}
    for name, (base, spread) in spreads.items():
        noise = np.random.default_rng([zlib.crc32(name.encode()), seed]).standard_normal(out[name].shape)
        drawn = base * np.exp(spread * noise) if base else spread * noise
        out[name] = __import__('jax').numpy.asarray(drawn.astype(out[name].dtype))
    for name, factor in factors.items():
        out[name] = (out[name] * factor).astype(out[name].dtype)
    return out
```

```python
from contextlib import ExitStack

import concourse.bass as bass
from concourse import mybir

F32 = mybir.dt.float32
F32R = mybir.dt.float32r
BF16 = mybir.dt.bfloat16
ALU = mybir.AluOpType
ACT = mybir.ActivationFunctionType
AX_X = mybir.AxisListType.X

P = 128
SLOTS = 4
EPS = 1e-6


class Steps:

    def __init__(self, eng, sem):
        self.eng, self.sem, self.n = eng, sem, 0

    def done(self, ins):
        self.n += 1
        ins.then_inc(self.sem, 1)
        return self.n

    def need(self, n):
        self.eng.wait_ge(self.sem, n)

    def link(self, ins):
        self.need(self.done(ins))


def trunk_kernel(nc, x, ffn1_norm_pre, ffn1_w_in, ffn1_w_out, ffn1_norm_post, mix_norm_pre, mix_w_in,
                 gdn_conv_w, gdn_a_log, gdn_dt_bias, gdn_out_norm, cm_dw_w, cm_dw_b, cm_ln_g, cm_ln_b,
                 mix_w_out, mix_norm_post, ffn2_norm_pre, ffn2_w_in, ffn2_w_out, ffn2_norm_post,
                 block_norm, out):
    L, D = ffn1_norm_pre.shape
    T = x.shape[1]
    FF = ffn1_w_out.shape[1]
    H = gdn_a_log.shape[1]
    DH = gdn_out_norm.shape[1]
    GW = H * DH
    GTAPS, CTAPS = gdn_conv_w.shape[1], cm_dw_w.shape[1]
    CW = cm_dw_w.shape[2]
    KD = D // P
    KF = FF // P
    NC = T // P
    CT = CW // P
    assert (KD, KF, NC, H, CT, DH, T) == (8, 22, 4, 4, 4, P, 512)
    K0, V0, Z0, A0 = GW, 2 * GW, 3 * GW, 4 * GW
    G0 = A0 + 2 * H

    IN_U = 2 * KF
    OUT_PARTS = [(0, 8), (8, 7), (15, 7)]
    FFN_U = IN_U + len(OUT_PARTS) * KD
    MIX_IN_U = 2 * CT + 4 * H
    MIX_U = MIX_IN_U + KD
    UNITS = 2 * FFN_U + MIX_U
    UBASE = [0, FFN_U + MIX_U]
    MBASE = FFN_U
    assert UNITS % SLOTS == 0 and FFN_U % SLOTS == 0 and MIX_U % SLOTS == 0
    PER_SLOT = UNITS // SLOTS
    NX, NXS, NSQ, NST, NY, NP = 4 * KD, 3 * KD, 7 * KD, 7, 3 * KD, 2 * KF

    GAINS = [ffn1_norm_pre, ffn1_norm_post, mix_norm_pre, mix_norm_post, ffn2_norm_pre, ffn2_norm_post,
             block_norm]
    G_F1PRE, G_F1POST, G_MPRE, G_MPOST, G_F2PRE, G_F2POST, G_BLOCK = range(0, 7 * KD, KD)
    C_QKV = 7 * KD
    C_DWB = C_QKV + GTAPS * 3 * H
    C_LNG, C_LNB, C_OUT = C_DWB + CT, C_DWB + 2 * CT, C_DWB + 3 * CT
    ROWS_A = C_OUT + 1
    ROWS_B = CTAPS * CT
    C_DW = ROWS_A
    NCONST = ROWS_A + ROWS_B
    assert ROWS_A <= P and ROWS_B <= P

    base = -(-nc.sbuf_base // 32) * 32
    XT_B = T * 4

    def at(name, shape, dt, offset):
        return nc.alloc_sbuf_tensor_at(name, shape, dt, offset=base + offset)

    o_x = 0
    o_xh = o_x + KD * XT_B
    o_xl = o_xh + KD * XT_B
    o_raw = o_xl + KD * XT_B
    o_wh = o_raw + SLOTS * 8 * P * 4
    o_wl = o_wh + SLOTS * 8 * P * 4
    o_h = o_wl + SLOTS * 8 * P * 4
    o_tmp = o_h + 2 * KF * XT_B
    o_sq = o_tmp + 5 * XT_B
    o_rs = o_sq + 2 * XT_B
    o_c = o_rs + XT_B

    xt = at("xt", [P, KD, T], F32, o_x)
    xh = at("xh", [P, KD, T], F32R, o_xh)
    xl = at("xl", [P, KD, T], F32R, o_xl)
    yg = at("yg", [P, KD, T], F32, o_xh)
    raw = at("raw", [P, SLOTS, 8, P], F32, o_raw)
    wh = at("wh", [P, SLOTS, 8, P], F32R, o_wh)
    wl = at("wl", [P, SLOTS, 8, P], F32R, o_wl)
    hh = at("hh", [P, KF, T], F32R, o_h)
    hl = at("hl", [P, KF, T], F32R, o_h + KF * XT_B)
    gs = at("gs", [P, 2, T], F32, o_tmp)
    us = at("us", [P, 2, T], F32, o_tmp + 2 * XT_B)
    hf = at("hf", [P, T], F32, o_tmp + 4 * XT_B)
    diag = at("diag", [P, NC, P], F32, o_tmp + 4 * XT_B)
    upd = at("upd", [P, 2, T], F32, o_tmp)
    sqr = at("sqr", [P, 2, T], F32, o_sq)
    rs = at("rs", [P, T], F32, o_rs)
    xin = at("xin", [P, NC, D], F32, o_h)

    kT = at("kT", [P, H, T], F32, o_h)
    vT = at("vT", [P, H, T], F32, o_h + 8192)
    kdec = at("kdec", [P, H, NC, P], F32, o_h + 8192)
    qT = at("qT", [P, H, T], F32, o_h + 16384)
    zT = at("zT", [P, H, T], F32, o_h + 24576)
    PADC = CTAPS - 1
    glu = at("glu", [P, CT, PADC + T], F32, o_h + 32768)
    u = at("u", [P, CT, T], F32, o_h + 41472)
    ch = at("ch", [P, KD, T], F32R, o_h + 49664)
    cl = at("cl", [P, KD, T], F32R, o_h + 66048)
    kbT = at("kbT", [P, H, T], F32, o_h + 49664)
    vb = at("vb", [P, H, NC, P], F32, o_h + 66048)
    pm = at("pm", [P, H * NC, 64], F32, o_h + 82432)
    o_gate = o_h + 86528
    GN = ["ab", "xa", "na", "lnv", "g", "eb", "beta", "egc", "egl", "dgl", "ekd", "bk", "kd", "rq8", "ss",
          "rq", "rk", "oss", "orr"]
    gt = {}
    for n, name in enumerate(GN):
        w = 32
        gt[name] = at("gate_" + name, [P, w], F32, o_gate + 128 * n)
    assert 128 * len(GN) <= 3584
    Bm = at("Bm", [P, H, NC, P], F32, o_xh)
    QK = at("QK", [P, H, NC, P], F32, o_xh + 8192)
    Tm = at("Tm", [P, H, NC, P], F32, o_xh + 16384)
    Dm = at("Dm", [P, H, NC, P], F32, o_xh + 16384)
    on = at("on", [P, H, NC, P], F32, o_xh + 16384)
    Um = at("Um", [P, H, NC, P], F32, o_xh + 24576)
    PADG = GTAPS - 1
    pre = at("pre", [P, PADG + T], F32, o_tmp)
    cacc = at("cacc", [P, 2, T], F32, o_tmp + 2080)
    ga = at("ga", [P, T], F32, o_h + 82432)
    gb = at("gb", [P, T], F32, o_h + 82432 + XT_B)
    Wm = at("Wm", [P, 2, NC, P], F32, o_tmp)
    St = at("St", [P, H, P], F32, o_tmp)
    Xd = at("Xd", [P, H, P], F32, o_tmp + XT_B)
    vn = at("vn", [P, H, P], F32, o_tmp + 2 * XT_B)
    oq = at("oq", [P, H, P], F32, o_tmp + 3 * XT_B)
    sd = at("sd", [P, H, P], F32, o_tmp + 4 * XT_B)
    co = [o_c]

    def const(name, shape, dt=F32, size=4):
        n = size
        for s in shape[1:]:
            n *= s
        t = at(name, shape, dt, co[0])
        co[0] += -(-n // 32) * 32
        return t

    ident = const("ident", [P, P])
    ones = const("ones", [P, P])
    upper = const("upper", [P, P])
    lowst = const("lowst", [P, P])
    LEVELS = [1, 2, 4, 8, 16, 32, 64]
    lmask = const("lmask", [P, 6, 64], BF16, 2)
    call = const("call", [P, L, NCONST])
    cur = const("cur", [P, NCONST])
    hcall = const("hcall", [P, L, 2, H])
    hcur = const("hcur", [P, 2, H])
    wabr = const("wabr", [P, L, KD, 2 * H])
    wabf = const("wabf", [P, KD, 2 * H])
    rcol = const("rcol", [P, NC])
    rsq = const("rsq", [P, NC])
    rmix = const("rmix", [P, NC])
    eps = const("eps", [P, 1])
    zero4 = const("zero4", [P, 2 * NC])
    YB = 4
    crows = at("crows", [P, L, 2, P], F32, o_raw)
    assert base + co[0] <= nc.sbuf_usable_end, (base + co[0], nc.sbuf_usable_end)

    ctx = ExitStack()
    with ctx:
        def psum(name, shape):
            return ctx.enter_context(nc.psum_tensor(name, shape, F32))

        res = psum("res", [P, 4, T])
        stat = psum("stat", [P, T])
        bc = psum("bc", [P, T])
        pq = psum("pq", [P, 2, T])

        def sem(name):
            return ctx.enter_context(nc.semaphore(name))

        raw_full = [sem(f"raw_full{i}") for i in range(SLOTS)]
        hi_full, lo_full, unit_done = sem("hi_full"), sem("lo_full"), sem("unit_done")
        s_load, s_rows, s_heads = sem("s_load"), sem("s_rows"), sem("s_heads")
        s_mask, s_seed, s_cc, s_seedv = sem("s_mask"), sem("s_seed"), sem("s_cc"), sem("s_seedv")
        s_xturn, s_cturn, s_negA = sem("s_xturn"), sem("s_cturn"), sem("s_negA")
        x_ready, xh_ready, xs_ready = sem("x_ready"), sem("xh_ready"), sem("xs_ready")
        cur_ready = sem("cur_ready")
        sq_ready, sq_used = sem("sq_ready"), sem("sq_used")
        ssq_full, root_ready, diag_ready, bc_full = sem("ssq_full"), sem("root_ready"), sem("diag_ready"), sem("bc_full")
        rs_ready = sem("rs_ready")
        gate_scaled, pair_free, silu_done, h_ready = sem("gate_scaled"), sem("pair_free"), sem("silu_done"), sem("h_ready")
        y_done = sem("y_done")
        dve_step, pair_step = sem("dve_step"), sem("pair_step")
        mix_free = sem("mix_free")
        sig_ready, cv_ready, act_kvqz, gate_hi = sem("sig_ready"), sem("cv_ready"), sem("act_kvqz"), sem("gate_hi")
        u_ready, usum_full, mu_ready, mubc_full, uc_ready, usq_ready, vsum_full, uroot, udiag, uvbc_full, un_ready = [
            sem(n) for n in ("u_ready", "usum_full", "mu_ready", "mubc_full", "uc_ready", "usq_ready", "vsum_full",
                             "uroot", "udiag", "uvbc_full", "un_ready")]
        us_ready, uh_ready, cmix_ready = sem("us_ready"), sem("uh_ready"), sem("cmix_ready")
        wab_ready = sem("wab_ready")
        ab_full, na_ready, ln_ready, g_ready, gc_full, egc_ready, dgl_ready, ekd_ready = [
            sem(n) for n in ("ab_full", "na_ready", "ln_ready", "g_ready", "gc_full", "egc_ready", "dgl_ready",
                             "ekd_ready")]
        l2_sq, l2_used, l2_full, l2_root, scal_ready = [sem(n) for n in ("l2_sq", "l2_used", "l2_full", "l2_root", "scal_ready")]
        w_ready, e_full, d_exp, d_ready = sem("w_ready"), sem("e_full"), sem("d_exp"), sem("d_ready")
        job_full, vt_free, kt_free, kb_free, b_free, qk_free = [
            sem(n) for n in ("job_full", "vt_free", "kt_free", "kb_free", "b_free", "qk_free")]
        u1_ready, t1_full, t_ready, p_full, pm_ready, q_full, t_upd, tt_full, u_upd = [
            sem(n) for n in ("u1_ready", "t1_full", "t_ready", "p_full", "pm_ready", "q_full", "t_upd", "tt_full",
                             "u_upd")]
        ks_full, xd_ready, vn_full, vn_ready, o_full, o_free, su_full, s_ready = [
            sem(n) for n in ("ks_full", "xd_ready", "vn_full", "vn_ready", "o_full", "o_free", "su_full", "s_ready")]
        osq_ready, oss_ready, oroot, on_ready, ot_full, gm_ready, gh_ready = [
            sem(n) for n in ("osq_ready", "oss_ready", "oroot", "on_ready", "ot_full", "gm_ready", "gh_ready")]
        y_turn, y_copied, s_out = sem("y_turn"), sem("y_copied"), sem("s_out")

        XR0 = KD
        ffn_w = [(ffn1_w_in, ffn1_w_out), (ffn2_w_in, ffn2_w_out)]
        block = ctx.enter_context(nc.Block())

        @block.sync
        def _(sp):
            for c in range(NC):
                sp.dma_start(xin[:, c, :], x[0, c * P:(c + 1) * P, :]).then_inc(s_load, 16)
            for l in range(L):
                rows = [(0, G_ * KD, g[l].rearrange("(r p) -> r p", p=P)) for G_, g in enumerate(GAINS)]
                rows += [(0, C_QKV, gdn_conv_w[l].rearrange("k (r p) -> (k r) p", p=P)),
                         (0, C_DWB, cm_dw_b[l].rearrange("(r p) -> r p", p=P)),
                         (0, C_LNG, cm_ln_g[l].rearrange("(r p) -> r p", p=P)),
                         (0, C_LNB, cm_ln_b[l].rearrange("(r p) -> r p", p=P)),
                         (0, C_OUT, gdn_out_norm[l].rearrange("(r p) -> r p", p=P)),
                         (1, 0, cm_dw_w[l].rearrange("k (r p) -> (k r) p", p=P))]
                for which, r0, src in rows:
                    sp.dma_start(crows[r0:r0 + src.shape[0], l, which, :], src).then_inc(s_rows, 16)
                sp.dma_start(hcall[:, l, 0, :], gdn_a_log[l:l + 1, :].broadcast_to([P, H])).then_inc(s_heads, 16)
                sp.dma_start(hcall[:, l, 1, :], gdn_dt_bias[l:l + 1, :].broadcast_to([P, H])).then_inc(s_heads, 16)
                sp.dma_start(wabr[:, l, :, :],
                             mix_w_in[l].rearrange("(k p) c -> p k c", p=P)[:, :, A0:G0]).then_inc(s_heads, 16)
            sp.wait_ge(s_cc, 2 * L)

            def load(n, slot, src, l):
                sp.wait_ge(lo_full, l * UNITS + n + 1)
                sp.dma_start(raw[:, slot, 0:src.shape[1], :], src).then_inc(raw_full[slot], 16)

            with sp.Fori(0, L) as l:
                def ffn(f):
                    w_in = ffn_w[f][0].rearrange("l (k p) c -> l p k c", p=P)
                    w_out = ffn_w[f][1].rearrange("l (k p) c -> l p k c", p=P)
                    with sp.Fori(0, KF // 2) as i:
                        for q in range(2):
                            for half in range(2):
                                col = i * (2 * P) + (q * P + half * FF)
                                load(i * 4 + (UBASE[f] + 2 * q + half), 2 * q + half,
                                     w_in[l, :, :, bass.ds(col, P)], l)
                    with sp.Fori(0, KD // 4) as i:
                        for q in range(4):
                            for part, (k0, nk) in enumerate(OUT_PARTS):
                                n = q * 3 + part
                                load(i * 12 + (UBASE[f] + IN_U + n), n % SLOTS,
                                     w_out[l, :, k0:k0 + nk, bass.ds(i * (4 * P) + q * P, P)], l)

                ffn(0)
                w_mix = mix_w_in.rearrange("l (k p) c -> l p k c", p=P)
                with sp.Fori(0, CT // 2) as i:
                    for q in range(4):
                        col = i * (2 * P) + (G0 + (q // 2) * P + (q % 2) * CW)
                        load(i * 4 + (MBASE + q), q, w_mix[l, :, :, bass.ds(col, P)], l)
                for n0, col0, step in ((2 * CT, K0, V0 - K0), (2 * CT + 2 * H, 0, Z0)):
                    with sp.Fori(0, 2) as i:
                        for h in range(H):
                            load(i * 4 + (MBASE + n0 + h), h, w_mix[l, :, :, bass.ds(i * step + (col0 + h * P), P)], l)
                w_mo = mix_w_out.rearrange("l (k p) c -> l p k c", p=P)
                with sp.Fori(0, KD // 4) as i:
                    for q in range(4):
                        load(i * 4 + (MBASE + MIX_IN_U + q), q, w_mo[l, :, :, bass.ds(i * (4 * P) + q * P, P)], l)
                ffn(1)
            for c in range(NC):
                sp.wait_ge(y_copied, 2 * (c + 1))
                sp.dma_start(out[0, c * P:(c + 1) * P, :], xin[:, c, :]).then_inc(s_out, 16)
            sp.wait_ge(s_out, 16 * NC)

        @block.gpsimd
        def _(pool):
            pool.memset(ident[:], 0.0).then_inc(s_seed, 1)
            pool.memset(ones[:], 1.0).then_inc(s_seed, 1)
            pool.memset(eps[:], EPS).then_inc(s_seed, 1)
            pool.memset(lmask[:], 1.0).then_inc(s_seed, 1)
            pool.wait_ge(s_seed, 4)
            pool.affine_select(out=ident[:], in_=ident[:], compare_op=ALU.not_equal, fill=1.0, base=0,
                               pattern=[[-1, P]], channel_multiplier=1).then_inc(s_mask, 1)
            pool.affine_select(out=upper[:], in_=ones[:], compare_op=ALU.is_ge, fill=0.0, base=0,
                               pattern=[[1, P]], channel_multiplier=-1).then_inc(s_mask, 1)
            pool.affine_select(out=lowst[:], in_=ones[:], compare_op=ALU.is_ge, fill=0.0, base=-1,
                               pattern=[[-1, P]], channel_multiplier=1).then_inc(s_mask, 1)
            for n, s in enumerate(LEVELS[1:]):
                v = lmask[:, n, :].rearrange("p (b e) -> p b e", e=s)
                pool.affine_select(out=v, in_=v, compare_op=ALU.is_ge, fill=0.0, base=-s,
                                   pattern=[[-2 * s, 64 // s], [0, s]], channel_multiplier=1).then_inc(s_mask, 1)
                pool.wait_ge(s_mask, 4 + 2 * n)
                pool.affine_select(out=v, in_=v, compare_op=ALU.is_ge, fill=0.0, base=2 * s - 1,
                                   pattern=[[2 * s, 64 // s], [0, s]], channel_multiplier=-1).then_inc(s_mask, 1)
            pool.sem_inc(lo_full, SLOTS)

            def low(n, slot, nk, l):
                pool.wait_ge(hi_full, l * UNITS + n + 1)
                pool.tensor_tensor(wl[:, slot, 0:nk, :], raw[:, slot, 0:nk, :],
                                   wh[:, slot, 0:nk, :].bitcast(F32), ALU.subtract).then_inc(lo_full, 1)

            with pool.Fori(0, L) as l:
                def ffn(f):
                    with pool.Fori(0, KF // 2) as i:
                        for q in range(4):
                            low(i * 4 + (UBASE[f] + q), q, 8, l)
                    with pool.Fori(0, KD // 4) as i:
                        for n in range(12):
                            low(i * 12 + (UBASE[f] + IN_U + n), n % SLOTS, OUT_PARTS[n % 3][1], l)

                ffn(0)
                with pool.Fori(0, MIX_IN_U // 4) as i:
                    for q in range(4):
                        low(i * 4 + (MBASE + q), q, 8, l)
                for h in range(H):
                    pool.wait_ge(d_exp, l * H + h + 1)
                    pool.tensor_tensor(Dm[:, h], Dm[:, h], upper[:].unsqueeze(1).broadcast_to([P, NC, P]),
                                       ALU.mult).then_inc(d_ready, 1)
                with pool.Fori(0, KD // 4) as i:
                    for q in range(4):
                        low(i * 4 + (MBASE + MIX_IN_U + q), q, 8, l)
                ffn(1)

        @block.tensor
        def _(pe):
            pe.sem_inc(unit_done, SLOTS)
            pe.sem_inc(sq_used, 2)
            pe.wait_ge(s_mask, 3)
            pe.wait_ge(s_rows, 16 * 13 * L)
            for l in range(L):
                for which, n in ((0, ROWS_A), (1, ROWS_B)):
                    pe.transpose(pq[:, 0, (2 * l + which) * P:(2 * l + which) * P + n], crows[0:n, l, which, :],
                                 ident[0:n, 0:n]).then_inc(s_cturn, 1)
            pe.wait_ge(s_load, 16 * NC)
            for k in range(KD):
                if k >= 4:
                    pe.wait_ge(x_ready, k - 3)
                for c in range(NC):
                    mm = pe.transpose(res[:, k % 4, c * P:(c + 1) * P], xin[:, c, k * P:(k + 1) * P], ident[:])
                mm.then_inc(s_xturn, 1)

            def tile(bank, slot, j, hi, lo, first, last):
                pe.matmul(res[:, bank, :], wh[:, slot, j, :], hi, start=first, stop=False)
                pe.matmul(res[:, bank, :], wh[:, slot, j, :], lo, start=False, stop=False)
                return pe.matmul(res[:, bank, :], wl[:, slot, j, :], hi, start=False, stop=last)

            def open_sums(n=NC):
                pe.matmul(stat[:, 0:n], ident[:], zero4[:, 0:n], start=True, stop=False, skip_group_check=True)

            def token_sums(sq, col=0, cols=NC):
                for c in range(cols):
                    mm = pe.matmul(stat[:, col + c:col + c + 1], sq[:, c * P:(c + 1) * P], ones[:, 0:1],
                                   start=False, stop=False, skip_group_check=True)
                return mm

            def squares(n, l):
                pe.wait_ge(sq_ready, l * NSQ + n + 1)
                token_sums(sqr[:, n % 2, :]).then_inc(sq_used, 1)

            def spread(q, l):
                pe.wait_ge(diag_ready, l * NST + q + 1)
                pe.matmul(bc[:, :], ones[:], diag[:].rearrange("p c t -> p (c t)"), start=True,
                          stop=True).then_inc(bc_full, 1)

            def first_units(u0, stage, stat_q, sq0, l):
                for k in range(KD):
                    pe.wait_ge(xs_ready, l * NXS + stage * KD + k + 1)
                    for n in range(2):
                        if k == 0:
                            pe.wait_ge(lo_full, l * UNITS + (u0 + n + 1 + SLOTS))
                        mm = tile(n, n, k, xh[:, k, :], xl[:, k, :], k == 0, k == KD - 1)
                        if k == KD - 1:
                            mm.then_inc(unit_done, 1)
                    if k == 0:
                        open_sums()
                    else:
                        squares(sq0 + k - 1, l)
                pe.wait_ge(sq_ready, l * NSQ + sq0 + KD)
                token_sums(sqr[:, (KD - 1) % 2, :]).then_inc(sq_used, 1)
                pe.matmul(stat[:, NC:2 * NC], ident[:], zero4[:, 0:NC], start=False, stop=True,
                          skip_group_check=True).then_inc(ssq_full, 1)
                in_unit(u0 + 2, 2, 2, l)
                spread(stat_q, l)
                in_unit(u0 + 3, 3, 3, l)

            def in_unit(n, slot, bank, l):
                pe.wait_ge(lo_full, l * UNITS + n + (1 + SLOTS))
                for k in range(KD):
                    mm = tile(bank, slot, k, xh[:, k, :], xl[:, k, :], k == 0, k == KD - 1)
                mm.then_inc(unit_done, 1)

            def close_sums():
                pe.matmul(stat[:, NC:2 * NC], ident[:], zero4[:, 0:NC], start=False, stop=True,
                          skip_group_check=True).then_inc(ssq_full, 1)

            def ffn(f, l):
                stage, u0 = 2 * f, UBASE[f]
                first_units(u0, stage, [0, 4][f], [0, 4 * KD][f], l)
                with pe.Fori(1, KF // 2) as i:
                    for q in range(2):
                        pe.wait_ge(pair_free, l * NP + i * 2 + (f * KF + q - 1))
                        for half in range(2):
                            in_unit(i * 4 + (u0 + 2 * q + half), 2 * q + half, 2 * q + half, l)
                open_sums()
                with pe.Fori(0, KD // 4) as i:
                    for q in range(4):
                        if q == 0:
                            pe.wait_ge(h_ready, l * NP + (f * KF + KF - 1))
                        pe.wait_ge(y_done, l * NY + i * 4 + (YB + stage * KD + q - 3))
                        for part, (k0, nk) in enumerate(OUT_PARTS):
                            n = 3 * q + part
                            pe.wait_ge(lo_full, l * UNITS + i * 12 + (u0 + IN_U + n + 1 + SLOTS))
                            for j in range(nk):
                                k = k0 + j
                                if q == 0 and k == KF - 1:
                                    pe.wait_ge(h_ready, l * NP + (f * KF + KF))
                                mm = tile(q, n % SLOTS, j, hh[:, k, :], hl[:, k, :], k == 0, k == KF - 1)
                            mm.then_inc(unit_done, 1)
                        if q > 0:
                            y_squares(i, q - 1, stage, l)
                    y_squares(i, 3, stage, l)
                close_sums()
                spread([1, 5][f], l)

            def y_squares(i, q, stage, l):
                sq0 = (2 * stage + 1) * KD
                pe.wait_ge(sq_ready, l * NSQ + i * 4 + (sq0 + q + 1))
                token_sums(sqr[:, q % 2, :]).then_inc(sq_used, 1)

            pe.wait_ge(s_seedv, 1)
            with pe.Fori(0, L) as l:
                ffn(0, l)
                first_units(MBASE, 1, 2, 2 * KD, l)
                with pe.Fori(1, MIX_IN_U // 4) as i:
                    for q in range(4):
                        pe.wait_ge(mix_free, l * MIX_IN_U + i * 4 + (q - 3))
                        in_unit(i * 4 + (MBASE + q), q, q, l)
                pe.wait_ge(wab_ready, l + 1)
                for c in range(NC):
                    for k in range(KD):
                        for half, src in enumerate((xh, xl)):
                            mm = pe.matmul(stat[:, 64 + c * 2 * H:64 + (c + 1) * 2 * H],
                                           src[:, k, c * P:(c + 1) * P].bitcast(F32), wabf[:, k, :],
                                           start=(k == 0 and half == 0), stop=(k == KD - 1 and half == 1))
                mm.then_inc(ab_full, 1)
                pe.wait_ge(g_ready, l + 1)
                pe.matmul(stat[:, 96:112], upper[:], gt["g"][:, 0:16], start=True, stop=True)
                pe.matmul(stat[:, 112:128], ones[:], gt["g"][:, 0:16], start=True, stop=True).then_inc(gc_full, 1)
                pe.wait_ge(ekd_ready, l + 1)
                pe.wait_ge(u_ready, l + 1)
                for c in range(NC):
                    for t in range(CT):
                        mm = pe.matmul(stat[:, c:c + 1], u[:, t, c * P:(c + 1) * P], ones[:, 0:1],
                                       start=(t == 0), stop=(t == CT - 1))
                mm.then_inc(usum_full, 1)
                pe.wait_ge(mu_ready, l + 1)
                pe.matmul(bc[:, :], ones[:], diag[:].rearrange("p c t -> p (c t)"), start=True,
                          stop=True).then_inc(mubc_full, 1)
                pe.wait_ge(usq_ready, l * CT + CT)
                for c in range(NC):
                    for t in range(CT):
                        mm = pe.matmul(stat[:, c:c + 1], glu[:, t, PADC + c * P:PADC + (c + 1) * P], ones[:, 0:1],
                                       start=(t == 0), stop=(t == CT - 1))
                mm.then_inc(vsum_full, 1)
                pe.wait_ge(udiag, l + 1)
                pe.matmul(bc[:, :], ones[:], diag[:].rearrange("p c t -> p (c t)"), start=True,
                          stop=True).then_inc(uvbc_full, 1)
                for n in range(2 * H):
                    pe.wait_ge(l2_sq, l * 2 * H + n + 1)
                    for c in range(NC):
                        mm = pe.matmul(stat[:, 128 + n * NC + c:129 + n * NC + c], sqr[:, n % 2, c * P:(c + 1) * P],
                                       ones[:, 0:1], start=True, stop=True)
                    mm.then_inc(l2_used, 1)
                pe.wait_ge(mix_free, l * MIX_IN_U + MIX_IN_U)
                for h in range(H):
                    pe.wait_ge(w_ready, l * H + h + 1)
                    pe.matmul(res[:, h, :], lowst[:], Wm[:, h % 2].rearrange("p c t -> p (c t)"), start=True,
                              stop=True).then_inc(e_full, 1)
                for h in range(H):
                    pe.wait_ge(d_exp, l * H + h + 1)
                    for c in range(NC):
                        mm = pe.transpose(res[:, h, c * P:(c + 1) * P], vT[:, h, c * P:(c + 1) * P], ident[:])
                    mm.then_inc(job_full, 1)
                for h in range(H):
                    pe.wait_ge(vt_free, l * H + h + 1)
                    for c in range(NC):
                        mm = pe.transpose(res[:, h, c * P:(c + 1) * P], kT[:, h, c * P:(c + 1) * P], ident[:])
                    mm.then_inc(job_full, 1)
                for h in range(H):
                    pe.wait_ge(kt_free, l * H + h + 1)
                    for c in range(NC):
                        mm = pe.transpose(res[:, h, c * P:(c + 1) * P], Um[:, h, c, :], ident[:])
                    mm.then_inc(job_full, 1)
                for h in range(H):
                    pe.wait_ge(kb_free, l * H + h + 1)
                    for c in range(NC):
                        s = slice(c * P, (c + 1) * P)
                        mm = pe.matmul(res[:, h, s], kT[:, h, s], kbT[:, h, s], start=True, stop=True)
                    mm.then_inc(job_full, 1)
                for h in range(H):
                    pe.wait_ge(b_free, l * H + h + 1)
                    for c in range(NC):
                        s = slice(c * P, (c + 1) * P)
                        mm = pe.matmul(res[:, h, s], kT[:, h, s], qT[:, h, s], start=True, stop=True)
                    mm.then_inc(job_full, 1)
                for h in range(H):
                    pe.wait_ge(u1_ready, l * H + h + 1)
                    pe.wait_ge(qk_free, l * H + h + 1)
                    for c in range(NC):
                        mm = pe.transpose(res[:, h, c * P:(c + 1) * P], Um[:, h, c, :], ident[:])
                    mm.then_inc(t1_full, 1)
                for n, s in enumerate(LEVELS[1:]):
                    for g in range(2):
                        if n == 0:
                            pe.wait_ge(t_ready, l * H + 2 * g + 2)
                        else:
                            pe.wait_ge(u_upd, l * 12 + 2 * (n - 1) + g + 1)
                        for j in range(8):
                            h, c = 2 * g + j // 4, j % 4
                            even = Tm[:, h, c, :].rearrange("p (b two e) -> p b two e", two=2, e=s)[:, :, 0, :]
                            mm = pe.matmul(pq[:, g, j * 64:(j + 1) * 64].rearrange("p (b e) -> p b e", e=s),
                                           Bm[:, h, c, :], even, start=True, stop=True)
                        mm.then_inc(p_full, 1)
                    for g in range(2):
                        pe.wait_ge(pm_ready, l * 12 + 2 * n + g + 1)
                        for j in range(8):
                            h, c = 2 * g + j // 4, j % 4
                            mm = pe.matmul(pq[:, g, j * 64:(j + 1) * 64], Um[:, h, c, :], pm[:, 4 * h + c, :],
                                           start=True, stop=True)
                        mm.then_inc(q_full, 1)
                    for g in range(2):
                        pe.wait_ge(t_upd, l * 12 + 2 * n + g + 1)
                        for j in range(8):
                            h, c = 2 * g + j // 4, j % 4
                            mm = pe.transpose(res[:, h, c * P:(c + 1) * P], Tm[:, h, c, :], ident[:])
                        mm.then_inc(tt_full, 1)
                for g in range(2):
                    pe.wait_ge(u_upd, l * 12 + 10 + g + 1)
                for c in range(NC):
                    s = slice(c * P, (c + 1) * P)
                    if c > 0:
                        pe.wait_ge(s_ready, l * NC + c)
                        for h in range(H):
                            mm = pe.matmul(pq[:, 0, h * P:(h + 1) * P], kbT[:, h, s], St[:, h, :], start=True,
                                           stop=True)
                        mm.then_inc(ks_full, 1)
                    pe.wait_ge(xd_ready, l * NC + c + 1)
                    for h in range(H):
                        mm = pe.matmul(pq[:, 1, h * P:(h + 1) * P], Um[:, h, c, :], Xd[:, h, :], start=True,
                                       stop=True)
                    mm.then_inc(vn_full, 1)
                    if c > 0:
                        pe.wait_ge(o_free, l * NC + c)
                        for h in range(H):
                            pe.matmul(res[:, 2, h * P:(h + 1) * P], qT[:, h, s], St[:, h, :], start=True, stop=True)
                    pe.wait_ge(vn_ready, l * NC + c + 1)
                    for h in range(H):
                        mm = pe.matmul(res[:, 0, h * P:(h + 1) * P], kdec[:, h, c, :], vn[:, h, :], start=True,
                                       stop=True)
                    mm.then_inc(su_full, 1)
                    for h in range(H):
                        mm = pe.matmul(res[:, 3, h * P:(h + 1) * P], QK[:, h, c, :], vn[:, h, :], start=True,
                                       stop=True)
                    mm.then_inc(o_full, 1)
                pe.wait_ge(s_ready, l * NC + NC)
                for h in range(H):
                    pe.wait_ge(on_ready, l * H + h + 1)
                    for c in range(NC):
                        mm = pe.transpose(res[:, h, c * P:(c + 1) * P], on[:, h, c, :], ident[:])
                    mm.then_inc(ot_full, 1)
                pe.wait_ge(cmix_ready, l * CT + CT)
                pe.wait_ge(gm_ready, l * H + H)
                open_sums()
                with pe.Fori(0, KD // 4) as i:
                    for q in range(4):
                        pe.wait_ge(y_done, l * NY + i * 4 + (YB + KD + q - 3))
                        pe.wait_ge(lo_full, l * UNITS + i * 4 + (MBASE + MIX_IN_U + q + 1 + SLOTS))
                        for k in range(KD):
                            mm = tile(q, q, k, ch[:, k, :], cl[:, k, :], k == 0, k == KD - 1)
                        mm.then_inc(unit_done, 1)
                        if q > 0:
                            y_squares(i, q - 1, 1, l)
                    y_squares(i, 3, 1, l)
                close_sums()
                spread(3, l)
                ffn(1, l)
                open_sums()
                for k in range(KD):
                    squares(6 * KD + k, l)
                close_sums()
                spread(6, l)
            pe.wait_ge(x_ready, XR0 + L * NX)
            for c in range(NC):
                for half in range(2):
                    n = 2 * c + half
                    if n >= 4:
                        pe.wait_ge(y_copied, n - 3)
                    for k in range(4):
                        mm = pe.transpose(res[:, n % 4, k * P:(k + 1) * P], xt[:, half * 4 + k, c * P:(c + 1) * P],
                                          ident[:])
                    mm.then_inc(y_turn, 1)

        @block.scalar
        def _(act):
            def high(n, slot, nk, l):
                act.wait_ge(raw_full[slot], l * (16 * PER_SLOT) + _slot_count(n, slot))
                act.wait_ge(unit_done, l * UNITS + n + 1)
                act.activation(wh[:, slot, 0:nk, :], raw[:, slot, 0:nk, :], ACT.Copy).then_inc(hi_full, 1)

            def _slot_count(n, slot):
                return (n - slot) * (16 // SLOTS) + 16

            def root(q, l, ss, dst, scale):
                act.wait_ge(ssq_full, l * NST + q + 1)
                act.activation(dst, ss, ACT.Sqrt, bias=eps[:, 0:1], scale=scale).then_inc(root_ready, 1)

            def inputs(stage, gain, xr, sq0, l):
                for k in range(KD):
                    act.wait_ge(x_ready, l * NX + xr + k + 1)
                    if stage == 0 and k == 0:
                        act.wait_ge(cur_ready, l + 1)
                    act.activation(xh[:, k, :], xt[:, k, :], ACT.Copy,
                                   scale=cur[:, gain + k:gain + k + 1]).then_inc(xh_ready, 1)
                    square(xt[:, k, :], sq0 + k, l)

            def square(src, n, l):
                act.wait_ge(sq_used, l * NSQ + n + 1)
                act.activation(sqr[:, n % 2, :], src, ACT.Square).then_inc(sq_ready, 1)

            def row_out(q, n, l):
                act.wait_ge(bc_full, l * NST + q + 1)
                act.activation(rs[:], bc[:, :], ACT.Copy).then_inc(rs_ready, 1)

            def y_tile(bank, m, gain, scale, stage, l):
                square(res[:, bank, :], (2 * stage + 1) * KD + m, l)
                act.activation(yg[:, m, :], res[:, bank, :], ACT.Copy,
                               scale=cur[:, gain + m:gain + m + 1]).then_inc(y_done, 1)

            def ffn(f, l):
                stage, u0 = 2 * f, UBASE[f]
                inputs(stage, [G_F1PRE, G_F2PRE][f], XR0 + (2 * KD) * f - KD, [0, 4 * KD][f], l)
                root([0, 4][f], l, stat[:, 0:NC], rsq[:], 1.0 / D)
                row_out([0, 4][f], 2 * f, l)

                def pair(i, q, sizes):
                    for half in range(2):
                        n = 2 * q + half
                        high(i * 4 + (u0 + 4 + n) if not isinstance(i, int) else 4 * i + u0 + 4 + n, n, sizes[n], l)
                    act.wait_ge(gate_scaled, l * NP + i * 2 + (f * KF + q + 1))
                    act.activation(gs[:, q, :], gs[:, q, :], ACT.Silu).then_inc(silu_done, 1)

                with act.Fori(0, KF // 2 - 1) as i:
                    for q in range(2):
                        pair(i, q, [8, 8, 8, 8])
                for q in range(2):
                    pair(KF // 2 - 1, q, [OUT_PARTS[n % 3][1] for n in range(4)])
                gain = [G_F1POST, G_F2POST][f]
                for m in range(KD):
                    for part in range(3):
                        v = 3 * m + part + 4
                        if v < 3 * KD:
                            high(u0 + IN_U + v, v % SLOTS, OUT_PARTS[v % 3][1], l)
                        elif f == 0:
                            high(u0 + IN_U + v, v % SLOTS, 8, l)
                    act.wait_ge(unit_done, l * UNITS + (u0 + IN_U + 3 * m + 3 + SLOTS))
                    y_tile(m % 4, m, gain, 1.0, stage, l)
                root([1, 5][f], l, stat[:, 0:NC], rsq[:], 1.0 / D)

            act.sem_inc(y_done, YB)
            act.wait_ge(s_mask, 3)
            act.wait_ge(s_heads, 16 * 3 * L)
            for l in range(L):
                act.activation(hcall[:, l, 0, :], hcall[:, l, 0, :], ACT.Exp).then_inc(s_negA, 1)
            with act.Fori(0, L) as l:
                for n in range(SLOTS):
                    high(n, n, 8, l)
                ffn(0, l)
                inputs(1, G_MPRE, XR0, 2 * KD, l)
                root(2, l, stat[:, 0:NC], rsq[:], 1.0 / D)
                row_out(2, 1, l)
                for r in range(MIX_IN_U):
                    high(MBASE + r + 4, r % SLOTS, 8, l)
                    if r < 2 * CT:
                        if r % 2:
                            act.wait_ge(mix_free, l * MIX_IN_U + r + 1)
                            act.activation(gb[:], gb[:], ACT.Sigmoid).then_inc(sig_ready, 1)
                    elif r < 2 * CT + 3 * H:
                        n = r - 2 * CT
                        act.wait_ge(cv_ready, l * 3 * H + n + 1)
                        act.activation((kT, vT, qT)[n // H][:, n % H, :], cacc[:, n % 2, :],
                                       ACT.Silu).then_inc(act_kvqz, 1)
                    else:
                        n = r - 2 * CT - 3 * H
                        act.wait_ge(mix_free, l * MIX_IN_U + r + 1)
                        act.activation(zT[:, n, :], zT[:, n, :], ACT.Silu).then_inc(act_kvqz, 1)
                act.wait_ge(na_ready, l + 1)
                act.activation(gt["na"][:, 0:16], gt["na"][:, 0:16], ACT.Exp).then_inc(ln_ready, 1)
                act.wait_ge(ln_ready, l * 2 + 1)
                act.activation(gt["eb"][:, 0:16], gt["eb"][:, 0:16], ACT.Exp)
                act.activation(gt["lnv"][:, 0:16], gt["na"][:, 0:16], ACT.Ln, bias=1.0).then_inc(ln_ready, 1)
                act.wait_ge(gc_full, l + 1)
                act.activation(gt["egc"][:, 0:16], stat[:, 96:112], ACT.Exp)
                act.activation(gt["egl"][:, 0:16], stat[:, 112:128], ACT.Exp).then_inc(egc_ready, 1)
                act.wait_ge(dgl_ready, l + 1)
                act.activation(gt["ekd"][:, 0:16], gt["dgl"][:, 0:16], ACT.Exp).then_inc(ekd_ready, 1)
                for t in range(CT):
                    act.wait_ge(uc_ready, l * CT + t + 1)
                    act.activation(glu[:, t, PADC:], u[:, t, :], ACT.Square).then_inc(usq_ready, 1)
                act.wait_ge(vsum_full, l + 1)
                act.activation(rsq[:], stat[:, 0:NC], ACT.Sqrt, bias=eps[:, 0:1], scale=1.0 / CW).then_inc(uroot, 1)
                for t in range(CT):
                    act.wait_ge(un_ready, l * CT + t + 1)
                    act.activation(u[:, t, :], u[:, t, :], ACT.Silu, bias=cur[:, C_LNB + t:C_LNB + t + 1],
                                   scale=cur[:, C_LNG + t:C_LNG + t + 1]).then_inc(us_ready, 1)
                    act.wait_ge(us_ready, l * CT + t + 1)
                    act.activation(ch[:, H + t, :], u[:, t, :], ACT.Copy).then_inc(uh_ready, 1)
                for n in range(2 * H):
                    if n >= 2:
                        act.wait_ge(l2_used, l * 2 * H + n - 1)
                    src = (kT if n < H else qT)[:, n % H, :]
                    act.activation(sqr[:, n % 2, :], src, ACT.Square).then_inc(l2_sq, 1)
                act.wait_ge(l2_used, l * 2 * H + 2 * H)
                act.activation(gt["ss"][:, 0:32], stat[:, 128:160], ACT.Sqrt, bias=eps[:, 0:1]).then_inc(l2_root, 1)
                for h in range(H):
                    act.wait_ge(e_full, l * H + h + 1)
                    act.activation(Dm[:, h], res[:, h, :].rearrange("p (c t) -> p c t", c=NC),
                                   ACT.Exp).then_inc(d_exp, 1)
                for h in range(H):
                    act.wait_ge(job_full, l * 5 * H + 2 * H + h + 1)
                    act.activation(kbT[:, h, :], res[:, h, :], ACT.Copy).then_inc(kb_free, 1)
                for h in range(H):
                    act.wait_ge(t1_full, l * H + h + 1)
                    act.activation(Tm[:, h], res[:, h, :].rearrange("p (c t) -> p c t", c=NC),
                                   ACT.Copy).then_inc(t_ready, 1)
                for n in range(6):
                    for g in range(2):
                        act.wait_ge(tt_full, l * 12 + 2 * n + g + 1)
                        act.activation(Um[:, 2 * g:2 * g + 2].rearrange("p h c t -> p h (c t)"),
                                       res[:, 2 * g:2 * g + 2, :], ACT.Copy).then_inc(u_upd, 1)
                for c in range(NC):
                    act.wait_ge(vn_full, l * NC + c + 1)
                    act.activation(vn[:].rearrange("p h e -> p (h e)"), pq[:, 1, :], ACT.Copy).then_inc(vn_ready, 1)
                for h in range(H):
                    act.wait_ge(o_free, l * NC + NC)
                    if h >= 2:
                        act.wait_ge(oss_ready, l * H + h - 1)
                    act.activation(sqr[:, h % 2, :], on[:, h].rearrange("p c e -> p (c e)"),
                                   ACT.Square).then_inc(osq_ready, 1)
                act.wait_ge(oss_ready, l * H + H)
                act.activation(gt["orr"][:, 0:16], gt["oss"][:, 0:16], ACT.Sqrt, bias=eps[:, 0:1],
                               scale=1.0 / DH).then_inc(oroot, 1)
                for h in range(H):
                    act.wait_ge(gh_ready, l * H + h + 1)
                    act.activation(ch[:, h, :], Wm[:, h % 2].rearrange("p c t -> p (c t)"),
                                   ACT.Copy).then_inc(gate_hi, 1)
                for m in range(KD):
                    high(MBASE + MIX_IN_U + m + 4, m % SLOTS, 8, l)
                    y_tile(m % 4, m, G_MPOST, 1.0, 1, l)
                root(3, l, stat[:, 0:NC], rsq[:], 1.0 / D)
                ffn(1, l)
                for k in range(KD):
                    act.wait_ge(x_ready, l * NX + XR0 + 2 * KD + k + 1)
                    square(xt[:, k, :], 6 * KD + k, l)
                root(6, l, stat[:, 0:NC], rsq[:], 1.0 / D)
            for n in range(0, 2 * NC, 2):
                act.wait_ge(y_turn, n + 1)
                act.activation(xin[:, n // 2, 0:T], res[:, n % 4, :], ACT.Copy).then_inc(y_copied, 1)
                act.wait_ge(y_turn, n + 2)
                act.activation(xin[:, n // 2, T:2 * T], res[:, (n + 1) % 4, :], ACT.Copy).then_inc(y_copied, 1)

        @block.vector
        def _(dve):
            st = Steps(dve, dve_step)
            dve.memset(zero4[:], 0.0).then_inc(s_seedv, 1)
            dve.wait_ge(s_mask, 3 + 2 * 6)
            for l in range(L):
                for which, (n, at0) in enumerate(((ROWS_A, 0), (ROWS_B, ROWS_A))):
                    dve.wait_ge(s_cturn, 2 * L)
                    c0 = (2 * l + which) * P
                    dve.tensor_copy(call[:, l, at0:at0 + n], pq[:, 0, c0:c0 + n]).then_inc(s_cc, 1)
            for l in range(L):
                dve.wait_ge(s_negA, l + 1)
                dve.tensor_scalar(hcall[:, l, 0, :], hcall[:, l, 0, :], -1.0, None, ALU.mult).then_inc(s_cc, 1)
            for l in range(L):
                for g in (G_F1POST, G_F2POST):
                    dve.wait_ge(s_cc, 3 * L)
                    dve.tensor_scalar(call[:, l, g:g + KD], call[:, l, g:g + KD], 0.5, None,
                                      ALU.mult).then_inc(s_cc, 1)
            dve.wait_ge(s_cc, 5 * L)
            for k in range(KD):
                dve.wait_ge(s_xturn, k + 1)
                dve.tensor_copy(xt[:, k, :], res[:, k % 4, :]).then_inc(x_ready, 1)

            def row(q, l, col):
                dve.wait_ge(root_ready, l * NST + q + 1)
                st.link(dve.reciprocal(col[:], rsq[:]))
                dve.tensor_tensor(diag[:], ident[:].unsqueeze(1).broadcast_to([P, NC, P]),
                                  col[:].unsqueeze(2).broadcast_to([P, NC, P]), ALU.mult).then_inc(diag_ready, 1)

            def low(k, stage, gain, l):
                dve.wait_ge(xh_ready, l * NXS + stage * KD + k + 1)
                dve.scalar_tensor_tensor(xl[:, k, :], xt[:, k, :], cur[:, gain + k:gain + k + 1],
                                         xh[:, k, :].bitcast(F32), ALU.mult, ALU.subtract).then_inc(xs_ready, 1)

            def residual(k, q, l, xr):
                if k == 0:
                    dve.wait_ge(bc_full, l * NST + q + 1)
                st.link(dve.tensor_tensor(upd[:, k % 2, :], yg[:, k, :], bc[:, :], ALU.mult))
                dve.tensor_tensor(xt[:, k, :], xt[:, k, :], upd[:, k % 2, :], ALU.add).then_inc(x_ready, 1)

            def stage_inputs(stage, q, gain, xr, l):
                for k in range(KD):
                    residual(k, q, l, xr)
                    if k:
                        dve.wait_ge(x_ready, l * NX + xr + k)
                        low(k - 1, stage, gain, l)
                dve.wait_ge(x_ready, l * NX + xr + KD)
                low(KD - 1, stage, gain, l)

            def ffn(f, l):
                row([0, 4][f], l, rcol)
                with dve.Fori(0, KF // 2) as i:
                    dve.sem_clear(pair_step)
                    dve.wait_ge(rs_ready, l * 3 + (2 * f + 1))
                    ps = Steps(dve, pair_step)
                    for q in range(2):
                        n = i * 4 + (UBASE[f] + 2 * q + SLOTS)
                        dve.wait_ge(unit_done, l * UNITS + n + 1)
                        dve.tensor_tensor(gs[:, q, :], res[:, 2 * q, :], rs[:], ALU.mult).then_inc(gate_scaled, 1)
                        dve.wait_ge(unit_done, l * UNITS + n + 2)
                        dve.tensor_tensor(us[:, q, :], res[:, 2 * q + 1, :], rs[:], ALU.mult).then_inc(pair_free, 1)
                        dve.wait_ge(pair_free, l * NP + i * 2 + (f * KF + q + 1))
                        dve.wait_ge(silu_done, l * NP + i * 2 + (f * KF + q + 1))
                        ps.link(dve.tensor_tensor(hf[:], gs[:, q, :], us[:, q, :], ALU.mult))
                        ps.link(dve.tensor_scalar(hh[:, i * 2 + q, :], hf[:], 1.0, None, ALU.mult))
                        dve.tensor_tensor(hl[:, i * 2 + q, :], hf[:], hh[:, i * 2 + q, :].bitcast(F32),
                                          ALU.subtract).then_inc(h_ready, 1)
                dve.wait_ge(h_ready, l * NP + (f + 1) * KF)
                row([1, 5][f], l, rcol)

            with dve.Fori(0, L) as l:
                dve.sem_clear(dve_step)
                st.n = 0
                dve.tensor_copy(wabf[:], wabr[:, l]).then_inc(wab_ready, 1)
                st.link(dve.tensor_copy(hcur[:], hcall[:, l]))
                dve.tensor_copy(cur[:], call[:, l, :]).then_inc(cur_ready, 1)
                dve.wait_ge(cur_ready, l + 1)
                dve.wait_ge(x_ready, l * NX + KD)
                for k in range(KD):
                    low(k, 0, G_F1PRE, l)
                ffn(0, l)
                stage_inputs(1, 1, G_MPRE, XR0, l)
                row(2, l, rmix)
                st.link(dve.memset(pre[:, 0:PADG], 0.0))
                dve.wait_ge(rs_ready, l * 3 + 2)
                st.link(dve.memset(glu[:, :, 0:PADC], 0.0))

                taps = [(t, k) for k in range(CTAPS) for t in range(CT)]
                tap_mark = [0] * CT

                def conv_taps(n):
                    for _ in range(n):
                        if not taps:
                            return
                        t, k = taps.pop(0)
                        w = cur[:, C_DW + k * CT + t:C_DW + k * CT + t + 1]
                        src = glu[:, t, k:k + T]
                        if k == 0:
                            ins = dve.tensor_scalar(u[:, t, :], src, w, cur[:, C_DWB + t:C_DWB + t + 1], ALU.mult,
                                                    ALU.add)
                        else:
                            st.need(tap_mark[t])
                            ins = dve.scalar_tensor_tensor(u[:, t, :], src, w, u[:, t, :], ALU.mult, ALU.add)
                        tap_mark[t] = st.done(ins)

                for r in range(MIX_IN_U):
                    bank = r % 4
                    dve.wait_ge(unit_done, l * UNITS + (MBASE + r + 1 + SLOTS))
                    if r < 2 * CT:
                        if r % 2 == 0:
                            dve.tensor_tensor(ga[:], res[:, bank, :], rs[:], ALU.mult).then_inc(mix_free, 1)
                        else:
                            t = r // 2
                            dve.tensor_tensor(gb[:], res[:, bank, :], rs[:], ALU.mult).then_inc(mix_free, 1)
                            dve.wait_ge(mix_free, l * MIX_IN_U + r + 1)
                            dve.wait_ge(sig_ready, l * CT + t + 1)
                            st.link(dve.tensor_tensor(glu[:, t, PADC:], ga[:], gb[:], ALU.mult))
                    elif r < 2 * CT + 3 * H:
                        n = r - 2 * CT
                        if n:
                            dve.wait_ge(cv_ready, l * 3 * H + n)
                        dve.tensor_tensor(pre[:, PADG:], res[:, bank, :], rs[:], ALU.mult).then_inc(mix_free, 1)
                        dve.wait_ge(mix_free, l * MIX_IN_U + r + 1)
                        which = (1, 2, 0)[n // H]
                        if n >= 2:
                            dve.wait_ge(act_kvqz, l * 4 * H + n - 1)
                        for k in range(GTAPS):
                            w = cur[:, C_QKV + k * 3 * H + which * H + n % H:C_QKV + k * 3 * H + which * H + n % H + 1]
                            src = pre[:, k:k + T]
                            if k == 0:
                                mark = st.done(dve.tensor_scalar(cacc[:, n % 2, :], src, w, None, ALU.mult))
                            else:
                                st.need(mark)
                                ins = dve.scalar_tensor_tensor(cacc[:, n % 2, :], src, w, cacc[:, n % 2, :],
                                                               ALU.mult, ALU.add)
                                if k < GTAPS - 1:
                                    mark = st.done(ins)
                                else:
                                    ins.then_inc(cv_ready, 1)
                            conv_taps(1)
                    else:
                        n = r - 2 * CT - 3 * H
                        dve.tensor_tensor(zT[:, n, :], res[:, bank, :], rs[:], ALU.mult).then_inc(mix_free, 1)
                        dve.wait_ge(mix_free, l * MIX_IN_U + r + 1)
                        conv_taps(6)
                def hc(name):
                    return gt[name][:, 0:16].rearrange("p (h c) -> p h c", h=H)

                dve.wait_ge(ab_full, l + 1)
                st.link(dve.tensor_tensor(gt["ab"][:].rearrange("p (c j) -> p c j", c=NC),
                                          stat[:, 64:96].rearrange("p (c j) -> p c j", c=NC),
                                          rmix[:].unsqueeze(2).broadcast_to([P, NC, 2 * H]), ALU.mult))
                abv = gt["ab"][:].rearrange("p (c j) -> p j c", c=NC)
                st.link(dve.tensor_tensor(hc("xa"), abv[:, 0:H, :], hcur[:, 1, :].unsqueeze(2).broadcast_to([P, H, NC]),
                                          ALU.add))
                st.link(dve.tensor_scalar(hc("eb"), abv[:, H:2 * H, :], -1.0, 87.0, ALU.mult, ALU.min))
                dve.scalar_tensor_tensor(gt["na"][:, 0:16], gt["xa"][:, 0:16], -1.0, gt["xa"][:, 0:16], ALU.mult,
                                         ALU.min).then_inc(na_ready, 1)
                dve.wait_ge(ln_ready, l * 2 + 2)
                st.link(dve.scalar_tensor_tensor(gt["g"][:, 0:16], gt["xa"][:, 0:16], 0.0, gt["lnv"][:, 0:16],
                                                 ALU.max, ALU.add))
                dve.tensor_tensor(hc("g"), hc("g"), hcur[:, 0, :].unsqueeze(2).broadcast_to([P, H, NC]),
                                  ALU.mult).then_inc(g_ready, 1)
                st.link(dve.tensor_scalar(gt["eb"][:, 0:16], gt["eb"][:, 0:16], 1.0, None, ALU.add))
                st.link(dve.reciprocal(gt["beta"][:, 0:16], gt["eb"][:, 0:16]))
                dve.wait_ge(egc_ready, l + 1)
                st.link(dve.tensor_copy(gt["dgl"][:, 16:32], stat[:, 96:112]))
                dve.tensor_tensor(gt["dgl"][:, 0:16], stat[:, 112:128], gt["dgl"][:, 16:32],
                                  ALU.subtract).then_inc(dgl_ready, 1)
                conv_taps(len(taps))
                for t in range(CT):
                    st.need(tap_mark[t])
                dve.sem_inc(u_ready, 1)
                dve.wait_ge(usum_full, l + 1)
                st.link(dve.tensor_scalar(rcol[:], stat[:, 0:NC], 1.0 / CW, None, ALU.mult))
                dve.tensor_tensor(diag[:], ident[:].unsqueeze(1).broadcast_to([P, NC, P]),
                                  rcol[:].unsqueeze(2).broadcast_to([P, NC, P]), ALU.mult).then_inc(mu_ready, 1)
                dve.wait_ge(mubc_full, l + 1)
                for t in range(CT):
                    dve.tensor_tensor(u[:, t, :], u[:, t, :], bc[:, :], ALU.subtract).then_inc(uc_ready, 1)
                dve.wait_ge(uroot, l + 1)
                st.link(dve.reciprocal(rcol[:], rsq[:]))
                dve.tensor_tensor(diag[:], ident[:].unsqueeze(1).broadcast_to([P, NC, P]),
                                  rcol[:].unsqueeze(2).broadcast_to([P, NC, P]), ALU.mult).then_inc(udiag, 1)
                dve.wait_ge(uvbc_full, l + 1)
                dve.wait_ge(uc_ready, l * CT + CT)
                for t in range(CT):
                    dve.tensor_tensor(u[:, t, :], u[:, t, :], bc[:, :], ALU.mult).then_inc(un_ready, 1)
                for t in range(CT):
                    dve.wait_ge(uh_ready, l * CT + t + 1)
                    dve.tensor_tensor(cl[:, H + t, :], u[:, t, :], ch[:, H + t, :].bitcast(F32),
                                      ALU.subtract).then_inc(cmix_ready, 1)
                dve.wait_ge(l2_root, l + 1)
                dve.wait_ge(ekd_ready, l + 1)
                st.link(dve.reciprocal(gt["rk"][:, 0:32], gt["ss"][:, 0:32]))
                dve.tensor_tensor(gt["bk"][:, 0:16], gt["rk"][:, 0:16], gt["beta"][:, 0:16], ALU.mult)
                dve.tensor_scalar(gt["rq8"][:, 0:16], gt["rk"][:, 16:32], float(DH) ** -0.5, None, ALU.mult)
                st.link(dve.tensor_tensor(gt["kd"][:, 0:16], gt["rk"][:, 0:16], gt["ekd"][:, 0:16], ALU.mult))

                def per_token(name, h):
                    return gt[name][:, h * NC:(h + 1) * NC].unsqueeze(2).broadcast_to([P, NC, P])

                for h in range(H):
                    if h >= 2:
                        dve.wait_ge(e_full, l * H + h - 1)
                    dve.tensor_tensor(Wm[:, h % 2], upper[:].unsqueeze(1).broadcast_to([P, NC, P]),
                                      per_token("g", h), ALU.mult).then_inc(w_ready, 1)

                def heads(bank):
                    return res[:, bank, :].rearrange("p (c e) -> p c e", c=NC)

                for h in range(H):
                    dve.wait_ge(job_full, l * 5 * H + h + 1)
                    dve.tensor_tensor(vb[:, h], heads(h), per_token("beta", h), ALU.mult).then_inc(vt_free, 1)
                for h in range(H):
                    dve.wait_ge(job_full, l * 5 * H + H + h + 1)
                    dve.tensor_tensor(kdec[:, h], heads(h), per_token("kd", h), ALU.mult)
                    dve.tensor_tensor(Um[:, h], heads(h), per_token("bk", h), ALU.mult).then_inc(kt_free, 1)
                for h in range(H):
                    dve.wait_ge(d_ready, l * H + h + 1)
                    mark = st.done(dve.tensor_tensor(Dm[:, h], Dm[:, h], per_token("rk", h), ALU.mult))
                st.need(mark)
                for h in range(H):
                    dve.wait_ge(job_full, l * 5 * H + 3 * H + h + 1)
                    dve.tensor_tensor(Bm[:, h], heads(h), Dm[:, h], ALU.mult).then_inc(b_free, 1)
                dve.wait_ge(b_free, l * H + H)
                for h in range(H):
                    uv = Um[:, h].rearrange("p c (b two) -> p (c b) two", two=2)
                    bv = Bm[:, h].rearrange("p c (b two) -> p (c b) two", two=2)
                    idv = ident[:].unsqueeze(1).broadcast_to([P, NC, P])
                    st.link(dve.tensor_copy(Um[:, h], idv))
                    m = ident[:].rearrange("p (b two) -> p b two", two=2)[:, :, 0].unsqueeze(1).broadcast_to([P, NC, 64])
                    st.link(dve.tensor_tensor(pm[:, 4 * h:4 * h + 4, :],
                                              Bm[:, h].rearrange("p c (b two) -> p c b two", two=2)[:, :, :, 1], m,
                                              ALU.mult))
                    odd = Um[:, h].rearrange("p c (b two) -> p c b two", two=2)[:, :, :, 1]
                    dve.tensor_tensor(odd, odd, pm[:, 4 * h:4 * h + 4, :], ALU.subtract).then_inc(u1_ready, 1)
                for h in range(H):
                    dve.wait_ge(job_full, l * 5 * H + 4 * H + h + 1)
                    dve.tensor_tensor(QK[:, h], heads(h), Dm[:, h], ALU.mult).then_inc(qk_free, 1)
                for n, s in enumerate(LEVELS[1:]):
                    for g in range(2):
                        dve.wait_ge(p_full, l * 12 + 2 * n + g + 1)
                        dve.tensor_tensor(pm[:, 8 * g:8 * g + 8, :], pq[:, g, :].rearrange("p (j e) -> p j e", j=8),
                                          lmask[:, n, :].unsqueeze(1).broadcast_to([P, 8, 64]),
                                          ALU.mult).then_inc(pm_ready, 1)
                    for g in range(2):
                        dve.wait_ge(q_full, l * 12 + 2 * n + g + 1)
                        even = Tm[:, 2 * g:2 * g + 2].rearrange("p h c (b two e) -> p (h c b) two e", two=2,
                                                                e=s)[:, :, 0, :]
                        dve.tensor_tensor(even, even, pq[:, g, :].rearrange("p (b e) -> p b e", e=s),
                                          ALU.subtract).then_inc(t_upd, 1)

                def per_head(name, c, n=P):
                    return gt[name][:, 0:16].rearrange("p (h c) -> p h c", h=H)[:, :, c:c + 1].broadcast_to([P, H, P])

                def four(ap):
                    return ap.rearrange("p (h e) -> p h e", h=H)

                for c in range(NC):
                    if c == 0:
                        dve.wait_ge(vt_free, l * H + H)
                        dve.tensor_copy(Xd[:], vb[:, :, c, :]).then_inc(xd_ready, 1)
                    else:
                        dve.wait_ge(ks_full, l * (NC - 1) + c)
                        dve.wait_ge(vn_full, l * NC + c)
                        st.link(dve.tensor_tensor(Xd[:], four(pq[:, 0, :]), per_head("egc", c), ALU.mult))
                        dve.tensor_tensor(Xd[:], vb[:, :, c, :], Xd[:], ALU.subtract).then_inc(xd_ready, 1)
                        if c < NC:
                            mark = st.done(dve.tensor_tensor(sd[:], St[:], per_head("egl", c), ALU.mult))
                    dve.wait_ge(su_full, l * NC + c + 1)
                    if c == 0:
                        dve.tensor_copy(St[:], four(res[:, 0, :])).then_inc(s_ready, 1)
                    else:
                        st.need(mark)
                        dve.tensor_tensor(St[:], sd[:], four(res[:, 0, :]), ALU.add).then_inc(s_ready, 1)
                    dve.wait_ge(o_full, l * NC + c + 1)
                    if c == 0:
                        dve.tensor_tensor(on[:, :, c, :], four(res[:, 3, :]), per_head("rq8", c),
                                          ALU.mult).then_inc(o_free, 1)
                    else:
                        st.link(dve.tensor_tensor(oq[:], four(res[:, 2, :]), per_head("egc", c), ALU.mult))
                        st.link(dve.tensor_tensor(oq[:], oq[:], four(res[:, 3, :]), ALU.add))
                        dve.tensor_tensor(on[:, :, c, :], oq[:], per_head("rq8", c), ALU.mult).then_inc(o_free, 1)
                dve.wait_ge(o_free, l * NC + NC)
                for h in range(H):
                    dve.wait_ge(osq_ready, l * H + h + 1)
                    dve.tensor_reduce(gt["oss"][:, h * NC:(h + 1) * NC],
                                      sqr[:, h % 2, :].rearrange("p (c e) -> p c e", c=NC), AX_X,
                                      ALU.add).then_inc(oss_ready, 1)
                dve.wait_ge(oroot, l + 1)
                st.link(dve.reciprocal(gt["oss"][:, 0:16], gt["orr"][:, 0:16]))
                for h in range(H):
                    dve.tensor_tensor(on[:, h], on[:, h], per_token("oss", h), ALU.mult).then_inc(on_ready, 1)
                def head_low(h):
                    dve.wait_ge(gate_hi, l * H + h + 1)
                    dve.tensor_tensor(cl[:, h, :], Wm[:, h % 2].rearrange("p c t -> p (c t)"),
                                      ch[:, h, :].bitcast(F32), ALU.subtract).then_inc(gm_ready, 1)

                for h in range(H):
                    dve.wait_ge(ot_full, l * H + h + 1)
                    if h == 0:
                        dve.wait_ge(act_kvqz, l * 4 * H + 4 * H)
                    gf = Wm[:, h % 2].rearrange("p c t -> p (c t)")
                    if h >= 2:
                        dve.wait_ge(gm_ready, l * H + h - 1)
                    dve.scalar_tensor_tensor(gf, res[:, h, :], cur[:, C_OUT:C_OUT + 1], zT[:, h, :], ALU.mult,
                                             ALU.mult).then_inc(gh_ready, 1)
                    if h >= 1:
                        head_low(h - 1)
                head_low(H - 1)
                row(3, l, rcol)
                stage_inputs(2, 3, G_F2PRE, XR0 + KD, l)
                ffn(1, l)
                for k in range(KD):
                    residual(k, 5, l, XR0 + 2 * KD)
                    dve.wait_ge(x_ready, l * NX + (XR0 + 2 * KD + k + 1))
                row(6, l, rcol)
                dve.wait_ge(x_ready, l * NX + XR0 + 3 * KD)
                dve.wait_ge(bc_full, l * NST + 7)
                for k in range(KD):
                    dve.scalar_tensor_tensor(xt[:, k, :], xt[:, k, :], cur[:, G_BLOCK + k:G_BLOCK + k + 1], bc[:, :],
                                             ALU.mult, ALU.mult).then_inc(x_ready, 1)
    return nc


_INS = ["x", "ffn1_norm_pre", "ffn1_w_in", "ffn1_w_out", "ffn1_norm_post", "mix_norm_pre", "mix_w_in",
        "gdn_conv_w", "gdn_a_log", "gdn_dt_bias", "gdn_out_norm", "cm_dw_w", "cm_dw_b", "cm_ln_g", "cm_ln_b",
        "mix_w_out", "mix_norm_post", "ffn2_norm_pre", "ffn2_w_in", "ffn2_w_out", "ffn2_norm_post", "block_norm"]


def kernel(**inputs):
    import numpy as _np
    import concourse.bacc as _bacc
    from concourse import mybir as _mybir
    from concourse.bass_utils import run_bass_kernel_spmd as _run

    nc = _bacc.Bacc("TRN2", target_bir_lowering=False, num_devices=1)
    arrays, args = {}, []
    for name in _INS:
        a = _np.ascontiguousarray(inputs[name])
        arrays[f"in_{name}"] = a
        args.append(nc.dram_tensor(f"in_{name}", a.shape, _mybir.dt.from_np(a.dtype), kind="ExternalInput").ap())
    out = nc.dram_tensor("out_dram", arrays["in_x"].shape, _mybir.dt.float32, kind="ExternalOutput").ap()
    trunk_kernel(nc, *args, out)
    r = _run(nc, [arrays], core_ids=[0])
    return r.results[0]["out_dram"]
```

```python
from contextlib import ExitStack

import concourse.bass as bass
from concourse import mybir

F32 = mybir.dt.float32
F32R = mybir.dt.float32r
BF16 = mybir.dt.bfloat16
ALU = mybir.AluOpType
ACT = mybir.ActivationFunctionType
AX_X = mybir.AxisListType.X

P = 128
SLOTS = 4
EPS = 1e-6


class Steps:

    def __init__(self, eng, sem):
        self.eng, self.sem, self.n = eng, sem, 0

    def done(self, ins):
        self.n += 1
        ins.then_inc(self.sem, 1)
        return self.n

    def need(self, n):
        self.eng.wait_ge(self.sem, n)

    def link(self, ins):
        self.need(self.done(ins))


def trunk_kernel(nc, x, ffn1_norm_pre, ffn1_w_in, ffn1_w_out, ffn1_norm_post, mix_norm_pre, mix_w_in,
                 gdn_conv_w, gdn_a_log, gdn_dt_bias, gdn_out_norm, cm_dw_w, cm_dw_b, cm_ln_g, cm_ln_b,
                 mix_w_out, mix_norm_post, ffn2_norm_pre, ffn2_w_in, ffn2_w_out, ffn2_norm_post,
                 block_norm, out):
    L, D = ffn1_norm_pre.shape
    T = x.shape[1]
    FF = ffn1_w_out.shape[1]
    H = gdn_a_log.shape[1]
    DH = gdn_out_norm.shape[1]
    GW = H * DH
    GTAPS, CTAPS = gdn_conv_w.shape[1], cm_dw_w.shape[1]
    CW = cm_dw_w.shape[2]
    KD = D // P
    KF = FF // P
    NC = T // P
    CT = CW // P
    assert (KD, KF, NC, H, CT, DH, T) == (8, 22, 4, 4, 4, P, 512)
    K0, V0, Z0, A0 = GW, 2 * GW, 3 * GW, 4 * GW
    G0 = A0 + 2 * H

    IN_U = 2 * KF
    OUT_PARTS = [(0, 8), (8, 7), (15, 7)]
    FFN_U = IN_U + len(OUT_PARTS) * KD
    MIX_IN_U = 2 * CT + 4 * H
    MIX_U = MIX_IN_U + KD
    UNITS = 2 * FFN_U + MIX_U
    UBASE = [0, FFN_U + MIX_U]
    MBASE = FFN_U
    assert UNITS % SLOTS == 0 and FFN_U % SLOTS == 0 and MIX_U % SLOTS == 0
    PER_SLOT = UNITS // SLOTS
    NXS, NSQ, NST, NY, NP = 3 * KD, 7 * KD, 7, 3 * KD, 2 * KF

    GAINS = [ffn1_norm_pre, ffn1_norm_post, mix_norm_pre, mix_norm_post, ffn2_norm_pre, ffn2_norm_post,
             block_norm]
    G_F1PRE, G_F1POST, G_MPRE, G_MPOST, G_F2PRE, G_F2POST, G_BLOCK = range(0, 7 * KD, KD)
    C_QKV = 7 * KD
    C_DWB = C_QKV + GTAPS * 3 * H
    C_LNG, C_LNB, C_OUT = C_DWB + CT, C_DWB + 2 * CT, C_DWB + 3 * CT
    ROWS_A = C_OUT + 1
    ROWS_B = CTAPS * CT
    C_DW = ROWS_A
    NCONST = ROWS_A + ROWS_B
    assert ROWS_A <= P and ROWS_B <= P

    base = -(-nc.sbuf_base // 32) * 32
    XT_B = T * 4

    def at(name, shape, dt, offset):
        return nc.alloc_sbuf_tensor_at(name, shape, dt, offset=base + offset)

    o_x = 0
    o_xh = o_x + KD * XT_B
    o_xl = o_xh + KD * XT_B
    o_raw = o_xl + KD * XT_B
    o_wh = o_raw + SLOTS * 8 * P * 4
    o_wl = o_wh + SLOTS * 8 * P * 4
    o_h = o_wl + SLOTS * 8 * P * 4
    o_tmp = o_h + 2 * KF * XT_B
    o_sq = o_tmp + 5 * XT_B
    o_rs = o_sq + 2 * XT_B
    o_c = o_rs + XT_B

    xt = at("xt", [P, KD, T], F32, o_x)
    xh = at("xh", [P, KD, T], F32R, o_xh)
    xl = at("xl", [P, KD, T], F32R, o_xl)
    yg = at("yg", [P, KD, T], F32, o_xh)
    raw = at("raw", [P, SLOTS, 8, P], F32, o_raw)
    wh = at("wh", [P, SLOTS, 8, P], F32R, o_wh)
    wl = at("wl", [P, SLOTS, 8, P], F32R, o_wl)
    hh = at("hh", [P, KF, T], F32R, o_h)
    hl = at("hl", [P, KF, T], F32R, o_h + KF * XT_B)
    gs = at("gs", [P, 2, T], F32, o_tmp)
    us = at("us", [P, 2, T], F32, o_tmp + 2 * XT_B)
    hf = at("hf", [P, T], F32, o_tmp + 4 * XT_B)
    diag = at("diag", [P, NC, P], F32, o_tmp + 4 * XT_B)
    acc = at("acc", [P, T], F32, o_tmp + 4 * XT_B)
    upd = at("upd", [P, 2, T], F32, o_tmp)
    sqr = at("sqr", [P, 2, T], F32, o_sq)
    rs = at("rs", [P, T], F32, o_rs)
    xin = at("xin", [P, NC, D], F32, o_h)

    kT = at("kT", [P, H, T], F32, o_h)
    vT = at("vT", [P, H, T], F32, o_h + 8192)
    kdec = at("kdec", [P, H, NC, P], F32, o_h + 8192)
    qT = at("qT", [P, H, T], F32, o_h + 16384)
    zT = at("zT", [P, H, T], F32, o_h + 24576)
    PADC = CTAPS - 1
    glu = at("glu", [P, CT, PADC + T], F32, o_h + 32768)
    u = at("u", [P, CT, T], F32, o_h + 41472)
    ch = at("ch", [P, KD, T], F32R, o_h + 49664)
    cl = at("cl", [P, KD, T], F32R, o_h + 66048)
    ksq = at("ksq", [P, 2 * H, T], F32, o_h + 49664)
    kbT = at("kbT", [P, H, T], F32, o_h + 49664)
    vb = at("vb", [P, H, NC, P], F32, o_h + 66048)
    pm = at("pm", [P, H * NC, 64], F32, o_h + 82432)
    o_gate = o_h + 86528
    GN = ["ab", "xa", "na", "lnv", "g", "eb", "beta", "egc", "egl", "dgl", "ekd", "bk", "kd", "rq8", "ss",
          "rq", "rk", "oss", "orr"]
    gt = {}
    for n, name in enumerate(GN):
        w = 32
        gt[name] = at("gate_" + name, [P, w], F32, o_gate + 128 * n)
    assert 128 * len(GN) <= 3584
    Bm = at("Bm", [P, H, NC, P], F32, o_xh)
    QK = at("QK", [P, H, NC, P], F32, o_xh + 8192)
    Tm = at("Tm", [P, H, NC, P], F32, o_xh + 16384)
    Dm = at("Dm", [P, H, NC, P], F32, o_xh + 16384)
    on = at("on", [P, H, NC, P], F32, o_xh + 16384)
    Um = at("Um", [P, H, NC, P], F32, o_xh + 24576)
    PADG = GTAPS - 1
    pre = at("pre", [P, PADG + T], F32, o_tmp)
    cacc = at("cacc", [P, 2, T], F32, o_tmp + 2080)
    ga = at("ga", [P, T], F32, o_h + 82432)
    gb = at("gb", [P, T], F32, o_h + 82432 + XT_B)
    Wm = at("Wm", [P, 2, NC, P], F32, o_tmp)
    St = at("St", [P, H, P], F32, o_tmp)
    Xd = at("Xd", [P, H, P], F32, o_tmp + XT_B)
    vn = at("vn", [P, H, P], F32, o_tmp + 2 * XT_B)
    oq = at("oq", [P, H, P], F32, o_tmp + 3 * XT_B)
    sd = at("sd", [P, H, P], F32, o_tmp + 4 * XT_B)
    ldiag = at("ldiag", [P, NC, P], F32, o_sq)
    lacc = at("lacc", [P, T], F32, o_sq + XT_B)
    co = [o_c]

    def const(name, shape, dt=F32, size=4):
        n = size
        for s in shape[1:]:
            n *= s
        t = at(name, shape, dt, co[0])
        co[0] += -(-n // 32) * 32
        return t

    ident = const("ident", [P, P])
    ones = const("ones", [P, P])
    upper = const("upper", [P, P])
    lowst = const("lowst", [P, P])
    LEVELS = [1, 2, 4, 8, 16, 32, 64]
    lmask = const("lmask", [P, 6, 64], BF16, 2)
    call = const("call", [P, L, NCONST])
    cur = const("cur", [P, NCONST])
    hcall = const("hcall", [P, L, 2, H])
    hcur = const("hcur", [P, 2, H])
    wabr = const("wabr", [P, L, KD, 2 * H])
    wabh = const("wabh", [P, KD, 2 * H], F32R)
    wabl = const("wabl", [P, KD, 2 * H], F32R)
    gblk = const("gblk", [P, KD])
    rcol = const("rcol", [P, NC])
    rsq = const("rsq", [P, NC])
    rmix = const("rmix", [P, NC])
    eps = const("eps", [P, 1])
    YB = 4
    crows = at("crows", [P, L, 2, P], F32, o_raw)
    assert base + co[0] <= nc.sbuf_usable_end, (base + co[0], nc.sbuf_usable_end)

    ctx = ExitStack()
    with ctx:
        def psum(name, shape):
            return ctx.enter_context(nc.psum_tensor(name, shape, F32))

        res = psum("res", [P, 4, T])
        stat = psum("stat", [P, T])
        bc = psum("bc", [P, T])
        pq = psum("pq", [P, 2, T])

        def sem(name):
            return ctx.enter_context(nc.semaphore(name))

        raw_full = [sem(f"raw_full{i}") for i in range(SLOTS)]
        hi_full, lo_full, unit_done = sem("hi_full"), sem("lo_full"), sem("unit_done")
        s_load, s_rows, s_heads = sem("s_load"), sem("s_rows"), sem("s_heads")
        s_mask, s_seed, s_cc, s_seedv = sem("s_mask"), sem("s_seed"), sem("s_cc"), sem("s_seedv")
        s_seedg, blk_done = sem("s_seedg"), sem("blk_done")
        s_xturn, s_cturn, s_negA = sem("s_xturn"), sem("s_cturn"), sem("s_negA")
        x_turned, xn_ready, upd_ready = sem("x_turned"), sem("xn_ready"), sem("upd_ready")
        x_ready, xh_ready, xs_ready = sem("x_ready"), sem("xh_ready"), sem("xs_ready")
        cur_ready = sem("cur_ready")
        sq_ready, xsum, ysum = sem("sq_ready"), sem("xsum"), sem("ysum")
        ssq_full, root_ready, diag_ready, bc_full = sem("ssq_full"), sem("root_ready"), sem("diag_ready"), sem("bc_full")
        rs_ready = sem("rs_ready")
        gate_scaled, pair_free, silu_done, h_ready = sem("gate_scaled"), sem("pair_free"), sem("silu_done"), sem("h_ready")
        y_done = sem("y_done")
        dve_step, pair_step = sem("dve_step"), sem("pair_step")
        mix_free = sem("mix_free")
        sig_ready, cv_ready, act_kvqz, gate_hi = sem("sig_ready"), sem("cv_ready"), sem("act_kvqz"), sem("gate_hi")
        u_ready, usum_full, mu_ready, mubc_full, uc_ready, usq_ready, vsum_full, uroot, udiag, uvbc_full, un_ready = [
            sem(n) for n in ("u_ready", "usum_full", "mu_ready", "mubc_full", "uc_ready", "usq_ready", "vsum_full",
                             "uroot", "udiag", "uvbc_full", "un_ready")]
        us_ready, uh_ready, cmix_ready = sem("us_ready"), sem("uh_ready"), sem("cmix_ready")
        wab_ready = sem("wab_ready")
        ab_full, na_ready, ln_ready, g_ready, gc_full, egc_ready, dgl_ready, ekd_ready = [
            sem(n) for n in ("ab_full", "na_ready", "ln_ready", "g_ready", "gc_full", "egc_ready", "dgl_ready",
                             "ekd_ready")]
        l2_sq, l2_full, l2_root = sem("l2_sq"), sem("l2_full"), sem("l2_root")
        lsum = sem("lsum")
        w_ready, e_full, d_exp, d_ready = sem("w_ready"), sem("e_full"), sem("d_exp"), sem("d_ready")
        job_full, vt_free, kt_free, kb_free, b_free, qk_free = [
            sem(n) for n in ("job_full", "vt_free", "kt_free", "kb_free", "b_free", "qk_free")]
        u1_ready, t1_full, t_ready, p_full, pm_ready, q_full, t_upd, tt_full, u_upd = [
            sem(n) for n in ("u1_ready", "t1_full", "t_ready", "p_full", "pm_ready", "q_full", "t_upd", "tt_full",
                             "u_upd")]
        ks_full, xd_ready, vn_full, vn_ready, o_full, o_free, su_full, s_ready = [
            sem(n) for n in ("ks_full", "xd_ready", "vn_full", "vn_ready", "o_full", "o_free", "su_full", "s_ready")]
        osq_ready, oss_ready, oroot, on_ready, ot_full, gm_ready, gh_ready = [
            sem(n) for n in ("osq_ready", "oss_ready", "oroot", "on_ready", "ot_full", "gm_ready", "gh_ready")]
        y_turn, y_copied, s_out = sem("y_turn"), sem("y_copied"), sem("s_out")

        NXR = 3 * KD
        NXQ, NYQ = 4 * (KD - 1), 3 * (KD - 1)
        ffn_w = [(ffn1_w_in, ffn1_w_out), (ffn2_w_in, ffn2_w_out)]
        block = ctx.enter_context(nc.Block())

        @block.sync
        def _(sp):
            for c in range(NC):
                sp.dma_start(xin[:, c, :], x[0, c * P:(c + 1) * P, :]).then_inc(s_load, 16)
            for l in range(L):
                rows = [(0, G_ * KD, g[l].rearrange("(r p) -> r p", p=P)) for G_, g in enumerate(GAINS)]
                rows += [(0, C_QKV, gdn_conv_w[l].rearrange("k (r p) -> (k r) p", p=P)),
                         (0, C_DWB, cm_dw_b[l].rearrange("(r p) -> r p", p=P)),
                         (0, C_LNG, cm_ln_g[l].rearrange("(r p) -> r p", p=P)),
                         (0, C_LNB, cm_ln_b[l].rearrange("(r p) -> r p", p=P)),
                         (0, C_OUT, gdn_out_norm[l].rearrange("(r p) -> r p", p=P)),
                         (1, 0, cm_dw_w[l].rearrange("k (r p) -> (k r) p", p=P))]
                for which, r0, src in rows:
                    sp.dma_start(crows[r0:r0 + src.shape[0], l, which, :], src).then_inc(s_rows, 16)
                sp.dma_start(hcall[:, l, 0, :], gdn_a_log[l:l + 1, :].broadcast_to([P, H])).then_inc(s_heads, 16)
                sp.dma_start(hcall[:, l, 1, :], gdn_dt_bias[l:l + 1, :].broadcast_to([P, H])).then_inc(s_heads, 16)
                sp.dma_start(wabr[:, l, :, :],
                             mix_w_in[l].rearrange("(k p) c -> p k c", p=P)[:, :, A0:G0]).then_inc(s_heads, 16)
            sp.wait_ge(s_cc, 2 * L)

            def load(n, slot, src, l):
                sp.wait_ge(lo_full, l * UNITS + n + 1)
                sp.dma_start(raw[:, slot, 0:src.shape[1], :], src).then_inc(raw_full[slot], 16)

            with sp.Fori(0, L) as l:
                def ffn(f):
                    w_in = ffn_w[f][0].rearrange("l (k p) c -> l p k c", p=P)
                    w_out = ffn_w[f][1].rearrange("l (k p) c -> l p k c", p=P)
                    with sp.Fori(0, KF // 2) as i:
                        for q in range(2):
                            for half in range(2):
                                col = i * (2 * P) + (q * P + half * FF)
                                load(i * 4 + (UBASE[f] + 2 * q + half), 2 * q + half,
                                     w_in[l, :, :, bass.ds(col, P)], l)
                    with sp.Fori(0, KD // 4) as i:
                        for q in range(4):
                            for part, (k0, nk) in enumerate(OUT_PARTS):
                                n = q * 3 + part
                                load(i * 12 + (UBASE[f] + IN_U + n), n % SLOTS,
                                     w_out[l, :, k0:k0 + nk, bass.ds(i * (4 * P) + q * P, P)], l)

                ffn(0)
                w_mix = mix_w_in.rearrange("l (k p) c -> l p k c", p=P)
                with sp.Fori(0, CT // 2) as i:
                    for q in range(4):
                        col = i * (2 * P) + (G0 + (q // 2) * P + (q % 2) * CW)
                        load(i * 4 + (MBASE + q), q, w_mix[l, :, :, bass.ds(col, P)], l)
                for n0, col0, step in ((2 * CT, K0, V0 - K0), (2 * CT + 2 * H, 0, Z0)):
                    with sp.Fori(0, 2) as i:
                        for h in range(H):
                            load(i * 4 + (MBASE + n0 + h), h, w_mix[l, :, :, bass.ds(i * step + (col0 + h * P), P)], l)
                w_mo = mix_w_out.rearrange("l (k p) c -> l p k c", p=P)
                with sp.Fori(0, KD // 4) as i:
                    for q in range(4):
                        load(i * 4 + (MBASE + MIX_IN_U + q), q, w_mo[l, :, :, bass.ds(i * (4 * P) + q * P, P)], l)
                ffn(1)
            for c in range(NC):
                sp.wait_ge(y_copied, 2 * (c + 1))
                sp.dma_start(out[0, c * P:(c + 1) * P, :], xin[:, c, :]).then_inc(s_out, 16)
            sp.wait_ge(s_out, 16 * NC)

        @block.gpsimd
        def _(pool):
            pool.memset(ident[:], 0.0).then_inc(s_seed, 1)
            pool.memset(ones[:], 1.0).then_inc(s_seed, 1)
            pool.memset(eps[:], EPS).then_inc(s_seed, 1)
            pool.memset(lmask[:], 1.0).then_inc(s_seed, 1)
            pool.wait_ge(s_seed, 4)
            pool.affine_select(out=ident[:], in_=ident[:], compare_op=ALU.not_equal, fill=1.0, base=0,
                               pattern=[[-1, P]], channel_multiplier=1).then_inc(s_mask, 1)
            pool.affine_select(out=upper[:], in_=ones[:], compare_op=ALU.is_ge, fill=0.0, base=0,
                               pattern=[[1, P]], channel_multiplier=-1).then_inc(s_mask, 1)
            pool.affine_select(out=lowst[:], in_=ones[:], compare_op=ALU.is_ge, fill=0.0, base=-1,
                               pattern=[[-1, P]], channel_multiplier=1).then_inc(s_mask, 1)
            for n, s in enumerate(LEVELS[1:]):
                v = lmask[:, n, :].rearrange("p (b e) -> p b e", e=s)
                pool.affine_select(out=v, in_=v, compare_op=ALU.is_ge, fill=0.0, base=-s,
                                   pattern=[[-2 * s, 64 // s], [0, s]], channel_multiplier=1).then_inc(s_mask, 1)
                pool.wait_ge(s_mask, 4 + 2 * n)
                pool.affine_select(out=v, in_=v, compare_op=ALU.is_ge, fill=0.0, base=2 * s - 1,
                                   pattern=[[2 * s, 64 // s], [0, s]], channel_multiplier=-1).then_inc(s_mask, 1)
            pool.sem_inc(lo_full, SLOTS)

            def low(n, slot, nk, l):
                pool.wait_ge(hi_full, l * UNITS + n + 1)
                pool.tensor_tensor(wl[:, slot, 0:nk, :], raw[:, slot, 0:nk, :],
                                   wh[:, slot, 0:nk, :].bitcast(F32), ALU.subtract).then_inc(lo_full, 1)

            def y_sum(m, stage, l):
                if m > 0:
                    n = stage * (KD - 1) + m
                    pool.wait_ge(sq_ready, l * NSQ + ((2 * stage + 1) * KD + m + 1))
                    if m > 1:
                        pool.wait_ge(ysum, l * NYQ + (n - 1))
                    pool.tensor_tensor(acc[:], acc[:], sqr[:, m % 2, :], ALU.add).then_inc(ysum, 1)

            def residual(stage, l):
                for k in range(KD):
                    pool.wait_ge(upd_ready, l * NXR + (stage * KD + k + 1))
                    pool.tensor_tensor(xt[:, k, :], xt[:, k, :], upd[:, k % 2, :], ALU.add).then_inc(x_ready, 1)

            with pool.Fori(0, L) as l:
                def ffn(f):
                    u0 = UBASE[f]
                    with pool.Fori(0, KF // 2 - 1) as i:
                        for q in range(4):
                            low(i * 4 + (u0 + SLOTS + q), q, 8, l)
                    for v in range(4):
                        low(u0 + IN_U + v, v, OUT_PARTS[v % 3][1], l)
                    for m in range(KD):
                        for v in range(3 * m + 4, 3 * m + 7):
                            if v < 3 * KD:
                                low(u0 + IN_U + v, v % SLOTS, OUT_PARTS[v % 3][1], l)
                            elif f == 0 and v < 3 * KD + 3:
                                low(u0 + IN_U + v, v % SLOTS, 8, l)
                        y_sum(m, 2 * f, l)
                    if f == 0:
                        low(u0 + FFN_U + 3, 3, 8, l)

                for n in range(SLOTS):
                    low(n, n, 8, l)
                ffn(0)
                residual(0, l)
                with pool.Fori(0, MIX_IN_U // 4) as i:
                    for q in range(4):
                        low(i * 4 + (MBASE + SLOTS + q), q, 8, l)
                for h in range(H):
                    pool.wait_ge(d_exp, l * H + h + 1)
                    pool.tensor_tensor(Dm[:, h], Dm[:, h], upper[:].unsqueeze(1).broadcast_to([P, NC, P]),
                                       ALU.mult).then_inc(d_ready, 1)
                pool.wait_ge(u_ready, l + 1)
                for rnd, src in enumerate((u, glu)):
                    off = 0 if src is u else PADC
                    for t in range(1, CT):
                        n = rnd * (CT - 1) + t
                        if rnd == 1:
                            pool.wait_ge(usq_ready, l * CT + t + 1)
                            if t == 1:
                                pool.wait_ge(usum_full, l + 1)
                        if t == 1:
                            ins = pool.tensor_tensor(lacc[:], src[:, 0, off:off + T], src[:, 1, off:off + T], ALU.add)
                        else:
                            pool.wait_ge(lsum, l * 2 * (CT - 1) + n - 1)
                            ins = pool.tensor_tensor(lacc[:], lacc[:], src[:, t, off:off + T], ALU.add)
                        ins.then_inc(lsum, 1)
                for m in range(KD):
                    low(MBASE + MIX_IN_U + m + SLOTS, m % SLOTS, 8, l)
                    y_sum(m, 1, l)
                residual(1, l)
                ffn(1)
                residual(2, l)

        @block.tensor
        def _(pe):
            pe.sem_inc(unit_done, SLOTS)
            pe.wait_ge(s_mask, 3)
            pe.wait_ge(s_rows, 16 * 13 * L)
            for l in range(L):
                for which, n in ((0, ROWS_A), (1, ROWS_B)):
                    pe.transpose(pq[:, 0, (2 * l + which) * P:(2 * l + which) * P + n], crows[0:n, l, which, :],
                                 ident[0:n, 0:n]).then_inc(s_cturn, 1)
            pe.wait_ge(s_load, 16 * NC)
            for k in range(KD):
                if k >= 4:
                    pe.wait_ge(x_turned, k - 3)
                for c in range(NC):
                    mm = pe.transpose(res[:, k % 4, c * P:(c + 1) * P], xin[:, c, k * P:(k + 1) * P], ident[:])
                mm.then_inc(s_xturn, 1)

            def tile(bank, slot, j, hi, lo, first, last):
                pe.matmul(res[:, bank, :], wh[:, slot, j, :], hi, start=first, stop=False)
                pe.matmul(res[:, bank, :], wh[:, slot, j, :], lo, start=False, stop=False)
                return pe.matmul(res[:, bank, :], wl[:, slot, j, :], hi, start=False, stop=last)

            def token_sums(src):
                for c in range(NC):
                    mm = pe.matmul(stat[:, c:c + 1], src[:, c * P:(c + 1) * P], ones[:, 0:1], start=True, stop=True)
                return mm

            def x_sums(stage, l):
                pe.wait_ge(xsum, l * NXQ + (stage + 1) * (KD - 1))
                token_sums(acc[:]).then_inc(ssq_full, 1)

            def y_sums(stage, l):
                pe.wait_ge(ysum, l * NYQ + (stage + 1) * (KD - 1))
                token_sums(acc[:]).then_inc(ssq_full, 1)

            def spread(q, l):
                pe.wait_ge(diag_ready, l * NST + q + 1)
                pe.matmul(bc[:, :], ones[:], diag[:].rearrange("p c t -> p (c t)"), start=True,
                          stop=True).then_inc(bc_full, 1)

            def first_units(u0, stage, stat_q, l):
                for k in range(KD):
                    pe.wait_ge(xs_ready, l * NXS + stage * KD + k + 1)
                    for n in range(3):
                        if k == 0:
                            pe.wait_ge(lo_full, l * UNITS + (u0 + n + 1 + SLOTS))
                        mm = tile(n, n, k, xh[:, k, :], xl[:, k, :], k == 0, k == KD - 1)
                        if k == KD - 1:
                            mm.then_inc(unit_done, 1)
                x_sums(stage, l)
                pe.wait_ge(lo_full, l * UNITS + (u0 + 3 + 1 + SLOTS))
                for k in range(KD):
                    if k == KD // 2:
                        spread(stat_q, l)
                    mm = tile(3, 3, k, xh[:, k, :], xl[:, k, :], k == 0, k == KD - 1)
                mm.then_inc(unit_done, 1)

            def in_unit(n, slot, bank, l):
                pe.wait_ge(lo_full, l * UNITS + n + (1 + SLOTS))
                for k in range(KD):
                    mm = tile(bank, slot, k, xh[:, k, :], xl[:, k, :], k == 0, k == KD - 1)
                mm.then_inc(unit_done, 1)

            def ffn(f, l):
                stage, u0 = 2 * f, UBASE[f]
                first_units(u0, stage, [0, 4][f], l)
                with pe.Fori(1, KF // 2) as i:
                    for q in range(2):
                        pe.wait_ge(pair_free, l * NP + i * 2 + (f * KF + q - 1))
                        for half in range(2):
                            in_unit(i * 4 + (u0 + 2 * q + half), 2 * q + half, 2 * q + half, l)
                with pe.Fori(0, KD // 4) as i:
                    for q in range(4):
                        if q == 0:
                            pe.wait_ge(h_ready, l * NP + (f * KF + KF - 1))
                        pe.wait_ge(y_done, l * NY + i * 4 + (YB + stage * KD + q - 3))
                        for part, (k0, nk) in enumerate(OUT_PARTS):
                            n = 3 * q + part
                            pe.wait_ge(lo_full, l * UNITS + i * 12 + (u0 + IN_U + n + 1 + SLOTS))
                            for j in range(nk):
                                k = k0 + j
                                if q == 0 and k == KF - 1:
                                    pe.wait_ge(h_ready, l * NP + (f * KF + KF))
                                mm = tile(q, n % SLOTS, j, hh[:, k, :], hl[:, k, :], k == 0, k == KF - 1)
                            mm.then_inc(unit_done, 1)
                y_sums(stage, l)
                spread([1, 5][f], l)

            pe.wait_ge(s_seedv, 1)
            pe.sem_inc(bc_full, 1)
            with pe.Fori(0, L) as l:
                ffn(0, l)
                first_units(MBASE, 1, 2, l)

                def mixer_units(i0, i1):
                    with pe.Fori(i0, i1) as i:
                        for q in range(4):
                            pe.wait_ge(mix_free, l * MIX_IN_U + i * 4 + (q - 3))
                            in_unit(i * 4 + (MBASE + q), q, q, l)

                mixer_units(1, MIX_IN_U // 4 - 1)
                pe.wait_ge(wab_ready, l * 2 + 2)
                for c in range(NC):
                    s = slice(c * P, (c + 1) * P)
                    for k in range(KD):
                        for n, (x_, w_) in enumerate(((xh, wabh), (xl, wabh), (xh, wabl))):
                            mm = pe.matmul(stat[:, 64 + c * 2 * H:64 + (c + 1) * 2 * H], x_[:, k, s], w_[:, k, :],
                                           start=(k == 0 and n == 0), stop=(k == KD - 1 and n == 2))
                mm.then_inc(ab_full, 1)
                mixer_units(MIX_IN_U // 4 - 1, MIX_IN_U // 4)
                pe.wait_ge(l2_sq, l * 2 * H + 2 * H)
                for n in range(2 * H):
                    for c in range(NC):
                        mm = pe.matmul(pq[:, 0, n * NC + c:n * NC + c + 1], ksq[:, n, c * P:(c + 1) * P],
                                       ones[:, 0:1], start=True, stop=True)
                mm.then_inc(l2_full, 1)
                pe.wait_ge(g_ready, l + 1)
                pe.matmul(stat[:, 96:112], upper[:], gt["g"][:, 0:16], start=True, stop=True)
                pe.matmul(stat[:, 112:128], ones[:], gt["g"][:, 0:16], start=True, stop=True).then_inc(gc_full, 1)
                pe.wait_ge(mix_free, l * MIX_IN_U + MIX_IN_U)
                for h in range(H):
                    pe.wait_ge(w_ready, l * H + h + 1)
                    pe.matmul(res[:, h, :], lowst[:], Wm[:, h % 2].rearrange("p c t -> p (c t)"), start=True,
                              stop=True).then_inc(e_full, 1)
                for h in range(H):
                    pe.wait_ge(d_exp, l * H + h + 1)
                    for c in range(NC):
                        mm = pe.transpose(res[:, h, c * P:(c + 1) * P], vT[:, h, c * P:(c + 1) * P], ident[:])
                    mm.then_inc(job_full, 1)
                for h in range(H):
                    pe.wait_ge(vt_free, l * H + h + 1)
                    for c in range(NC):
                        mm = pe.transpose(res[:, h, c * P:(c + 1) * P], kT[:, h, c * P:(c + 1) * P], ident[:])
                    mm.then_inc(job_full, 1)
                for h in range(H):
                    pe.wait_ge(kt_free, l * H + h + 1)
                    for c in range(NC):
                        mm = pe.transpose(res[:, h, c * P:(c + 1) * P], Um[:, h, c, :], ident[:])
                    mm.then_inc(job_full, 1)
                for h in range(H):
                    pe.wait_ge(kb_free, l * H + h + 1)
                    for c in range(NC):
                        s = slice(c * P, (c + 1) * P)
                        mm = pe.matmul(res[:, h, s], kT[:, h, s], kbT[:, h, s], start=True, stop=True)
                    mm.then_inc(job_full, 1)
                for h in range(H):
                    pe.wait_ge(b_free, l * H + h + 1)
                    for c in range(NC):
                        s = slice(c * P, (c + 1) * P)
                        mm = pe.matmul(res[:, h, s], kT[:, h, s], qT[:, h, s], start=True, stop=True)
                    mm.then_inc(job_full, 1)
                for h in range(H):
                    pe.wait_ge(u1_ready, l * H + h + 1)
                    pe.wait_ge(qk_free, l * H + h + 1)
                    for c in range(NC):
                        mm = pe.transpose(res[:, h, c * P:(c + 1) * P], Um[:, h, c, :], ident[:])
                    mm.then_inc(t1_full, 1)
                for n, s in enumerate(LEVELS[1:]):
                    for g in range(2):
                        if n == 0:
                            pe.wait_ge(t_ready, l * H + 2 * g + 2)
                        else:
                            pe.wait_ge(u_upd, l * 12 + 2 * (n - 1) + g + 1)
                        for j in range(8):
                            h, c = 2 * g + j // 4, j % 4
                            even = Tm[:, h, c, :].rearrange("p (b two e) -> p b two e", two=2, e=s)[:, :, 0, :]
                            mm = pe.matmul(pq[:, g, j * 64:(j + 1) * 64].rearrange("p (b e) -> p b e", e=s),
                                           Bm[:, h, c, :], even, start=True, stop=True)
                        mm.then_inc(p_full, 1)
                    for g in range(2):
                        pe.wait_ge(pm_ready, l * 12 + 2 * n + g + 1)
                        for j in range(8):
                            h, c = 2 * g + j // 4, j % 4
                            mm = pe.matmul(pq[:, g, j * 64:(j + 1) * 64], Um[:, h, c, :], pm[:, 4 * h + c, :],
                                           start=True, stop=True)
                        mm.then_inc(q_full, 1)
                    if n == 5:
                        pe.wait_ge(lsum, l * 2 * (CT - 1) + CT - 1)
                        pe.wait_ge(ekd_ready, l + 1)
                        token_sums(lacc[:]).then_inc(usum_full, 1)
                    for g in range(2):
                        pe.wait_ge(t_upd, l * 12 + 2 * n + g + 1)
                        for j in range(8):
                            h, c = 2 * g + j // 4, j % 4
                            mm = pe.transpose(res[:, h, c * P:(c + 1) * P], Tm[:, h, c, :], ident[:])
                        mm.then_inc(tt_full, 1)
                pe.wait_ge(mu_ready, l + 1)
                pe.matmul(bc[:, :], ones[:], ldiag[:].rearrange("p c t -> p (c t)"), start=True,
                          stop=True).then_inc(mubc_full, 1)
                for g in range(2):
                    pe.wait_ge(u_upd, l * 12 + 10 + g + 1)
                for c in range(NC):
                    s = slice(c * P, (c + 1) * P)
                    if c > 0:
                        pe.wait_ge(s_ready, l * NC + c)
                        for h in range(H):
                            mm = pe.matmul(pq[:, 0, h * P:(h + 1) * P], kbT[:, h, s], St[:, h, :], start=True,
                                           stop=True)
                        mm.then_inc(ks_full, 1)
                    pe.wait_ge(xd_ready, l * NC + c + 1)
                    for h in range(H):
                        mm = pe.matmul(pq[:, 1, h * P:(h + 1) * P], Um[:, h, c, :], Xd[:, h, :], start=True,
                                       stop=True)
                    mm.then_inc(vn_full, 1)
                    if c > 0:
                        pe.wait_ge(o_free, l * NC + c)
                        for h in range(H):
                            pe.matmul(res[:, 2, h * P:(h + 1) * P], qT[:, h, s], St[:, h, :], start=True, stop=True)
                    pe.wait_ge(vn_ready, l * NC + c + 1)
                    for h in range(H):
                        mm = pe.matmul(res[:, 0, h * P:(h + 1) * P], kdec[:, h, c, :], vn[:, h, :], start=True,
                                       stop=True)
                    mm.then_inc(su_full, 1)
                    for h in range(H):
                        mm = pe.matmul(res[:, 3, h * P:(h + 1) * P], QK[:, h, c, :], vn[:, h, :], start=True,
                                       stop=True)
                    mm.then_inc(o_full, 1)
                    if c == 1:
                        pe.wait_ge(lsum, l * 2 * (CT - 1) + 2 * (CT - 1))
                        token_sums(lacc[:]).then_inc(vsum_full, 1)
                    if c == 2:
                        pe.wait_ge(udiag, l + 1)
                        pe.matmul(bc[:, :], ones[:], ldiag[:].rearrange("p c t -> p (c t)"), start=True,
                                  stop=True).then_inc(uvbc_full, 1)
                pe.wait_ge(s_ready, l * NC + NC)
                for h in range(H):
                    pe.wait_ge(on_ready, l * H + h + 1)
                    for c in range(NC):
                        mm = pe.transpose(res[:, h, c * P:(c + 1) * P], on[:, h, c, :], ident[:])
                    mm.then_inc(ot_full, 1)
                with pe.Fori(0, KD // 4) as i:
                    for q in range(4):
                        pe.wait_ge(y_done, l * NY + i * 4 + (YB + KD + q - 3))
                        pe.wait_ge(lo_full, l * UNITS + i * 4 + (MBASE + MIX_IN_U + q + 1 + SLOTS))
                        if q == 0:
                            pe.wait_ge(cmix_ready, l * CT + CT)
                            pe.wait_ge(gm_ready, l * H + H)
                        for k in range(KD):
                            mm = tile(q, q, k, ch[:, k, :], cl[:, k, :], k == 0, k == KD - 1)
                        mm.then_inc(unit_done, 1)
                y_sums(1, l)
                spread(3, l)
                ffn(1, l)
                x_sums(3, l)
                spread(6, l)
            pe.wait_ge(xn_ready, (L + 1) * KD)
            for c in range(NC):
                for half in range(2):
                    n = 2 * c + half
                    if n >= 4:
                        pe.wait_ge(y_copied, n - 3)
                    for k in range(4):
                        mm = pe.transpose(res[:, n % 4, k * P:(k + 1) * P], xt[:, half * 4 + k, c * P:(c + 1) * P],
                                          ident[:])
                    mm.then_inc(y_turn, 1)

        @block.scalar
        def _(act):
            def high(n, slot, nk, l):
                act.wait_ge(raw_full[slot], l * (16 * PER_SLOT) + _slot_count(n, slot))
                act.wait_ge(unit_done, l * UNITS + n + 1)
                act.activation(wh[:, slot, 0:nk, :], raw[:, slot, 0:nk, :], ACT.Copy).then_inc(hi_full, 1)

            def _slot_count(n, slot):
                return (n - slot) * (16 // SLOTS) + 16

            def root(q, l, ss, dst, scale):
                act.wait_ge(ssq_full, l * NST + q + 1)
                act.activation(dst, ss, ACT.Sqrt, bias=eps[:, 0:1], scale=scale).then_inc(root_ready, 1)

            def inputs(stage, gain, l):
                for k in range(KD):
                    if stage == 0:
                        act.wait_ge(xn_ready, l * KD + k + 1)
                    else:
                        act.wait_ge(x_ready, l * NXR + ((stage - 1) * KD + k + 1))
                    if stage == 0 and k == 0:
                        act.wait_ge(cur_ready, l * 2 + 2)
                    act.activation(xh[:, k, :], xt[:, k, :], ACT.Copy,
                                   scale=cur[:, gain + k:gain + k + 1]).then_inc(xh_ready, 1)
                    x_square(k, stage, l)

            def x_square(k, stage, l):
                if k > 2:
                    act.wait_ge(xsum, l * NXQ + (stage * (KD - 1) + k - 2))
                act.activation(sqr[:, k % 2, :] if k else acc[:], xt[:, k, :], ACT.Square).then_inc(sq_ready, 1)

            def row_out(q, n, l):
                act.wait_ge(bc_full, l * NST + q + 2)
                act.activation(rs[:], bc[:, :], ACT.Copy).then_inc(rs_ready, 1)

            def y_tile(bank, m, gain, scale, stage, l):
                if m > 2:
                    act.wait_ge(ysum, l * NYQ + (stage * (KD - 1) + m - 2))
                act.activation(sqr[:, m % 2, :] if m else acc[:], res[:, bank, :], ACT.Square).then_inc(sq_ready, 1)
                act.activation(yg[:, m, :], res[:, bank, :], ACT.Copy,
                               scale=cur[:, gain + m:gain + m + 1]).then_inc(y_done, 1)

            def ffn(f, l):
                stage, u0 = 2 * f, UBASE[f]
                inputs(stage, [G_F1PRE, G_F2PRE][f], l)
                root([0, 4][f], l, stat[:, 0:NC], rsq[:], 1.0 / D)
                row_out([0, 4][f], 2 * f, l)

                def pair(i, q, sizes):
                    for half in range(2):
                        n = 2 * q + half
                        high(i * 4 + (u0 + 4 + n) if not isinstance(i, int) else 4 * i + u0 + 4 + n, n, sizes[n], l)
                    act.wait_ge(gate_scaled, l * NP + i * 2 + (f * KF + q + 1))
                    act.activation(gs[:, q, :], gs[:, q, :], ACT.Silu).then_inc(silu_done, 1)

                with act.Fori(0, KF // 2 - 1) as i:
                    for q in range(2):
                        pair(i, q, [8, 8, 8, 8])
                for q in range(2):
                    pair(KF // 2 - 1, q, [OUT_PARTS[n % 3][1] for n in range(4)])
                gain = [G_F1POST, G_F2POST][f]
                for m in range(KD):
                    for part in range(3):
                        v = 3 * m + part + 4
                        if v < 3 * KD:
                            high(u0 + IN_U + v, v % SLOTS, OUT_PARTS[v % 3][1], l)
                        elif f == 0 and v < 3 * KD + 3:
                            high(u0 + IN_U + v, v % SLOTS, 8, l)
                    act.wait_ge(unit_done, l * UNITS + (u0 + IN_U + 3 * m + 3 + SLOTS))
                    y_tile(m % 4, m, gain, 1.0, stage, l)
                if f == 0:
                    high(u0 + FFN_U + 3, 3, 8, l)
                root([1, 5][f], l, stat[:, 0:NC], rsq[:], 1.0 / D)

            act.sem_inc(y_done, YB)
            act.wait_ge(s_mask, 3)
            act.wait_ge(s_heads, 16 * 3 * L)
            for l in range(L):
                act.activation(hcall[:, l, 0, :], hcall[:, l, 0, :], ACT.Exp).then_inc(s_negA, 1)
            with act.Fori(0, L) as l:
                for n in range(SLOTS):
                    high(n, n, 8, l)
                ffn(0, l)
                inputs(1, G_MPRE, l)
                root(2, l, stat[:, 0:NC], rsq[:], 1.0 / D)
                row_out(2, 1, l)
                for r in range(MIX_IN_U):
                    high(MBASE + r + 4, r % SLOTS, 8, l)
                    if r < 2 * CT:
                        if r % 2:
                            act.wait_ge(mix_free, l * MIX_IN_U + r + 1)
                            act.activation(gb[:], gb[:], ACT.Sigmoid).then_inc(sig_ready, 1)
                    elif r < 2 * CT + 3 * H:
                        n = r - 2 * CT
                        act.wait_ge(cv_ready, l * 3 * H + n + 1)
                        dst = (kT, vT, qT)[n // H][:, n % H, :]
                        act.activation(dst, cacc[:, n % 2, :], ACT.Silu).then_inc(act_kvqz, 1)
                        if n // H != 1:
                            act.wait_ge(act_kvqz, l * 4 * H + n + 1)
                            act.activation(ksq[:, n if n < H else n - H, :], dst, ACT.Square).then_inc(l2_sq, 1)
                    else:
                        n = r - 2 * CT - 3 * H
                        act.wait_ge(mix_free, l * MIX_IN_U + r + 1)
                        act.activation(zT[:, n, :], zT[:, n, :], ACT.Silu).then_inc(act_kvqz, 1)
                    if r == 2 * CT + 3 * H:
                        act.wait_ge(na_ready, l + 1)
                        act.activation(gt["na"][:, 0:16], gt["na"][:, 0:16], ACT.Exp).then_inc(ln_ready, 1)
                        act.wait_ge(ln_ready, l * 2 + 1)
                        act.activation(gt["eb"][:, 0:16], gt["eb"][:, 0:16], ACT.Exp)
                        act.activation(gt["lnv"][:, 0:16], gt["na"][:, 0:16], ACT.Ln, bias=1.0).then_inc(ln_ready, 1)
                act.wait_ge(l2_full, l + 1)
                act.activation(gt["ss"][:, 0:32], pq[:, 0, 0:32], ACT.Sqrt, bias=eps[:, 0:1]).then_inc(l2_root, 1)
                act.wait_ge(gc_full, l + 1)
                act.activation(gt["egc"][:, 0:16], stat[:, 96:112], ACT.Exp)
                act.activation(gt["egl"][:, 0:16], stat[:, 112:128], ACT.Exp).then_inc(egc_ready, 1)
                act.wait_ge(dgl_ready, l + 1)
                act.activation(gt["ekd"][:, 0:16], gt["dgl"][:, 0:16], ACT.Exp).then_inc(ekd_ready, 1)
                for h in range(H):
                    act.wait_ge(e_full, l * H + h + 1)
                    act.activation(Dm[:, h], res[:, h, :].rearrange("p (c t) -> p c t", c=NC),
                                   ACT.Exp).then_inc(d_exp, 1)
                for h in range(H):
                    act.wait_ge(job_full, l * 5 * H + 2 * H + h + 1)
                    act.activation(kbT[:, h, :], res[:, h, :], ACT.Copy).then_inc(kb_free, 1)
                for h in range(H):
                    act.wait_ge(t1_full, l * H + h + 1)
                    act.activation(Tm[:, h], res[:, h, :].rearrange("p (c t) -> p c t", c=NC),
                                   ACT.Copy).then_inc(t_ready, 1)
                for n in range(6):
                    for g in range(2):
                        act.wait_ge(tt_full, l * 12 + 2 * n + g + 1)
                        act.activation(Um[:, 2 * g:2 * g + 2].rearrange("p h c t -> p h (c t)"),
                                       res[:, 2 * g:2 * g + 2, :], ACT.Copy).then_inc(u_upd, 1)
                for c in range(NC):
                    act.wait_ge(vn_full, l * NC + c + 1)
                    act.activation(vn[:].rearrange("p h e -> p (h e)"), pq[:, 1, :], ACT.Copy).then_inc(vn_ready, 1)
                    if c == 0:
                        for t in range(CT):
                            act.wait_ge(uc_ready, l * CT + t + 1)
                            act.activation(glu[:, t, PADC:], u[:, t, :], ACT.Square).then_inc(usq_ready, 1)
                    if c == 1:
                        act.wait_ge(vsum_full, l + 1)
                        act.activation(rsq[:], stat[:, 0:NC], ACT.Sqrt, bias=eps[:, 0:1],
                                       scale=1.0 / CW).then_inc(uroot, 1)
                for t in range(CT):
                    act.wait_ge(un_ready, l * CT + t + 1)
                    act.activation(u[:, t, :], u[:, t, :], ACT.Silu, bias=cur[:, C_LNB + t:C_LNB + t + 1],
                                   scale=cur[:, C_LNG + t:C_LNG + t + 1]).then_inc(us_ready, 1)
                    act.wait_ge(us_ready, l * CT + t + 1)
                    act.activation(ch[:, H + t, :], u[:, t, :], ACT.Copy).then_inc(uh_ready, 1)
                for h in range(H):
                    act.wait_ge(o_free, l * NC + NC)
                    if h >= 2:
                        act.wait_ge(oss_ready, l * H + h - 1)
                    act.activation(sqr[:, h % 2, :], on[:, h].rearrange("p c e -> p (c e)"),
                                   ACT.Square).then_inc(osq_ready, 1)
                act.wait_ge(oss_ready, l * H + H)
                act.activation(gt["orr"][:, 0:16], gt["oss"][:, 0:16], ACT.Sqrt, bias=eps[:, 0:1],
                               scale=1.0 / DH).then_inc(oroot, 1)
                for h in range(H):
                    act.wait_ge(gh_ready, l * H + h + 1)
                    act.activation(ch[:, h, :], Wm[:, h % 2].rearrange("p c t -> p (c t)"),
                                   ACT.Copy).then_inc(gate_hi, 1)
                for m in range(KD):
                    high(MBASE + MIX_IN_U + m + SLOTS, m % SLOTS, 8, l)
                    y_tile(m % 4, m, G_MPOST, 1.0, 1, l)
                root(3, l, stat[:, 0:NC], rsq[:], 1.0 / D)
                ffn(1, l)
                for k in range(KD):
                    act.wait_ge(x_ready, l * NXR + (2 * KD + k + 1))
                    x_square(k, 3, l)
                root(6, l, stat[:, 0:NC], rsq[:], 1.0 / D)
            for n in range(0, 2 * NC, 2):
                act.wait_ge(y_turn, n + 1)
                act.activation(xin[:, n // 2, 0:T], res[:, n % 4, :], ACT.Copy).then_inc(y_copied, 1)
                act.wait_ge(y_turn, n + 2)
                act.activation(xin[:, n // 2, T:2 * T], res[:, (n + 1) % 4, :], ACT.Copy).then_inc(y_copied, 1)

        @block.vector
        def _(dve):
            st = Steps(dve, dve_step)
            dve.memset(bc[:, :], 1.0).then_inc(s_seedv, 1)
            dve.memset(gblk[:], 1.0).then_inc(s_seedg, 1)
            dve.wait_ge(s_mask, 3 + 2 * 6)
            for l in range(L):
                for which, (n, at0) in enumerate(((ROWS_A, 0), (ROWS_B, ROWS_A))):
                    dve.wait_ge(s_cturn, 2 * L)
                    c0 = (2 * l + which) * P
                    dve.tensor_copy(call[:, l, at0:at0 + n], pq[:, 0, c0:c0 + n]).then_inc(s_cc, 1)
            for l in range(L):
                dve.wait_ge(s_negA, l + 1)
                dve.tensor_scalar(hcall[:, l, 0, :], hcall[:, l, 0, :], -1.0, None, ALU.mult).then_inc(s_cc, 1)
            for l in range(L):
                for g in (G_F1POST, G_F2POST):
                    dve.wait_ge(s_cc, 3 * L)
                    dve.tensor_scalar(call[:, l, g:g + KD], call[:, l, g:g + KD], 0.5, None,
                                      ALU.mult).then_inc(s_cc, 1)
            dve.wait_ge(s_cc, 5 * L)
            for k in range(KD):
                dve.wait_ge(s_xturn, k + 1)
                dve.tensor_copy(xt[:, k, :], res[:, k % 4, :]).then_inc(x_turned, 1)
            dve.wait_ge(x_turned, KD)
            dve.wait_ge(s_seedg, 1)

            def row(q, l, col):
                dve.wait_ge(root_ready, l * NST + q + 1)
                st.link(dve.reciprocal(col[:], rsq[:]))
                dve.tensor_tensor(diag[:], ident[:].unsqueeze(1).broadcast_to([P, NC, P]),
                                  col[:].unsqueeze(2).broadcast_to([P, NC, P]), ALU.mult).then_inc(diag_ready, 1)

            def low(k, stage, gain, l):
                dve.wait_ge(xh_ready, l * NXS + stage * KD + k + 1)
                dve.scalar_tensor_tensor(xl[:, k, :], xt[:, k, :], cur[:, gain + k:gain + k + 1],
                                         xh[:, k, :].bitcast(F32), ALU.mult, ALU.subtract).then_inc(xs_ready, 1)

            def x_sum(k, stage, l):
                if k > 0:
                    n = stage * (KD - 1) + k
                    dve.wait_ge(sq_ready, l * NSQ + ((6 if stage == 3 else 2 * stage) * KD + k + 1))
                    if k > 1:
                        dve.wait_ge(xsum, l * NXQ + (n - 1))
                    dve.tensor_tensor(acc[:], acc[:], sqr[:, k % 2, :], ALU.add).then_inc(xsum, 1)

            def update(k, stage, l):
                n = stage * KD + k
                if k > 1:
                    dve.wait_ge(x_ready, l * NXR + (n - 1))
                dve.tensor_tensor(upd[:, k % 2, :], yg[:, k, :], bc[:, :], ALU.mult).then_inc(upd_ready, 1)

            def stage_inputs(stage, q, gain, l):
                dve.wait_ge(bc_full, l * NST + q + 2)
                for k in range(KD + 2):
                    if k < KD:
                        update(k, stage - 1, l)
                    if k >= 2:
                        low(k - 2, stage, gain, l)
                        x_sum(k - 2, stage, l)

            def block_scale(k, l):
                dve.scalar_tensor_tensor(xt[:, k, :], xt[:, k, :], gblk[:, k:k + 1], bc[:, :],
                                         ALU.mult, ALU.mult).then_inc(xn_ready, 1)

            def ffn(f, l):
                row([0, 4][f], l, rcol)
                with dve.Fori(0, KF // 2) as i:
                    dve.sem_clear(pair_step)
                    dve.wait_ge(rs_ready, l * 3 + (2 * f + 1))
                    ps = Steps(dve, pair_step)
                    for q in range(2):
                        n = i * 4 + (UBASE[f] + 2 * q + SLOTS)
                        dve.wait_ge(unit_done, l * UNITS + n + 1)
                        dve.tensor_tensor(gs[:, q, :], res[:, 2 * q, :], rs[:], ALU.mult).then_inc(gate_scaled, 1)
                        dve.wait_ge(unit_done, l * UNITS + n + 2)
                        dve.tensor_tensor(us[:, q, :], res[:, 2 * q + 1, :], rs[:], ALU.mult).then_inc(pair_free, 1)
                        dve.wait_ge(pair_free, l * NP + i * 2 + (f * KF + q + 1))
                        dve.wait_ge(silu_done, l * NP + i * 2 + (f * KF + q + 1))
                        ps.link(dve.tensor_tensor(hf[:], gs[:, q, :], us[:, q, :], ALU.mult))
                        ps.link(dve.tensor_scalar(hh[:, i * 2 + q, :], hf[:], 1.0, None, ALU.mult))
                        dve.tensor_tensor(hl[:, i * 2 + q, :], hf[:], hh[:, i * 2 + q, :].bitcast(F32),
                                          ALU.subtract).then_inc(h_ready, 1)
                dve.wait_ge(h_ready, l * NP + (f + 1) * KF)
                row([1, 5][f], l, rcol)

            with dve.Fori(0, L) as l:
                dve.sem_clear(dve_step)
                st.n = 0
                dve.tensor_copy(wabh[:], wabr[:, l]).then_inc(wab_ready, 1)
                dve.wait_ge(wab_ready, l * 2 + 1)
                dve.tensor_tensor(wabl[:], wabr[:, l], wabh[:].bitcast(F32), ALU.subtract).then_inc(wab_ready, 1)
                dve.tensor_copy(hcur[:], hcall[:, l]).then_inc(cur_ready, 1)
                dve.tensor_copy(cur[:], call[:, l, :]).then_inc(cur_ready, 1)
                dve.wait_ge(cur_ready, l * 2 + 2)
                dve.wait_ge(bc_full, l * NST + 1)
                for k in range(KD + 1):
                    if k < KD:
                        block_scale(k, l)
                    if k >= 1:
                        dve.wait_ge(xn_ready, l * KD + k)
                        low(k - 1, 0, G_F1PRE, l)
                        x_sum(k - 1, 0, l)
                dve.wait_ge(xn_ready, l * KD + KD)
                dve.tensor_copy(gblk[:], cur[:, G_BLOCK:G_BLOCK + KD]).then_inc(blk_done, 1)
                ffn(0, l)
                stage_inputs(1, 1, G_MPRE, l)
                row(2, l, rmix)
                st.link(dve.memset(pre[:, 0:PADG], 0.0))
                dve.wait_ge(rs_ready, l * 3 + 2)
                st.link(dve.memset(glu[:, :, 0:PADC], 0.0))

                taps = [(t, k) for k in range(CTAPS) for t in range(CT)]
                tap_mark = [0] * CT

                def conv_taps(n):
                    for _ in range(n):
                        if not taps:
                            return
                        t, k = taps.pop(0)
                        w = cur[:, C_DW + k * CT + t:C_DW + k * CT + t + 1]
                        src = glu[:, t, k:k + T]
                        if k == 0:
                            ins = dve.tensor_scalar(u[:, t, :], src, w, cur[:, C_DWB + t:C_DWB + t + 1], ALU.mult,
                                                    ALU.add)
                        else:
                            st.need(tap_mark[t])
                            ins = dve.scalar_tensor_tensor(u[:, t, :], src, w, u[:, t, :], ALU.mult, ALU.add)
                        tap_mark[t] = st.done(ins)

                def hc(name):
                    return gt[name][:, 0:16].rearrange("p (h c) -> p h c", h=H)

                def gates_in():
                    dve.wait_ge(ab_full, l + 1)
                    st.link(dve.tensor_tensor(gt["ab"][:].rearrange("p (c j) -> p c j", c=NC),
                                              stat[:, 64:96].rearrange("p (c j) -> p c j", c=NC),
                                              rmix[:].unsqueeze(2).broadcast_to([P, NC, 2 * H]), ALU.mult))
                    abv = gt["ab"][:].rearrange("p (c j) -> p j c", c=NC)
                    st.link(dve.tensor_tensor(hc("xa"), abv[:, 0:H, :],
                                              hcur[:, 1, :].unsqueeze(2).broadcast_to([P, H, NC]), ALU.add))
                    st.link(dve.tensor_scalar(hc("eb"), abv[:, H:2 * H, :], -1.0, 87.0, ALU.mult, ALU.min))
                    dve.scalar_tensor_tensor(gt["na"][:, 0:16], gt["xa"][:, 0:16], -1.0, gt["xa"][:, 0:16], ALU.mult,
                                             ALU.min).then_inc(na_ready, 1)

                def gates_out():
                    dve.wait_ge(ln_ready, l * 2 + 2)
                    st.link(dve.scalar_tensor_tensor(gt["g"][:, 0:16], gt["xa"][:, 0:16], 0.0, gt["lnv"][:, 0:16],
                                                     ALU.max, ALU.add))
                    dve.tensor_tensor(hc("g"), hc("g"), hcur[:, 0, :].unsqueeze(2).broadcast_to([P, H, NC]),
                                      ALU.mult).then_inc(g_ready, 1)
                    st.link(dve.tensor_scalar(gt["eb"][:, 0:16], gt["eb"][:, 0:16], 1.0, None, ALU.add))
                    st.link(dve.reciprocal(gt["beta"][:, 0:16], gt["eb"][:, 0:16]))

                for r in range(MIX_IN_U):
                    bank = r % 4
                    dve.wait_ge(unit_done, l * UNITS + (MBASE + r + 1 + SLOTS))
                    if r < 2 * CT:
                        if r % 2 == 0:
                            dve.tensor_tensor(ga[:], res[:, bank, :], rs[:], ALU.mult).then_inc(mix_free, 1)
                        else:
                            t = r // 2
                            dve.tensor_tensor(gb[:], res[:, bank, :], rs[:], ALU.mult).then_inc(mix_free, 1)
                            dve.wait_ge(mix_free, l * MIX_IN_U + r + 1)
                            dve.wait_ge(sig_ready, l * CT + t + 1)
                            st.link(dve.tensor_tensor(glu[:, t, PADC:], ga[:], gb[:], ALU.mult))
                    elif r < 2 * CT + 3 * H:
                        n = r - 2 * CT
                        if n:
                            dve.wait_ge(cv_ready, l * 3 * H + n)
                        dve.tensor_tensor(pre[:, PADG:], res[:, bank, :], rs[:], ALU.mult).then_inc(mix_free, 1)
                        dve.wait_ge(mix_free, l * MIX_IN_U + r + 1)
                        which = (1, 2, 0)[n // H]
                        if n >= 2:
                            dve.wait_ge(act_kvqz, l * 4 * H + n - 1)
                        for k in range(GTAPS):
                            w = cur[:, C_QKV + k * 3 * H + which * H + n % H:C_QKV + k * 3 * H + which * H + n % H + 1]
                            src = pre[:, k:k + T]
                            if k == 0:
                                mark = st.done(dve.tensor_scalar(cacc[:, n % 2, :], src, w, None, ALU.mult))
                            else:
                                conv_taps(1)
                                st.need(mark)
                                ins = dve.scalar_tensor_tensor(cacc[:, n % 2, :], src, w, cacc[:, n % 2, :],
                                                               ALU.mult, ALU.add)
                                if k < GTAPS - 1:
                                    mark = st.done(ins)
                                else:
                                    ins.then_inc(cv_ready, 1)
                    else:
                        n = r - 2 * CT - 3 * H
                        dve.tensor_tensor(zT[:, n, :], res[:, bank, :], rs[:], ALU.mult).then_inc(mix_free, 1)
                        dve.wait_ge(mix_free, l * MIX_IN_U + r + 1)
                        if n == 0:
                            gates_in()
                        if n == 1:
                            gates_out()
                        conv_taps(7)
                dve.wait_ge(l2_root, l + 1)
                st.link(dve.reciprocal(gt["rk"][:, 0:32], gt["ss"][:, 0:32]))
                dve.tensor_tensor(gt["bk"][:, 0:16], gt["rk"][:, 0:16], gt["beta"][:, 0:16], ALU.mult)
                dve.tensor_scalar(gt["rq8"][:, 0:16], gt["rk"][:, 16:32], float(DH) ** -0.5, None, ALU.mult)
                dve.wait_ge(egc_ready, l + 1)
                st.link(dve.tensor_copy(gt["dgl"][:, 16:32], stat[:, 96:112]))
                dve.tensor_tensor(gt["dgl"][:, 0:16], stat[:, 112:128], gt["dgl"][:, 16:32],
                                  ALU.subtract).then_inc(dgl_ready, 1)
                conv_taps(4)
                dve.wait_ge(ekd_ready, l + 1)
                st.link(dve.tensor_tensor(gt["kd"][:, 0:16], gt["rk"][:, 0:16], gt["ekd"][:, 0:16], ALU.mult))

                def per_token(name, h):
                    return gt[name][:, h * NC:(h + 1) * NC].unsqueeze(2).broadcast_to([P, NC, P])

                for h in range(H):
                    if h >= 2:
                        dve.wait_ge(e_full, l * H + h - 1)
                    dve.tensor_tensor(Wm[:, h % 2], upper[:].unsqueeze(1).broadcast_to([P, NC, P]),
                                      per_token("g", h), ALU.mult).then_inc(w_ready, 1)

                def heads(bank):
                    return res[:, bank, :].rearrange("p (c e) -> p c e", c=NC)

                for h in range(H):
                    dve.wait_ge(job_full, l * 5 * H + h + 1)
                    dve.tensor_tensor(vb[:, h], heads(h), per_token("beta", h), ALU.mult).then_inc(vt_free, 1)
                for h in range(H):
                    dve.wait_ge(job_full, l * 5 * H + H + h + 1)
                    dve.tensor_tensor(kdec[:, h], heads(h), per_token("kd", h), ALU.mult)
                    dve.tensor_tensor(Um[:, h], heads(h), per_token("bk", h), ALU.mult).then_inc(kt_free, 1)
                for h in range(H):
                    dve.wait_ge(d_ready, l * H + h + 1)
                    mark = st.done(dve.tensor_tensor(Dm[:, h], Dm[:, h], per_token("rk", h), ALU.mult))
                st.need(mark)
                for h in range(H):
                    dve.wait_ge(job_full, l * 5 * H + 3 * H + h + 1)
                    dve.tensor_tensor(Bm[:, h], heads(h), Dm[:, h], ALU.mult).then_inc(b_free, 1)
                dve.wait_ge(b_free, l * H + H)
                for h in range(H):
                    uv = Um[:, h].rearrange("p c (b two) -> p (c b) two", two=2)
                    bv = Bm[:, h].rearrange("p c (b two) -> p (c b) two", two=2)
                    idv = ident[:].unsqueeze(1).broadcast_to([P, NC, P])
                    st.link(dve.tensor_copy(Um[:, h], idv))
                    m = ident[:].rearrange("p (b two) -> p b two", two=2)[:, :, 0].unsqueeze(1).broadcast_to([P, NC, 64])
                    st.link(dve.tensor_tensor(pm[:, 4 * h:4 * h + 4, :],
                                              Bm[:, h].rearrange("p c (b two) -> p c b two", two=2)[:, :, :, 1], m,
                                              ALU.mult))
                    odd = Um[:, h].rearrange("p c (b two) -> p c b two", two=2)[:, :, :, 1]
                    dve.tensor_tensor(odd, odd, pm[:, 4 * h:4 * h + 4, :], ALU.subtract).then_inc(u1_ready, 1)
                for h in range(H):
                    dve.wait_ge(job_full, l * 5 * H + 4 * H + h + 1)
                    dve.tensor_tensor(QK[:, h], heads(h), Dm[:, h], ALU.mult).then_inc(qk_free, 1)
                conv_taps(8)
                for n, s in enumerate(LEVELS[1:]):
                    for g in range(2):
                        dve.wait_ge(p_full, l * 12 + 2 * n + g + 1)
                        dve.tensor_tensor(pm[:, 8 * g:8 * g + 8, :], pq[:, g, :].rearrange("p (j e) -> p j e", j=8),
                                          lmask[:, n, :].unsqueeze(1).broadcast_to([P, 8, 64]),
                                          ALU.mult).then_inc(pm_ready, 1)
                        conv_taps(2)
                    if n == 4:
                        conv_taps(len(taps))
                        for t in range(CT):
                            st.need(tap_mark[t])
                        dve.sem_inc(u_ready, 1)
                    if n == 5:
                        dve.wait_ge(usum_full, l + 1)
                        st.link(dve.tensor_scalar(rcol[:], stat[:, 0:NC], 1.0 / CW, None, ALU.mult))
                        dve.tensor_tensor(ldiag[:], ident[:].unsqueeze(1).broadcast_to([P, NC, P]),
                                          rcol[:].unsqueeze(2).broadcast_to([P, NC, P]), ALU.mult).then_inc(mu_ready, 1)
                    for g in range(2):
                        dve.wait_ge(q_full, l * 12 + 2 * n + g + 1)
                        even = Tm[:, 2 * g:2 * g + 2].rearrange("p h c (b two e) -> p (h c b) two e", two=2,
                                                                e=s)[:, :, 0, :]
                        dve.tensor_tensor(even, even, pq[:, g, :].rearrange("p (b e) -> p b e", e=s),
                                          ALU.subtract).then_inc(t_upd, 1)
                        conv_taps(2)
                dve.wait_ge(mubc_full, l + 1)
                for t in range(CT):
                    dve.tensor_tensor(u[:, t, :], u[:, t, :], bc[:, :], ALU.subtract).then_inc(uc_ready, 1)

                def per_head(name, c, n=P):
                    return gt[name][:, 0:16].rearrange("p (h c) -> p h c", h=H)[:, :, c:c + 1].broadcast_to([P, H, P])

                def four(ap):
                    return ap.rearrange("p (h e) -> p h e", h=H)

                for c in range(NC):
                    if c == 0:
                        dve.wait_ge(vt_free, l * H + H)
                        dve.tensor_copy(Xd[:], vb[:, :, c, :]).then_inc(xd_ready, 1)
                    else:
                        dve.wait_ge(ks_full, l * (NC - 1) + c)
                        dve.wait_ge(vn_full, l * NC + c)
                        st.link(dve.tensor_tensor(Xd[:], four(pq[:, 0, :]), per_head("egc", c), ALU.mult))
                        dve.tensor_tensor(Xd[:], vb[:, :, c, :], Xd[:], ALU.subtract).then_inc(xd_ready, 1)
                        mark = st.done(dve.tensor_tensor(sd[:], St[:], per_head("egl", c), ALU.mult))
                        if c == 2:
                            dve.wait_ge(uroot, l + 1)
                            st.link(dve.reciprocal(rcol[:], rsq[:]))
                            dve.tensor_tensor(ldiag[:], ident[:].unsqueeze(1).broadcast_to([P, NC, P]),
                                              rcol[:].unsqueeze(2).broadcast_to([P, NC, P]),
                                              ALU.mult).then_inc(udiag, 1)
                    dve.wait_ge(su_full, l * NC + c + 1)
                    if c == 0:
                        dve.tensor_copy(St[:], four(res[:, 0, :])).then_inc(s_ready, 1)
                    else:
                        st.need(mark)
                        dve.tensor_tensor(St[:], sd[:], four(res[:, 0, :]), ALU.add).then_inc(s_ready, 1)
                    dve.wait_ge(o_full, l * NC + c + 1)
                    if c == 0:
                        dve.tensor_tensor(on[:, :, c, :], four(res[:, 3, :]), per_head("rq8", c),
                                          ALU.mult).then_inc(o_free, 1)
                    else:
                        st.link(dve.tensor_tensor(oq[:], four(res[:, 2, :]), per_head("egc", c), ALU.mult))
                        st.link(dve.tensor_tensor(oq[:], oq[:], four(res[:, 3, :]), ALU.add))
                        dve.tensor_tensor(on[:, :, c, :], oq[:], per_head("rq8", c), ALU.mult).then_inc(o_free, 1)
                dve.wait_ge(uvbc_full, l + 1)
                dve.wait_ge(uc_ready, l * CT + CT)
                for t in range(CT):
                    dve.tensor_tensor(u[:, t, :], u[:, t, :], bc[:, :], ALU.mult).then_inc(un_ready, 1)
                dve.wait_ge(o_free, l * NC + NC)
                for h in range(H):
                    dve.wait_ge(osq_ready, l * H + h + 1)
                    dve.tensor_reduce(gt["oss"][:, h * NC:(h + 1) * NC],
                                      sqr[:, h % 2, :].rearrange("p (c e) -> p c e", c=NC), AX_X,
                                      ALU.add).then_inc(oss_ready, 1)
                dve.wait_ge(oroot, l + 1)
                st.link(dve.reciprocal(gt["oss"][:, 0:16], gt["orr"][:, 0:16]))
                for h in range(H):
                    dve.tensor_tensor(on[:, h], on[:, h], per_token("oss", h), ALU.mult).then_inc(on_ready, 1)
                for t in range(CT):
                    dve.wait_ge(uh_ready, l * CT + t + 1)
                    dve.tensor_tensor(cl[:, H + t, :], u[:, t, :], ch[:, H + t, :].bitcast(F32),
                                      ALU.subtract).then_inc(cmix_ready, 1)

                def head_low(h):
                    dve.wait_ge(gate_hi, l * H + h + 1)
                    dve.tensor_tensor(cl[:, h, :], Wm[:, h % 2].rearrange("p c t -> p (c t)"),
                                      ch[:, h, :].bitcast(F32), ALU.subtract).then_inc(gm_ready, 1)

                for h in range(H):
                    dve.wait_ge(ot_full, l * H + h + 1)
                    if h == 0:
                        dve.wait_ge(act_kvqz, l * 4 * H + 4 * H)
                    gf = Wm[:, h % 2].rearrange("p c t -> p (c t)")
                    if h >= 2:
                        dve.wait_ge(gm_ready, l * H + h - 1)
                    dve.scalar_tensor_tensor(gf, res[:, h, :], cur[:, C_OUT:C_OUT + 1], zT[:, h, :], ALU.mult,
                                             ALU.mult).then_inc(gh_ready, 1)
                    if h >= 1:
                        head_low(h - 1)
                head_low(H - 1)
                row(3, l, rcol)
                stage_inputs(2, 3, G_F2PRE, l)
                ffn(1, l)
                dve.wait_ge(bc_full, l * NST + 7)
                for k in range(KD + 2):
                    if k < KD:
                        update(k, 2, l)
                    if k >= 2:
                        x_sum(k - 2, 3, l)
                row(6, l, rcol)
                dve.wait_ge(blk_done, l + 1)
            dve.wait_ge(bc_full, L * NST + 1)
            for k in range(KD):
                block_scale(k, L)
    return nc


_INS = ["x", "ffn1_norm_pre", "ffn1_w_in", "ffn1_w_out", "ffn1_norm_post", "mix_norm_pre", "mix_w_in",
        "gdn_conv_w", "gdn_a_log", "gdn_dt_bias", "gdn_out_norm", "cm_dw_w", "cm_dw_b", "cm_ln_g", "cm_ln_b",
        "mix_w_out", "mix_norm_post", "ffn2_norm_pre", "ffn2_w_in", "ffn2_w_out", "ffn2_norm_post", "block_norm"]


def kernel(**inputs):
    import numpy as _np
    import concourse.bacc as _bacc
    from concourse import mybir as _mybir
    from concourse.bass_utils import run_bass_kernel_spmd as _run

    nc = _bacc.Bacc("TRN2", target_bir_lowering=False, num_devices=1)
    arrays, args = {}, []
    for name in _INS:
        a = _np.ascontiguousarray(inputs[name])
        arrays[f"in_{name}"] = a
        args.append(nc.dram_tensor(f"in_{name}", a.shape, _mybir.dt.from_np(a.dtype), kind="ExternalInput").ap())
    out = nc.dram_tensor("out_dram", arrays["in_x"].shape, _mybir.dt.float32, kind="ExternalOutput").ap()
    trunk_kernel(nc, *args, out)
    r = _run(nc, [arrays], core_ids=[0])
    return r.results[0]["out_dram"]
```

```python
from contextlib import ExitStack

import concourse.bass as bass
from concourse import mybir

F32 = mybir.dt.float32
F32R = mybir.dt.float32r
BF16 = mybir.dt.bfloat16
ALU = mybir.AluOpType
ACT = mybir.ActivationFunctionType
AX_X = mybir.AxisListType.X

P = 128
SLOTS = 4
EPS = 1e-6


class Steps:

    def __init__(self, eng, sem):
        self.eng, self.sem, self.n = eng, sem, 0

    def done(self, ins):
        self.n += 1
        ins.then_inc(self.sem, 1)
        return self.n

    def need(self, n):
        self.eng.wait_ge(self.sem, n)

    def link(self, ins):
        self.need(self.done(ins))


def trunk_kernel(nc, x, ffn1_norm_pre, ffn1_w_in, ffn1_w_out, ffn1_norm_post, mix_norm_pre, mix_w_in,
                 gdn_conv_w, gdn_a_log, gdn_dt_bias, gdn_out_norm, cm_dw_w, cm_dw_b, cm_ln_g, cm_ln_b,
                 mix_w_out, mix_norm_post, ffn2_norm_pre, ffn2_w_in, ffn2_w_out, ffn2_norm_post,
                 block_norm, out):
    L, D = ffn1_norm_pre.shape
    T = x.shape[1]
    FF = ffn1_w_out.shape[1]
    H = gdn_a_log.shape[1]
    DH = gdn_out_norm.shape[1]
    GW = H * DH
    GTAPS, CTAPS = gdn_conv_w.shape[1], cm_dw_w.shape[1]
    CW = cm_dw_w.shape[2]
    KD = D // P
    KF = FF // P
    NC = T // P
    CT = CW // P
    assert (KD, KF, NC, H, CT, DH, T) == (8, 22, 4, 4, 4, P, 512)
    K0, V0, Z0, A0 = GW, 2 * GW, 3 * GW, 4 * GW
    G0 = A0 + 2 * H

    IN_U = 2 * KF
    OUT_PARTS = [(0, 8), (8, 7), (15, 7)]
    FFN_U = IN_U + len(OUT_PARTS) * KD
    MIX_IN_U = 2 * CT + 4 * H
    MIX_U = MIX_IN_U + KD
    UNITS = 2 * FFN_U + MIX_U
    UBASE = [0, FFN_U + MIX_U]
    MBASE = FFN_U
    assert UNITS % SLOTS == 0 and FFN_U % SLOTS == 0 and MIX_U % SLOTS == 0
    PER_SLOT = UNITS // SLOTS
    NXS, NSQ, NST, NY, NP = 3 * KD, 7 * KD, 7, 3 * KD, 2 * KF

    GAINS = [ffn1_norm_pre, ffn1_norm_post, mix_norm_pre, mix_norm_post, ffn2_norm_pre, ffn2_norm_post,
             block_norm]
    G_F1PRE, G_F1POST, G_MPRE, G_MPOST, G_F2PRE, G_F2POST, G_BLOCK = range(0, 7 * KD, KD)
    C_QKV = 7 * KD
    C_DWB = C_QKV + GTAPS * 3 * H
    C_LNG, C_LNB, C_OUT = C_DWB + CT, C_DWB + 2 * CT, C_DWB + 3 * CT
    ROWS_A = C_OUT + 1
    ROWS_B = CTAPS * CT
    C_DW = ROWS_A
    NCONST = ROWS_A + ROWS_B
    assert ROWS_A <= P and ROWS_B <= P

    base = -(-nc.sbuf_base // 32) * 32
    XT_B = T * 4

    def at(name, shape, dt, offset):
        return nc.alloc_sbuf_tensor_at(name, shape, dt, offset=base + offset)

    o_x = 0
    o_xh = o_x + KD * XT_B
    o_xl = o_xh + KD * XT_B
    o_raw = o_xl + KD * XT_B
    o_wh = o_raw + SLOTS * 8 * P * 4
    o_wl = o_wh + SLOTS * 8 * P * 4
    o_h = o_wl + SLOTS * 8 * P * 4
    o_tmp = o_h + 2 * KF * XT_B
    o_sq = o_tmp + 5 * XT_B
    o_rs = o_sq + 2 * XT_B
    o_c = o_rs + XT_B

    xt = at("xt", [P, KD, T], F32, o_x)
    xh = at("xh", [P, KD, T], F32R, o_xh)
    xl = at("xl", [P, KD, T], F32R, o_xl)
    yg = at("yg", [P, KD, T], F32, o_xh)
    raw = at("raw", [P, SLOTS, 8, P], F32, o_raw)
    wh = at("wh", [P, SLOTS, 8, P], F32R, o_wh)
    wl = at("wl", [P, SLOTS, 8, P], F32R, o_wl)
    hh = at("hh", [P, KF, T], F32R, o_h)
    hl = at("hl", [P, KF, T], F32R, o_h + KF * XT_B)
    gs = at("gs", [P, 2, T], F32, o_tmp)
    us = at("us", [P, 2, T], F32, o_tmp + 2 * XT_B)
    hf = at("hf", [P, T], F32, o_tmp + 4 * XT_B)
    diag_h = at("diag_h", [P, NC, P], F32R, o_tmp + 4 * XT_B)
    diag_l = at("diag_l", [P, NC, P], F32R, o_sq)
    acc = at("acc", [P, T], F32, o_tmp + 4 * XT_B)
    upd = at("upd", [P, 2, T], F32, o_tmp)
    sqr = at("sqr", [P, 2, T], F32, o_sq)
    rs = at("rs", [P, T], F32, o_rs)
    xin = at("xin", [P, NC, D], F32, o_h)

    kT = at("kT", [P, H, T], F32, o_h)
    vT = at("vT", [P, H, T], F32, o_h + 8192)
    kdec = at("kdec", [P, H, NC, P], F32, o_h + 8192)
    qT = at("qT", [P, H, T], F32, o_h + 16384)
    zT = at("zT", [P, H, T], F32, o_h + 24576)
    PADC = CTAPS - 1
    glu = at("glu", [P, CT, PADC + T], F32, o_h + 32768)
    u = at("u", [P, CT, T], F32, o_h + 41472)
    ch = at("ch", [P, KD, T], F32R, o_h + 49664)
    cl = at("cl", [P, KD, T], F32R, o_h + 66048)
    ksq = at("ksq", [P, 2 * H, T], F32, o_h + 49664)
    kbT = at("kbT", [P, H, T], F32, o_h + 49664)
    vb = at("vb", [P, H, NC, P], F32, o_h + 66048)
    pm = at("pm", [P, H * NC, 64], F32, o_h + 82432)
    o_gate = o_h + 86528
    GN = ["ab", "xa", "na", "lnv", "g", "eb", "beta", "egc", "egl", "dgl", "ekd", "bk", "kd", "rq8", "ss",
          "rk", "oss", "orr"]
    gt = {}
    for n, name in enumerate(GN):
        w = 32
        gt[name] = at("gate_" + name, [P, w], F32, o_gate + 128 * n)
    assert 128 * len(GN) <= 3584
    Bm = at("Bm", [P, H, NC, P], F32, o_xh)
    QK = at("QK", [P, H, NC, P], F32, o_xh + 8192)
    Tm = at("Tm", [P, H, NC, P], F32, o_xh + 16384)
    Dm = at("Dm", [P, H, NC, P], F32, o_xh + 16384)
    osq = at("osq", [P, H, T], F32, o_h)
    on = at("on", [P, H, NC, P], F32, o_xh + 16384)
    Um = at("Um", [P, H, NC, P], F32, o_xh + 24576)
    PADG = GTAPS - 1
    pre = at("pre", [P, PADG + T], F32, o_tmp)
    cacc = at("cacc", [P, 2, T], F32, o_tmp + 2080)
    ga = at("ga", [P, T], F32, o_h + 82432)
    abT = at("abT", [2 * H, T], F32, o_h + 82432)
    gb = at("gb", [P, T], F32, o_h + 82432 + XT_B)
    Wm = at("Wm", [P, 2, NC, P], F32, o_tmp)
    St = at("St", [P, H, P], F32, o_tmp)
    Xd = at("Xd", [P, H, P], F32, o_tmp + XT_B)
    vn = at("vn", [P, H, P], F32, o_tmp + 2 * XT_B)
    oq = at("oq", [P, H, P], F32, o_tmp + 3 * XT_B)
    sd = at("sd", [P, H, P], F32, o_tmp + 4 * XT_B)
    ldiag_h = at("ldiag_h", [P, NC, P], F32R, o_sq)
    ldiag_l = at("ldiag_l", [P, NC, P], F32R, o_sq + XT_B)
    lacc = at("lacc", [P, T], F32, o_sq + XT_B)
    co = [o_c]

    def const(name, shape, dt=F32, size=4):
        n = size
        for s in shape[1:]:
            n *= s
        t = at(name, shape, dt, co[0])
        co[0] += -(-n // 32) * 32
        return t

    ident = const("ident", [P, P])
    ones = const("ones", [P, P])
    upper = const("upper", [P, P])
    lowst = const("lowst", [P, P])
    LEVELS = [1, 2, 4, 8, 16, 32, 64]
    lmask = const("lmask", [P, 6, 64], BF16, 2)
    call = const("call", [P, L, NCONST])
    cur = const("cur", [P, NCONST])
    hcall = const("hcall", [P, L, 2, H])
    hcur = const("hcur", [P, 2, H])
    wabr = const("wabr", [P, L, KD, 2 * H])
    wabh = const("wabh", [P, KD, 2 * H], F32R)
    wabl = const("wabl", [P, KD, 2 * H], F32R)
    gblk = const("gblk", [P, KD])
    onesr = const("onesr", [P, P], F32R)
    col_h = const("col_h", [P, NC], F32R)
    col_l = const("col_l", [P, NC])
    rcol = const("rcol", [P, NC])
    rsq = const("rsq", [P, NC])
    rmix = const("rmix", [P, NC])
    eps = const("eps", [P, 1])
    YB = 4
    crows = at("crows", [P, L, 2, P], F32, o_h + NC * D * 4)
    assert base + co[0] <= nc.sbuf_usable_end, (base + co[0], nc.sbuf_usable_end)

    ctx = ExitStack()
    with ctx:
        def psum(name, shape):
            return ctx.enter_context(nc.psum_tensor(name, shape, F32))

        res = psum("res", [P, 4, T])
        stat = psum("stat", [P, T])
        bc = psum("bc", [P, T])
        pq = psum("pq", [P, 2, T])

        turned = [pq[:, 0, :], pq[:, 1, :], bc[:, :], stat[:, :]]

        def sem(name):
            return ctx.enter_context(nc.semaphore(name))

        raw_full = [sem(f"raw_full{i}") for i in range(SLOTS)]
        hi_full, lo_full, unit_done = sem("hi_full"), sem("lo_full"), sem("unit_done")
        s_load, s_rows, s_heads = sem("s_load"), sem("s_rows"), sem("s_heads")
        s_mask, s_seed, s_cc, s_seedv = sem("s_mask"), sem("s_seed"), sem("s_cc"), sem("s_seedv")
        s_rows2, s_heads2 = sem("s_rows2"), sem("s_heads2")
        s_seedg, blk_done = sem("s_seedg"), sem("blk_done")
        s_xturn, s_cturn, s_negA = sem("s_xturn"), sem("s_cturn"), sem("s_negA")
        x_turned, xn_ready, upd_ready = sem("x_turned"), sem("xn_ready"), sem("upd_ready")
        x_ready, xh_ready, xs_ready = sem("x_ready"), sem("xh_ready"), sem("xs_ready")
        cur_ready = sem("cur_ready")
        sq_ready, xsum, ysum = sem("sq_ready"), sem("xsum"), sem("ysum")
        ssq_full, root_ready, diag_ready, bc_full = sem("ssq_full"), sem("root_ready"), sem("diag_ready"), sem("bc_full")
        rs_ready = sem("rs_ready")
        gate_scaled, pair_free, silu_done, h_ready = sem("gate_scaled"), sem("pair_free"), sem("silu_done"), sem("h_ready")
        y_done = sem("y_done")
        dve_step, pair_step = sem("dve_step"), sem("pair_step")
        mix_free = sem("mix_free")
        sig_ready, cv_ready, act_kvqz, gate_hi = sem("sig_ready"), sem("cv_ready"), sem("act_kvqz"), sem("gate_hi")
        u_ready, usum_full, mu_ready, mubc_full, uc_ready, usq_ready, vsum_full, uroot, udiag, uvbc_full, un_ready = [
            sem(n) for n in ("u_ready", "usum_full", "mu_ready", "mubc_full", "uc_ready", "usq_ready", "vsum_full",
                             "uroot", "udiag", "uvbc_full", "un_ready")]
        ui_ready, rk_ready, kd_ready, kdec_ready, d_masked = [
            sem(n) for n in ("ui_ready", "rk_ready", "kd_ready", "kdec_ready", "d_masked")]
        us_ready, uh_ready, cmix_ready = sem("us_ready"), sem("uh_ready"), sem("cmix_ready")
        wab_ready, abT_full, abT_ready = sem("wab_ready"), sem("abT_full"), sem("abT_ready")
        ab_full, na_ready, ln_ready, g_ready, gc_full, egc_ready, dgl_ready, ekd_ready = [
            sem(n) for n in ("ab_full", "na_ready", "ln_ready", "g_ready", "gc_full", "egc_ready", "dgl_ready",
                             "ekd_ready")]
        l2_sq, l2_full, l2_root = sem("l2_sq"), sem("l2_full"), sem("l2_root")
        lsum = sem("lsum")
        w_ready, e_full, d_exp, d_ready = sem("w_ready"), sem("e_full"), sem("d_exp"), sem("d_ready")
        job_full, vt_free, kt_free, kb_free, b_free, qk_free = [
            sem(n) for n in ("job_full", "vt_free", "kt_free", "kb_free", "b_free", "qk_free")]
        u1_ready, t1_full, t_ready, p_full, pm_ready, q_full, t_upd, tt_full, u_upd = [
            sem(n) for n in ("u1_ready", "t1_full", "t_ready", "p_full", "pm_ready", "q_full", "t_upd", "tt_full",
                             "u_upd")]
        ks_full, xd_ready, vn_full, vn_ready, o_full, o_free, su_full, s_ready = [
            sem(n) for n in ("ks_full", "xd_ready", "vn_full", "vn_ready", "o_full", "o_free", "su_full", "s_ready")]
        osq_ready, oss_ready, oroot, on_ready, ot_full, gm_ready, gh_ready = [
            sem(n) for n in ("osq_ready", "oss_ready", "oroot", "on_ready", "ot_full", "gm_ready", "gh_ready")]
        y_turn, y_copied, s_out = sem("y_turn"), sem("y_copied"), sem("s_out")

        NXR = 3 * KD
        NXQ, NYQ = 4 * (KD - 1), 3 * (KD - 1)
        ffn_w = [(ffn1_w_in, ffn1_w_out), (ffn2_w_in, ffn2_w_out)]
        block = ctx.enter_context(nc.Block())

        def load_constants(eng, l, rows_sem, heads_sem):
            rows = [(0, G_ * KD, g[l].rearrange("(r p) -> r p", p=P)) for G_, g in enumerate(GAINS)]
            rows += [(0, C_QKV, gdn_conv_w[l].rearrange("k (r p) -> (k r) p", p=P)),
                     (0, C_DWB, cm_dw_b[l].rearrange("(r p) -> r p", p=P)),
                     (0, C_LNG, cm_ln_g[l].rearrange("(r p) -> r p", p=P)),
                     (0, C_LNB, cm_ln_b[l].rearrange("(r p) -> r p", p=P)),
                     (0, C_OUT, gdn_out_norm[l].rearrange("(r p) -> r p", p=P)),
                     (1, 0, cm_dw_w[l].rearrange("k (r p) -> (k r) p", p=P))]
            for which, r0, src in rows:
                eng.dma_start(crows[r0:r0 + src.shape[0], l, which, :], src).then_inc(rows_sem, 16)
            eng.dma_start(hcall[:, l, 0, :], gdn_a_log[l:l + 1, :].broadcast_to([P, H])).then_inc(heads_sem, 16)
            eng.dma_start(hcall[:, l, 1, :], gdn_dt_bias[l:l + 1, :].broadcast_to([P, H])).then_inc(heads_sem, 16)
            eng.dma_start(wabr[:, l, :, :],
                         mix_w_in[l].rearrange("(k p) c -> p k c", p=P)[:, :, A0:G0]).then_inc(heads_sem, 16)

        @block.sync
        def _(sp):
            for c in range(NC):
                sp.dma_start(xin[:, c, :], x[0, c * P:(c + 1) * P, :]).then_inc(s_load, 16)

            for l in range(1, L):
                load_constants(sp, l, s_rows2, s_heads2)

            def load(n, slot, src, l):
                sp.wait_ge(lo_full, l * UNITS + n + 1)
                sp.dma_start(raw[:, slot, 0:src.shape[1], :], src).then_inc(raw_full[slot], 16)

            with sp.Fori(0, L) as l:
                def ffn(f):
                    w_in = ffn_w[f][0].rearrange("l (k p) c -> l p k c", p=P)
                    w_out = ffn_w[f][1].rearrange("l (k p) c -> l p k c", p=P)
                    with sp.Fori(0, KF // 2) as i:
                        for q in range(2):
                            for half in range(2):
                                col = i * (2 * P) + (q * P + half * FF)
                                load(i * 4 + (UBASE[f] + 2 * q + half), 2 * q + half,
                                     w_in[l, :, :, bass.ds(col, P)], l)
                    with sp.Fori(0, KD // 4) as i:
                        for q in range(4):
                            for part, (k0, nk) in enumerate(OUT_PARTS):
                                n = q * 3 + part
                                load(i * 12 + (UBASE[f] + IN_U + n), n % SLOTS,
                                     w_out[l, :, k0:k0 + nk, bass.ds(i * (4 * P) + q * P, P)], l)

                ffn(0)
                w_mix = mix_w_in.rearrange("l (k p) c -> l p k c", p=P)
                with sp.Fori(0, CT // 2) as i:
                    for q in range(4):
                        col = i * (2 * P) + (G0 + (q // 2) * P + (q % 2) * CW)
                        load(i * 4 + (MBASE + q), q, w_mix[l, :, :, bass.ds(col, P)], l)
                for n0, col0, step in ((2 * CT, K0, V0 - K0), (2 * CT + 2 * H, 0, Z0)):
                    with sp.Fori(0, 2) as i:
                        for h in range(H):
                            load(i * 4 + (MBASE + n0 + h), h, w_mix[l, :, :, bass.ds(i * step + (col0 + h * P), P)], l)
                w_mo = mix_w_out.rearrange("l (k p) c -> l p k c", p=P)
                with sp.Fori(0, KD // 4) as i:
                    for q in range(4):
                        load(i * 4 + (MBASE + MIX_IN_U + q), q, w_mo[l, :, :, bass.ds(i * (4 * P) + q * P, P)], l)
                ffn(1)
            for n in range(SLOTS):
                load(n, n, ffn1_w_in.rearrange("l (k p) c -> l p k c", p=P)[0, :, :, 0:P], L)
            for c in range(NC):
                sp.wait_ge(y_copied, 2 * (c + 1))
                sp.dma_start(out[0, c * P:(c + 1) * P, :], xin[:, c, :]).then_inc(s_out, 16)
            sp.wait_ge(s_out, 16 * NC)

        @block.gpsimd
        def _(pool):
            pool.memset(ident[:], 0.0).then_inc(s_seed, 1)
            pool.memset(ones[:], 1.0).then_inc(s_seed, 1)
            pool.memset(eps[:], EPS).then_inc(s_seed, 1)
            pool.memset(lmask[:], 1.0).then_inc(s_seed, 1)
            pool.wait_ge(s_seed, 4)
            pool.affine_select(out=ident[:], in_=ident[:], compare_op=ALU.not_equal, fill=1.0, base=0,
                               pattern=[[-1, P]], channel_multiplier=1).then_inc(s_mask, 1)
            pool.affine_select(out=upper[:], in_=ones[:], compare_op=ALU.is_ge, fill=0.0, base=0,
                               pattern=[[1, P]], channel_multiplier=-1).then_inc(s_mask, 1)
            pool.affine_select(out=lowst[:], in_=ones[:], compare_op=ALU.is_ge, fill=0.0, base=-1,
                               pattern=[[-1, P]], channel_multiplier=1).then_inc(s_mask, 1)
            for n, s in enumerate(LEVELS[1:]):
                v = lmask[:, n, :].rearrange("p (b e) -> p b e", e=s)
                pool.affine_select(out=v, in_=v, compare_op=ALU.is_ge, fill=0.0, base=-s,
                                   pattern=[[-2 * s, 64 // s], [0, s]], channel_multiplier=1).then_inc(s_mask, 1)
                pool.wait_ge(s_mask, 4 + 2 * n)
                pool.affine_select(out=v, in_=v, compare_op=ALU.is_ge, fill=0.0, base=2 * s - 1,
                                   pattern=[[2 * s, 64 // s], [0, s]], channel_multiplier=-1).then_inc(s_mask, 1)
            pool.sem_inc(lo_full, SLOTS)

            def low(n, slot, nk, l):
                pool.wait_ge(hi_full, l * UNITS + n + 1)
                pool.tensor_tensor(wl[:, slot, 0:nk, :], raw[:, slot, 0:nk, :],
                                   wh[:, slot, 0:nk, :].bitcast(F32), ALU.subtract).then_inc(lo_full, 1)

            def y_sum(m, stage, l):
                if m > 0:
                    n = stage * (KD - 1) + m
                    pool.wait_ge(sq_ready, l * NSQ + ((2 * stage + 1) * KD + m + 1))
                    if m > 1:
                        pool.wait_ge(ysum, l * NYQ + (n - 1))
                    pool.tensor_tensor(acc[:], acc[:], sqr[:, m % 2, :], ALU.add).then_inc(ysum, 1)

            def residual(stage, l):
                for k in range(KD):
                    pool.wait_ge(upd_ready, l * NXR + (stage * KD + k + 1))
                    pool.tensor_tensor(xt[:, k, :], xt[:, k, :], upd[:, k % 2, :], ALU.add).then_inc(x_ready, 1)

            for n in range(SLOTS):
                low(n, n, 8, 0)
            with pool.Fori(0, L) as l:
                def ffn(f):
                    u0 = UBASE[f]
                    with pool.Fori(0, KF // 2 - 1) as i:
                        for q in range(4):
                            low(i * 4 + (u0 + SLOTS + q), q, 8, l)
                    for v in range(4):
                        low(u0 + IN_U + v, v, OUT_PARTS[v % 3][1], l)
                    for m in range(KD):
                        for v in range(3 * m + 4, 3 * m + 7):
                            if v < 3 * KD:
                                low(u0 + IN_U + v, v % SLOTS, OUT_PARTS[v % 3][1], l)
                            elif v < 3 * KD + 3:
                                low(u0 + IN_U + v, v % SLOTS, 8, l)
                        y_sum(m, 2 * f, l)
                    low(u0 + FFN_U + 3, 3, 8, l)

                ffn(0)
                residual(0, l)
                with pool.Fori(0, MIX_IN_U // 4) as i:
                    for q in range(4):
                        low(i * 4 + (MBASE + SLOTS + q), q, 8, l)
                for h in range(H):
                    pool.wait_ge(d_exp, l * H + h + 1)
                    pool.tensor_tensor(Dm[:, h], Dm[:, h], upper[:].unsqueeze(1).broadcast_to([P, NC, P]),
                                       ALU.mult).then_inc(d_masked, 1)
                pool.wait_ge(rk_ready, l + 1)
                for h in range(H):
                    pool.wait_ge(d_masked, l * H + h + 1)
                    pool.tensor_tensor(Dm[:, h], Dm[:, h],
                                       gt["rk"][:, h * NC:(h + 1) * NC].unsqueeze(2).broadcast_to([P, NC, P]),
                                       ALU.mult).then_inc(d_ready, 1)
                pool.wait_ge(u_ready, l + 1)
                for rnd, src in enumerate((u, glu)):
                    off = 0 if src is u else PADC
                    for t in range(1, CT):
                        n = rnd * (CT - 1) + t
                        if rnd == 1:
                            pool.wait_ge(usq_ready, l * CT + t + 1)
                            if t == 1:
                                pool.wait_ge(usum_full, l + 1)
                        if t == 1:
                            ins = pool.tensor_tensor(lacc[:], src[:, 0, off:off + T], src[:, 1, off:off + T], ALU.add)
                        else:
                            pool.wait_ge(lsum, l * 2 * (CT - 1) + n - 1)
                            ins = pool.tensor_tensor(lacc[:], lacc[:], src[:, t, off:off + T], ALU.add)
                        ins.then_inc(lsum, 1)
                for m in range(KD):
                    if m < KD - 1:
                        low(MBASE + MIX_IN_U + m + SLOTS, m % SLOTS, 8, l)
                    y_sum(m, 1, l)
                low(MBASE + MIX_U + 3, 3, 8, l)
                residual(1, l)
                ffn(1)
                residual(2, l)

        @block.tensor
        def _(pe):
            pe.sem_inc(unit_done, SLOTS)
            pe.wait_ge(s_mask, 3)
            pe.wait_ge(s_load, 16 * NC)
            for k in range(KD):
                if k >= 4:
                    pe.wait_ge(x_turned, k - 3)
                for c in range(NC):
                    mm = pe.transpose(res[:, k % 4, c * P:(c + 1) * P], xin[:, c, k * P:(k + 1) * P], ident[:])
                mm.then_inc(s_xturn, 1)
            pe.wait_ge(s_rows, 16 * 13)
            pe.wait_ge(s_rows2, 16 * 13 * (L - 1))
            for l in range(L):
                for which, n in ((0, ROWS_A), (1, ROWS_B)):
                    pe.transpose(pq[:, 0, (2 * l + which) * P:(2 * l + which) * P + n], crows[0:n, l, which, :],
                                 ident[0:n, 0:n]).then_inc(s_cturn, 1)

            def tile(bank, slot, j, hi, lo, first, last):
                pe.matmul(res[:, bank, :], wh[:, slot, j, :], hi, start=first, stop=False)
                pe.matmul(res[:, bank, :], wh[:, slot, j, :], lo, start=False, stop=False)
                return pe.matmul(res[:, bank, :], wl[:, slot, j, :], hi, start=False, stop=last)

            def token_sums(src):
                for c in range(NC):
                    mm = pe.matmul(stat[:, c:c + 1], src[:, c * P:(c + 1) * P], ones[:, 0:1], start=True, stop=True)
                return mm

            def x_sums(stage, l):
                pe.wait_ge(xsum, l * NXQ + (stage + 1) * (KD - 1))
                token_sums(acc[:]).then_inc(ssq_full, 1)

            def y_sums(stage, l):
                pe.wait_ge(ysum, l * NYQ + (stage + 1) * (KD - 1))
                token_sums(acc[:]).then_inc(ssq_full, 1)

            def spread(q, l):
                pe.wait_ge(diag_ready, l * 2 * NST + (2 * q + 1))
                pe.matmul(bc[:, :], onesr[:], diag_h[:].rearrange("p c t -> p (c t)"), start=True, stop=False)
                pe.wait_ge(diag_ready, l * 2 * NST + (2 * q + 2))
                pe.matmul(bc[:, :], onesr[:], diag_l[:].rearrange("p c t -> p (c t)"), start=False,
                          stop=True).then_inc(bc_full, 1)

            def first_units(u0, stage, stat_q, l):
                for k in range(KD):
                    pe.wait_ge(xs_ready, l * NXS + stage * KD + k + 1)
                    for n in range(3):
                        if k == 0:
                            pe.wait_ge(lo_full, l * UNITS + (u0 + n + 1 + SLOTS))
                        mm = tile(n, n, k, xh[:, k, :], xl[:, k, :], k == 0, k == KD - 1)
                        if k == KD - 1:
                            mm.then_inc(unit_done, 1)
                x_sums(stage, l)
                pe.wait_ge(lo_full, l * UNITS + (u0 + 3 + 1 + SLOTS))
                for k in range(KD):
                    if k == KD // 2:
                        spread(stat_q, l)
                    mm = tile(3, 3, k, xh[:, k, :], xl[:, k, :], k == 0, k == KD - 1)
                mm.then_inc(unit_done, 1)

            def in_unit(n, slot, bank, l):
                pe.wait_ge(lo_full, l * UNITS + n + (1 + SLOTS))
                for k in range(KD):
                    mm = tile(bank, slot, k, xh[:, k, :], xl[:, k, :], k == 0, k == KD - 1)
                mm.then_inc(unit_done, 1)

            def ffn(f, l):
                stage, u0 = 2 * f, UBASE[f]
                first_units(u0, stage, [0, 4][f], l)
                with pe.Fori(1, KF // 2) as i:
                    for q in range(2):
                        pe.wait_ge(pair_free, l * NP + i * 2 + (f * KF + q - 1))
                        for half in range(2):
                            in_unit(i * 4 + (u0 + 2 * q + half), 2 * q + half, 2 * q + half, l)
                with pe.Fori(0, KD // 4) as i:
                    for q in range(4):
                        if q == 0:
                            pe.wait_ge(h_ready, l * NP + (f * KF + KF - 1))
                        pe.wait_ge(y_done, l * NY + i * 4 + (YB + stage * KD + q - 3))
                        for part, (k0, nk) in enumerate(OUT_PARTS):
                            n = 3 * q + part
                            pe.wait_ge(lo_full, l * UNITS + i * 12 + (u0 + IN_U + n + 1 + SLOTS))
                            for j in range(nk):
                                k = k0 + j
                                if q == 0 and k == KF - 1:
                                    pe.wait_ge(h_ready, l * NP + (f * KF + KF))
                                mm = tile(q, n % SLOTS, j, hh[:, k, :], hl[:, k, :], k == 0, k == KF - 1)
                            mm.then_inc(unit_done, 1)
                y_sums(stage, l)
                spread([1, 5][f], l)

            pe.wait_ge(s_seedv, 1)
            pe.sem_inc(bc_full, 1)
            with pe.Fori(0, L) as l:
                ffn(0, l)
                first_units(MBASE, 1, 2, l)

                def mixer_units(i0, i1):
                    with pe.Fori(i0, i1) as i:
                        for q in range(4):
                            pe.wait_ge(mix_free, l * MIX_IN_U + i * 4 + (q - 3))
                            in_unit(i * 4 + (MBASE + q), q, q, l)

                mixer_units(1, MIX_IN_U // 4 - 2)
                pe.wait_ge(wab_ready, l * 2 + 2)
                for k in range(KD):
                    for n, (w_, x_) in enumerate(((wabh, xh), (wabh, xl), (wabl, xh))):
                        mm = pe.matmul(bc[0:2 * H, :], w_[:, k, :], x_[:, k, :], start=(k == 0 and n == 0),
                                       stop=(k == KD - 1 and n == 2))
                mm.then_inc(abT_full, 1)
                mixer_units(MIX_IN_U // 4 - 2, MIX_IN_U // 4 - 1)
                pe.wait_ge(abT_ready, l + 1)
                for c in range(NC):
                    mm = pe.matmul(stat[:, 64 + c * 2 * H:64 + (c + 1) * 2 * H], abT[:, c * P:(c + 1) * P],
                                   ident[0:2 * H, 0:2 * H], start=True, stop=True)
                mm.then_inc(ab_full, 1)
                mixer_units(MIX_IN_U // 4 - 1, MIX_IN_U // 4)
                pe.wait_ge(g_ready, l + 1)
                pe.matmul(stat[:, 96:112], upper[:], gt["g"][:, 0:16], start=True, stop=True)
                pe.matmul(stat[:, 112:128], ones[:], gt["g"][:, 0:16], start=True, stop=True).then_inc(gc_full, 1)
                pe.wait_ge(mix_free, l * MIX_IN_U + MIX_IN_U)
                for h in range(H):
                    pe.wait_ge(w_ready, l * H + h + 1)
                    pe.matmul(res[:, h, :], lowst[:], Wm[:, h % 2].rearrange("p c t -> p (c t)"), start=True,
                              stop=True).then_inc(e_full, 1)
                def norms(n):
                    for c in range(NC):
                        mm = pe.matmul(pq[:, n // H, n * NC + c:n * NC + c + 1], ksq[:, n, c * P:(c + 1) * P],
                                       ones[:, 0:1], start=True, stop=True)
                    return mm

                pe.wait_ge(l2_sq, l * 2 * H + 2 * H)
                for h in range(H):
                    mm = norms(h)
                mm.then_inc(l2_full, 1)
                for h in range(H):
                    pe.wait_ge(d_exp, l * H + h + 1)
                    for c in range(NC):
                        mm = pe.transpose(res[:, h, c * P:(c + 1) * P], vT[:, h, c * P:(c + 1) * P], ident[:])
                    mm.then_inc(job_full, 1)
                for h in range(H):
                    pe.wait_ge(vt_free, l * H + h + 1)
                    for c in range(NC):
                        mm = pe.transpose(res[:, h, c * P:(c + 1) * P], kT[:, h, c * P:(c + 1) * P], ident[:])
                    mm.then_inc(job_full, 1)
                for h in range(H):
                    pe.wait_ge(kt_free, l * H + h + 1)
                    pe.wait_ge(kdec_ready, l * H + h + 1)
                    for c in range(NC):
                        mm = pe.transpose(res[:, h, c * P:(c + 1) * P], Um[:, h, c, :], ident[:])
                    mm.then_inc(job_full, 1)
                    mm = norms(H + h)
                mm.then_inc(l2_full, 1)
                for h in range(H):
                    pe.wait_ge(kb_free, l * H + h + 1)
                    for c in range(NC):
                        s = slice(c * P, (c + 1) * P)
                        mm = pe.matmul(res[:, h, s], kT[:, h, s], kbT[:, h, s], start=True, stop=True)
                    mm.then_inc(job_full, 1)
                for h in range(H):
                    pe.wait_ge(b_free, l * H + h + 1)
                    for c in range(NC):
                        s = slice(c * P, (c + 1) * P)
                        mm = pe.matmul(res[:, h, s], kT[:, h, s], qT[:, h, s], start=True, stop=True)
                    mm.then_inc(job_full, 1)
                for h in range(H):
                    pe.wait_ge(u1_ready, l * H + h + 1)
                    pe.wait_ge(qk_free, l * H + h + 1)
                    for c in range(NC):
                        mm = pe.transpose(res[:, h, c * P:(c + 1) * P], Um[:, h, c, :], ident[:])
                    mm.then_inc(t1_full, 1)
                for n, s in enumerate(LEVELS[1:]):
                    for g in range(2):
                        if n == 0:
                            pe.wait_ge(t_ready, l * H + 2 * g + 2)
                        else:
                            pe.wait_ge(u_upd, l * 12 + 2 * (n - 1) + g + 1)
                        for j in range(8):
                            h, c = 2 * g + j // 4, j % 4
                            even = Tm[:, h, c, :].rearrange("p (b two e) -> p b two e", two=2, e=s)[:, :, 0, :]
                            mm = pe.matmul(pq[:, g, j * 64:(j + 1) * 64].rearrange("p (b e) -> p b e", e=s),
                                           Bm[:, h, c, :], even, start=True, stop=True)
                        mm.then_inc(p_full, 1)
                    for g in range(2):
                        pe.wait_ge(pm_ready, l * 12 + 2 * n + g + 1)
                        for j in range(8):
                            h, c = 2 * g + j // 4, j % 4
                            mm = pe.matmul(pq[:, g, j * 64:(j + 1) * 64], Um[:, h, c, :], pm[:, 4 * h + c, :],
                                           start=True, stop=True)
                        mm.then_inc(q_full, 1)
                    if n == 4:
                        pe.wait_ge(lsum, l * 2 * (CT - 1) + CT - 1)
                        pe.wait_ge(ekd_ready, l + 1)
                        token_sums(lacc[:]).then_inc(usum_full, 1)
                    for g in range(2):
                        pe.wait_ge(t_upd, l * 12 + 2 * n + g + 1)
                        for j in range(8):
                            h, c = 2 * g + j // 4, j % 4
                            mm = pe.transpose(res[:, h, c * P:(c + 1) * P], Tm[:, h, c, :], ident[:])
                        mm.then_inc(tt_full, 1)
                    if n == 4:
                        pe.wait_ge(mu_ready, l * 2 + 1)
                        pe.matmul(bc[:, :], onesr[:], ldiag_h[:].rearrange("p c t -> p (c t)"), start=True,
                                  stop=False)
                        pe.wait_ge(mu_ready, l * 2 + 2)
                        pe.matmul(bc[:, :], onesr[:], ldiag_l[:].rearrange("p c t -> p (c t)"), start=False,
                                  stop=True).then_inc(mubc_full, 1)
                for g in range(2):
                    pe.wait_ge(u_upd, l * 12 + 10 + g + 1)
                for c in range(NC):
                    s = slice(c * P, (c + 1) * P)
                    if c > 0:
                        pe.wait_ge(s_ready, l * NC + c)
                        for h in range(H):
                            mm = pe.matmul(pq[:, 0, h * P:(h + 1) * P], kbT[:, h, s], St[:, h, :], start=True,
                                           stop=True)
                        mm.then_inc(ks_full, 1)
                    pe.wait_ge(xd_ready, l * NC + c + 1)
                    for h in range(H):
                        mm = pe.matmul(pq[:, 1, h * P:(h + 1) * P], Um[:, h, c, :], Xd[:, h, :], start=True,
                                       stop=True)
                    mm.then_inc(vn_full, 1)
                    if c > 0:
                        pe.wait_ge(o_free, l * NC + c)
                        for h in range(H):
                            pe.matmul(res[:, 2, h * P:(h + 1) * P], qT[:, h, s], St[:, h, :], start=True, stop=True)
                    pe.wait_ge(vn_ready, l * NC + c + 1)
                    for h in range(H):
                        mm = pe.matmul(res[:, 0, h * P:(h + 1) * P], kdec[:, h, c, :], vn[:, h, :], start=True,
                                       stop=True)
                    mm.then_inc(su_full, 1)
                    for h in range(H):
                        mm = pe.matmul(res[:, 3, h * P:(h + 1) * P], QK[:, h, c, :], vn[:, h, :], start=True,
                                       stop=True)
                    mm.then_inc(o_full, 1)
                    if c == 1:
                        pe.wait_ge(lsum, l * 2 * (CT - 1) + 2 * (CT - 1))
                        token_sums(lacc[:]).then_inc(vsum_full, 1)
                    if c == 2:
                        pe.wait_ge(udiag, l * 2 + 1)
                        pe.matmul(bc[:, :], onesr[:], ldiag_h[:].rearrange("p c t -> p (c t)"), start=True,
                                  stop=False)
                        pe.wait_ge(udiag, l * 2 + 2)
                        pe.matmul(bc[:, :], onesr[:], ldiag_l[:].rearrange("p c t -> p (c t)"), start=False,
                                  stop=True).then_inc(uvbc_full, 1)
                pe.wait_ge(s_ready, l * NC + NC)
                def mix_out(m, half):
                    for k in range(half * CT, (half + 1) * CT):
                        if m == 0 and half == 1:
                            pe.wait_ge(cmix_ready, l * CT + k - CT + 1)
                        if m == 0 and half == 0:
                            pe.wait_ge(gm_ready, l * H + k + 1)
                        mm = tile(m % 4, m % SLOTS, k, ch[:, k, :], cl[:, k, :], k == CT, k == CT - 1)
                    return mm

                for m in range(4):
                    pe.wait_ge(lo_full, l * UNITS + (MBASE + MIX_IN_U + m + 1 + SLOTS))
                    mix_out(m, 1)
                    if m == 0:
                        for h in range(H):
                            pe.wait_ge(on_ready, l * H + h + 1)
                            for c in range(NC):
                                mm = pe.transpose(turned[h][:, c * P:(c + 1) * P], on[:, h, c, :], ident[:])
                            mm.then_inc(ot_full, 1)
                for m in range(KD):
                    if m >= 4:
                        pe.wait_ge(y_done, l * NY + (YB + KD + m - 3))
                        pe.wait_ge(lo_full, l * UNITS + (MBASE + MIX_IN_U + m + 1 + SLOTS))
                        mix_out(m, 1)
                    mix_out(m, 0).then_inc(unit_done, 1)
                y_sums(1, l)
                spread(3, l)
                ffn(1, l)
                x_sums(3, l)
                spread(6, l)
            pe.wait_ge(xn_ready, (L + 1) * KD)
            for c in range(NC):
                for half in range(2):
                    n = 2 * c + half
                    if n >= 4:
                        pe.wait_ge(y_copied, n - 3)
                    for k in range(4):
                        mm = pe.transpose(res[:, n % 4, k * P:(k + 1) * P], xt[:, half * 4 + k, c * P:(c + 1) * P],
                                          ident[:])
                    mm.then_inc(y_turn, 1)

        @block.scalar
        def _(act):
            def high(n, slot, nk, l):
                act.wait_ge(raw_full[slot], l * (16 * PER_SLOT) + _slot_count(n, slot))
                act.wait_ge(unit_done, l * UNITS + n + 1)
                act.activation(wh[:, slot, 0:nk, :], raw[:, slot, 0:nk, :], ACT.Copy).then_inc(hi_full, 1)

            def _slot_count(n, slot):
                return (n - slot) * (16 // SLOTS) + 16

            def root(q, l, ss, dst, scale):
                act.wait_ge(ssq_full, l * NST + q + 1)
                act.activation(dst, ss, ACT.Sqrt, bias=eps[:, 0:1], scale=scale).then_inc(root_ready, 1)

            def inputs(stage, gain, l):
                for k in range(KD):
                    if stage == 0:
                        act.wait_ge(xn_ready, l * KD + k + 1)
                    else:
                        act.wait_ge(x_ready, l * NXR + ((stage - 1) * KD + k + 1))
                    if stage == 0 and k == 0:
                        act.wait_ge(cur_ready, l * 2 + 2)
                    act.activation(xh[:, k, :], xt[:, k, :], ACT.Copy,
                                   scale=cur[:, gain + k:gain + k + 1]).then_inc(xh_ready, 1)
                    x_square(k, stage, l)

            def x_square(k, stage, l):
                if k > 2:
                    act.wait_ge(xsum, l * NXQ + (stage * (KD - 1) + k - 2))
                act.activation(sqr[:, k % 2, :] if k else acc[:], xt[:, k, :], ACT.Square).then_inc(sq_ready, 1)

            def row_out(q, n, l):
                act.wait_ge(bc_full, l * NST + q + 2)
                act.activation(rs[:], bc[:, :], ACT.Copy).then_inc(rs_ready, 1)

            def y_tile(bank, m, gain, stage, l):
                if m > 2:
                    act.wait_ge(ysum, l * NYQ + (stage * (KD - 1) + m - 2))
                act.activation(sqr[:, m % 2, :] if m else acc[:], res[:, bank, :], ACT.Square).then_inc(sq_ready, 1)
                act.activation(yg[:, m, :], res[:, bank, :], ACT.Copy,
                               scale=cur[:, gain + m:gain + m + 1]).then_inc(y_done, 1)

            def ffn(f, l):
                stage, u0 = 2 * f, UBASE[f]
                inputs(stage, [G_F1PRE, G_F2PRE][f], l)
                root([0, 4][f], l, stat[:, 0:NC], rsq[:], 1.0 / D)
                high(u0 + SLOTS, 0, 8, l)
                row_out([0, 4][f], 2 * f, l)

                def pair(i, q, sizes, first=0):
                    for half in range(first, 2):
                        n = 2 * q + half
                        high(i * 4 + (u0 + 4 + n) if not isinstance(i, int) else 4 * i + u0 + 4 + n, n, sizes[n], l)
                    act.wait_ge(gate_scaled, l * NP + i * 2 + (f * KF + q + 1))
                    act.activation(gs[:, q, :], gs[:, q, :], ACT.Silu).then_inc(silu_done, 1)

                for q in range(2):
                    pair(0, q, [8, 8, 8, 8], 1 - q)
                with act.Fori(1, KF // 2 - 1) as i:
                    for q in range(2):
                        pair(i, q, [8, 8, 8, 8])
                for q in range(2):
                    pair(KF // 2 - 1, q, [OUT_PARTS[n % 3][1] for n in range(4)])
                gain = [G_F1POST, G_F2POST][f]
                for m in range(KD):
                    for part in range(3):
                        v = 3 * m + part + 4
                        if v < 3 * KD:
                            high(u0 + IN_U + v, v % SLOTS, OUT_PARTS[v % 3][1], l)
                        elif v < 3 * KD + 3:
                            high(u0 + IN_U + v, v % SLOTS, 8, l)
                    act.wait_ge(unit_done, l * UNITS + (u0 + IN_U + 3 * m + 3 + SLOTS))
                    y_tile(m % 4, m, gain, stage, l)
                high(u0 + FFN_U + 3, 3, 8, l)
                root([1, 5][f], l, stat[:, 0:NC], rsq[:], 1.0 / D)

            load_constants(act, 0, s_rows, s_heads)
            act.sem_inc(y_done, YB)
            act.wait_ge(s_mask, 3)
            act.wait_ge(s_heads, 16 * 3)
            act.wait_ge(s_heads2, 16 * 3 * (L - 1))
            for l in range(L):
                act.activation(hcall[:, l, 0, :], hcall[:, l, 0, :], ACT.Exp).then_inc(s_negA, 1)
            for n in range(SLOTS):
                high(n, n, 8, 0)
            with act.Fori(0, L) as l:
                ffn(0, l)
                inputs(1, G_MPRE, l)
                root(2, l, stat[:, 0:NC], rsq[:], 1.0 / D)
                high(MBASE + SLOTS, 0, 8, l)
                row_out(2, 1, l)
                for r in range(MIX_IN_U):
                    if r > 0:
                        high(MBASE + r + SLOTS, r % SLOTS, 8, l)
                    if r < 2 * CT:
                        if r % 2:
                            act.wait_ge(mix_free, l * MIX_IN_U + r + 1)
                            act.activation(gb[:], gb[:], ACT.Sigmoid).then_inc(sig_ready, 1)
                    elif r < 2 * CT + 3 * H:
                        n = r - 2 * CT
                        act.wait_ge(cv_ready, l * 3 * H + n + 1)
                        dst = (kT, vT, qT)[n // H][:, n % H, :]
                        act.activation(dst, cacc[:, n % 2, :], ACT.Silu).then_inc(act_kvqz, 1)
                        if n // H != 1:
                            act.wait_ge(act_kvqz, l * 4 * H + n + 1)
                            act.activation(ksq[:, n if n < H else n - H, :], dst, ACT.Square).then_inc(l2_sq, 1)
                    else:
                        n = r - 2 * CT - 3 * H
                        act.wait_ge(mix_free, l * MIX_IN_U + r + 1)
                        act.activation(zT[:, n, :], zT[:, n, :], ACT.Silu).then_inc(act_kvqz, 1)
                    if r == 2 * CT + 3 * H:
                        act.wait_ge(na_ready, l + 1)
                        act.activation(gt["na"][:, 0:16], gt["na"][:, 0:16], ACT.Exp).then_inc(ln_ready, 1)
                        act.wait_ge(ln_ready, l * 2 + 1)
                        act.activation(gt["eb"][:, 0:16], gt["eb"][:, 0:16], ACT.Exp)
                        act.activation(gt["lnv"][:, 0:16], gt["na"][:, 0:16], ACT.Ln, bias=1.0).then_inc(ln_ready, 1)
                act.wait_ge(gc_full, l + 1)
                act.activation(gt["egc"][:, 0:16], stat[:, 96:112], ACT.Exp)
                act.activation(gt["egl"][:, 0:16], stat[:, 112:128], ACT.Exp).then_inc(egc_ready, 1)
                act.wait_ge(dgl_ready, l + 1)
                act.activation(gt["ekd"][:, 0:16], gt["dgl"][:, 0:16], ACT.Exp).then_inc(ekd_ready, 1)
                for h in range(H):
                    act.wait_ge(e_full, l * H + h + 1)
                    act.activation(Dm[:, h], res[:, h, :].rearrange("p (c t) -> p c t", c=NC),
                                   ACT.Exp).then_inc(d_exp, 1)
                act.wait_ge(l2_full, l * 2 + 1)
                act.activation(gt["ss"][:, 0:16], pq[:, 0, 0:16], ACT.Sqrt, bias=eps[:, 0:1]).then_inc(l2_root, 1)
                act.wait_ge(kd_ready, l + 1)
                for h in range(H):
                    act.wait_ge(kt_free, l * H + h + 1)
                    for c in range(NC):
                        n = h * NC + c
                        ins = act.activation(kdec[:, h, c, :], res[:, h, c * P:(c + 1) * P], ACT.Copy,
                                             scale=gt["kd"][:, n:n + 1])
                    ins.then_inc(kdec_ready, 1)
                for h in range(H):
                    act.wait_ge(job_full, l * 5 * H + 2 * H + h + 1)
                    act.activation(kbT[:, h, :], res[:, h, :], ACT.Copy).then_inc(kb_free, 1)
                act.wait_ge(l2_full, l * 2 + 2)
                act.activation(gt["ss"][:, 16:32], pq[:, 1, 16:32], ACT.Sqrt, bias=eps[:, 0:1]).then_inc(l2_root, 1)
                for h in range(H):
                    act.activation(Um[:, h], ident[:].unsqueeze(1).broadcast_to([P, NC, P]),
                                   ACT.Copy).then_inc(ui_ready, 1)
                for h in range(H):
                    act.wait_ge(t1_full, l * H + h + 1)
                    act.activation(Tm[:, h], res[:, h, :].rearrange("p (c t) -> p c t", c=NC),
                                   ACT.Copy).then_inc(t_ready, 1)
                for n in range(6):
                    for g in range(2):
                        act.wait_ge(tt_full, l * 12 + 2 * n + g + 1)
                        act.activation(Um[:, 2 * g:2 * g + 2].rearrange("p h c t -> p h (c t)"),
                                       res[:, 2 * g:2 * g + 2, :], ACT.Copy).then_inc(u_upd, 1)
                for c in range(NC):
                    act.wait_ge(vn_full, l * NC + c + 1)
                    act.activation(vn[:].rearrange("p h e -> p (h e)"), pq[:, 1, :], ACT.Copy).then_inc(vn_ready, 1)
                    if c == 0:
                        for t in range(CT):
                            act.wait_ge(uc_ready, l * CT + t + 1)
                            act.activation(glu[:, t, PADC:], u[:, t, :], ACT.Square).then_inc(usq_ready, 1)
                    if c == 1:
                        act.wait_ge(vsum_full, l + 1)
                        act.activation(rsq[:], stat[:, 0:NC], ACT.Sqrt, bias=eps[:, 0:1],
                                       scale=1.0 / CW).then_inc(uroot, 1)
                for t in range(CT):
                    act.wait_ge(un_ready, l * CT + t + 1)
                    act.activation(u[:, t, :], u[:, t, :], ACT.Silu, bias=cur[:, C_LNB + t:C_LNB + t + 1],
                                   scale=cur[:, C_LNG + t:C_LNG + t + 1]).then_inc(us_ready, 1)
                for t in range(CT):
                    act.wait_ge(us_ready, l * CT + t + 1)
                    act.activation(ch[:, H + t, :], u[:, t, :], ACT.Copy).then_inc(uh_ready, 1)
                for h in range(H):
                    act.wait_ge(o_free, l * NC + NC)
                    act.activation(osq[:, h, :], on[:, h].rearrange("p c e -> p (c e)"),
                                   ACT.Square).then_inc(osq_ready, 1)
                act.wait_ge(oss_ready, l * H + H)
                act.activation(gt["orr"][:, 0:16], gt["oss"][:, 0:16], ACT.Sqrt, bias=eps[:, 0:1],
                               scale=1.0 / DH).then_inc(oroot, 1)
                for h in range(H):
                    act.wait_ge(gh_ready, l * H + h + 1)
                    act.activation(ch[:, h, :], Wm[:, h % 2].rearrange("p c t -> p (c t)"),
                                   ACT.Copy).then_inc(gate_hi, 1)
                for m in range(KD):
                    if m < KD - 1:
                        high(MBASE + MIX_IN_U + m + SLOTS, m % SLOTS, 8, l)
                    else:
                        act.wait_ge(unit_done, l * UNITS + (MBASE + MIX_U + SLOTS))
                    y_tile(m % 4, m, G_MPOST, 1, l)
                high(MBASE + MIX_U + 3, 3, 8, l)
                root(3, l, stat[:, 0:NC], rsq[:], 1.0 / D)
                ffn(1, l)
                for k in range(KD):
                    act.wait_ge(x_ready, l * NXR + (2 * KD + k + 1))
                    x_square(k, 3, l)
                root(6, l, stat[:, 0:NC], rsq[:], 1.0 / D)
            for n in range(0, 2 * NC, 2):
                act.wait_ge(y_turn, n + 1)
                act.activation(xin[:, n // 2, 0:T], res[:, n % 4, :], ACT.Copy).then_inc(y_copied, 1)
                act.wait_ge(y_turn, n + 2)
                act.activation(xin[:, n // 2, T:2 * T], res[:, (n + 1) % 4, :], ACT.Copy).then_inc(y_copied, 1)

        @block.vector
        def _(dve):
            st = Steps(dve, dve_step)
            dve.memset(bc[:, :], 1.0).then_inc(s_seedv, 1)
            dve.memset(gblk[:], 1.0).then_inc(s_seedg, 1)
            dve.wait_ge(s_seed, 4)
            dve.tensor_copy(onesr[:], ones[:]).then_inc(s_seedg, 1)
            for k in range(KD):
                dve.wait_ge(s_xturn, k + 1)
                dve.tensor_copy(xt[:, k, :], res[:, k % 4, :]).then_inc(x_turned, 1)
            dve.wait_ge(s_mask, 3 + 2 * 6)
            for l in range(L):
                for which, (n, at0) in enumerate(((ROWS_A, 0), (ROWS_B, ROWS_A))):
                    dve.wait_ge(s_cturn, 2 * L)
                    c0 = (2 * l + which) * P
                    dve.tensor_copy(call[:, l, at0:at0 + n], pq[:, 0, c0:c0 + n]).then_inc(s_cc, 1)
            for l in range(L):
                dve.wait_ge(s_negA, l + 1)
                dve.tensor_scalar(hcall[:, l, 0, :], hcall[:, l, 0, :], -1.0, None, ALU.mult).then_inc(s_cc, 1)
            for l in range(L):
                for g in (G_F1POST, G_F2POST):
                    dve.wait_ge(s_cc, 3 * L)
                    dve.tensor_scalar(call[:, l, g:g + KD], call[:, l, g:g + KD], 0.5, None,
                                      ALU.mult).then_inc(s_cc, 1)
            dve.wait_ge(s_cc, 5 * L)
            dve.wait_ge(x_turned, KD)
            dve.wait_ge(s_seedg, 2)

            def diagonals(col, hi, lo, ready):
                split = st.done(dve.tensor_copy(col_h[:], col[:]))
                dve.tensor_tensor(hi[:], ident[:].unsqueeze(1).broadcast_to([P, NC, P]),
                                  col[:].unsqueeze(2).broadcast_to([P, NC, P]), ALU.mult).then_inc(ready, 1)
                st.need(split)
                st.link(dve.tensor_tensor(col_l[:], col[:], col_h[:].bitcast(F32), ALU.subtract))
                dve.tensor_tensor(lo[:], ident[:].unsqueeze(1).broadcast_to([P, NC, P]),
                                  col_l[:].unsqueeze(2).broadcast_to([P, NC, P]), ALU.mult).then_inc(ready, 1)

            def row(q, l, col):
                dve.wait_ge(root_ready, l * NST + q + 1)
                st.link(dve.reciprocal(col[:], rsq[:]))
                diagonals(col, diag_h, diag_l, diag_ready)

            def low(k, stage, gain, l):
                dve.wait_ge(xh_ready, l * NXS + stage * KD + k + 1)
                dve.scalar_tensor_tensor(xl[:, k, :], xt[:, k, :], cur[:, gain + k:gain + k + 1],
                                         xh[:, k, :].bitcast(F32), ALU.mult, ALU.subtract).then_inc(xs_ready, 1)

            def x_sum(k, stage, l):
                if k > 0:
                    n = stage * (KD - 1) + k
                    dve.wait_ge(sq_ready, l * NSQ + ((6 if stage == 3 else 2 * stage) * KD + k + 1))
                    if k > 1:
                        dve.wait_ge(xsum, l * NXQ + (n - 1))
                    dve.tensor_tensor(acc[:], acc[:], sqr[:, k % 2, :], ALU.add).then_inc(xsum, 1)

            def update(k, stage, l):
                n = stage * KD + k
                if k > 1:
                    dve.wait_ge(x_ready, l * NXR + (n - 1))
                dve.tensor_tensor(upd[:, k % 2, :], yg[:, k, :], bc[:, :], ALU.mult).then_inc(upd_ready, 1)

            def stage_inputs(stage, q, gain, l):
                dve.wait_ge(bc_full, l * NST + q + 2)
                for k in range(KD + 2):
                    if k < KD:
                        update(k, stage - 1, l)
                    if k >= 2:
                        low(k - 2, stage, gain, l)
                        x_sum(k - 2, stage, l)

            def block_scale(k, l):
                dve.scalar_tensor_tensor(xt[:, k, :], xt[:, k, :], gblk[:, k:k + 1], bc[:, :],
                                         ALU.mult, ALU.mult).then_inc(xn_ready, 1)

            def ffn(f, l):
                row([0, 4][f], l, rcol)
                with dve.Fori(0, KF // 2) as i:
                    dve.sem_clear(pair_step)
                    dve.wait_ge(rs_ready, l * 3 + (2 * f + 1))
                    ps = Steps(dve, pair_step)
                    for q in range(2):
                        n = i * 4 + (UBASE[f] + 2 * q + SLOTS)
                        dve.wait_ge(unit_done, l * UNITS + n + 1)
                        dve.tensor_tensor(gs[:, q, :], res[:, 2 * q, :], rs[:], ALU.mult).then_inc(gate_scaled, 1)
                        dve.wait_ge(unit_done, l * UNITS + n + 2)
                        dve.tensor_tensor(us[:, q, :], res[:, 2 * q + 1, :], rs[:], ALU.mult).then_inc(pair_free, 1)
                        dve.wait_ge(pair_free, l * NP + i * 2 + (f * KF + q + 1))
                        dve.wait_ge(silu_done, l * NP + i * 2 + (f * KF + q + 1))
                        ps.link(dve.tensor_tensor(hf[:], gs[:, q, :], us[:, q, :], ALU.mult))
                        ps.link(dve.tensor_scalar(hh[:, i * 2 + q, :], hf[:], 1.0, None, ALU.mult))
                        dve.tensor_tensor(hl[:, i * 2 + q, :], hf[:], hh[:, i * 2 + q, :].bitcast(F32),
                                          ALU.subtract).then_inc(h_ready, 1)
                dve.wait_ge(h_ready, l * NP + (f + 1) * KF)
                row([1, 5][f], l, rcol)

            with dve.Fori(0, L) as l:
                dve.sem_clear(dve_step)
                st.n = 0
                dve.tensor_copy(wabh[:], wabr[:, l]).then_inc(wab_ready, 1)
                dve.wait_ge(wab_ready, l * 2 + 1)
                dve.tensor_tensor(wabl[:], wabr[:, l], wabh[:].bitcast(F32), ALU.subtract).then_inc(wab_ready, 1)
                dve.tensor_copy(hcur[:], hcall[:, l]).then_inc(cur_ready, 1)
                dve.tensor_copy(cur[:], call[:, l, :]).then_inc(cur_ready, 1)
                dve.wait_ge(cur_ready, l * 2 + 2)
                dve.wait_ge(bc_full, l * NST + 1)
                for k in range(KD + 1):
                    if k < KD:
                        block_scale(k, l)
                    if k >= 1:
                        dve.wait_ge(xn_ready, l * KD + k)
                        low(k - 1, 0, G_F1PRE, l)
                        x_sum(k - 1, 0, l)
                dve.wait_ge(xn_ready, l * KD + KD)
                dve.tensor_copy(gblk[:], cur[:, G_BLOCK:G_BLOCK + KD]).then_inc(blk_done, 1)
                ffn(0, l)
                stage_inputs(1, 1, G_MPRE, l)
                row(2, l, rmix)
                st.link(dve.memset(pre[:, 0:PADG], 0.0))
                dve.wait_ge(rs_ready, l * 3 + 2)
                st.link(dve.memset(glu[:, :, 0:PADC], 0.0))

                next_tap, tap_mark = [0] * CT, [0] * CT

                def conv_taps(n, tiles=CT):
                    for _ in range(n):
                        t = min(range(tiles), key=lambda t: next_tap[t])
                        k = next_tap[t]
                        if k == CTAPS:
                            return
                        next_tap[t] += 1
                        w = cur[:, C_DW + k * CT + t:C_DW + k * CT + t + 1]
                        src = glu[:, t, k:k + T]
                        if k == 0:
                            ins = dve.tensor_scalar(u[:, t, :], src, w, cur[:, C_DWB + t:C_DWB + t + 1], ALU.mult,
                                                    ALU.add)
                        else:
                            st.need(tap_mark[t])
                            ins = dve.scalar_tensor_tensor(u[:, t, :], src, w, u[:, t, :], ALU.mult, ALU.add)
                        tap_mark[t] = st.done(ins)

                def hc(name):
                    return gt[name][:, 0:16].rearrange("p (h c) -> p h c", h=H)

                def gates_in():
                    dve.wait_ge(ab_full, l + 1)
                    st.link(dve.tensor_tensor(gt["ab"][:].rearrange("p (c j) -> p c j", c=NC),
                                              stat[:, 64:96].rearrange("p (c j) -> p c j", c=NC),
                                              rmix[:].unsqueeze(2).broadcast_to([P, NC, 2 * H]), ALU.mult))
                    abv = gt["ab"][:].rearrange("p (c j) -> p j c", c=NC)
                    st.link(dve.tensor_tensor(hc("xa"), abv[:, 0:H, :],
                                              hcur[:, 1, :].unsqueeze(2).broadcast_to([P, H, NC]), ALU.add))
                    st.link(dve.tensor_scalar(hc("eb"), abv[:, H:2 * H, :], -1.0, 87.0, ALU.mult, ALU.min))
                    dve.scalar_tensor_tensor(gt["na"][:, 0:16], gt["xa"][:, 0:16], -1.0, gt["xa"][:, 0:16], ALU.mult,
                                             ALU.min).then_inc(na_ready, 1)

                def gates_out():
                    dve.wait_ge(ln_ready, l * 2 + 2)
                    st.link(dve.scalar_tensor_tensor(gt["g"][:, 0:16], gt["xa"][:, 0:16], 0.0, gt["lnv"][:, 0:16],
                                                     ALU.max, ALU.add))
                    dve.tensor_tensor(hc("g"), hc("g"), hcur[:, 0, :].unsqueeze(2).broadcast_to([P, H, NC]),
                                      ALU.mult).then_inc(g_ready, 1)
                    st.link(dve.tensor_scalar(gt["eb"][:, 0:16], gt["eb"][:, 0:16], 1.0, None, ALU.add))
                    st.link(dve.reciprocal(gt["beta"][:, 0:16], gt["eb"][:, 0:16]))

                def per_token(name, h):
                    return gt[name][:, h * NC:(h + 1) * NC].unsqueeze(2).broadcast_to([P, NC, P])

                def decay_steps(h):
                    if h >= 2:
                        dve.wait_ge(e_full, l * H + h - 1)
                    else:
                        dve.wait_ge(g_ready, l + 1)
                        dve.wait_ge(act_kvqz, l * 4 * H + 3 * H)
                        dve.wait_ge(cv_ready, l * 3 * H + 3 * H)
                    dve.tensor_tensor(Wm[:, h % 2], upper[:].unsqueeze(1).broadcast_to([P, NC, P]),
                                      per_token("g", h), ALU.mult).then_inc(w_ready, 1)

                for r in range(MIX_IN_U):
                    bank = r % 4
                    dve.wait_ge(unit_done, l * UNITS + (MBASE + r + 1 + SLOTS))
                    if r < 2 * CT:
                        if r % 2 == 0:
                            dve.tensor_tensor(ga[:], res[:, bank, :], rs[:], ALU.mult).then_inc(mix_free, 1)
                        else:
                            t = r // 2
                            dve.tensor_tensor(gb[:], res[:, bank, :], rs[:], ALU.mult).then_inc(mix_free, 1)
                            dve.wait_ge(mix_free, l * MIX_IN_U + r + 1)
                            dve.wait_ge(sig_ready, l * CT + t + 1)
                            st.link(dve.tensor_tensor(glu[:, t, PADC:], ga[:], gb[:], ALU.mult))
                        if r >= 4:
                            conv_taps((7, 4)[r % 2], (r + 1) // 2)
                    elif r < 2 * CT + 3 * H:
                        n = r - 2 * CT
                        if n == 8:
                            dve.wait_ge(abT_full, l + 1)
                            dve.tensor_copy(abT[:], bc[0:2 * H, :]).then_inc(abT_ready, 1)
                        if n:
                            dve.wait_ge(cv_ready, l * 3 * H + n)
                        dve.tensor_tensor(pre[:, PADG:], res[:, bank, :], rs[:], ALU.mult).then_inc(mix_free, 1)
                        dve.wait_ge(mix_free, l * MIX_IN_U + r + 1)
                        which = (1, 2, 0)[n // H]
                        if n >= 2:
                            dve.wait_ge(act_kvqz, l * 4 * H + n - 1)
                        for k in range(GTAPS):
                            w = cur[:, C_QKV + k * 3 * H + which * H + n % H:C_QKV + k * 3 * H + which * H + n % H + 1]
                            src = pre[:, k:k + T]
                            if k == 0:
                                mark = st.done(dve.tensor_scalar(cacc[:, n % 2, :], src, w, None, ALU.mult))
                            else:
                                conv_taps(1)
                                st.need(mark)
                                ins = dve.scalar_tensor_tensor(cacc[:, n % 2, :], src, w, cacc[:, n % 2, :],
                                                               ALU.mult, ALU.add)
                                if k < GTAPS - 1:
                                    mark = st.done(ins)
                                else:
                                    ins.then_inc(cv_ready, 1)
                    else:
                        n = r - 2 * CT - 3 * H
                        dve.tensor_tensor(zT[:, n, :], res[:, bank, :], rs[:], ALU.mult).then_inc(mix_free, 1)
                        dve.wait_ge(mix_free, l * MIX_IN_U + r + 1)
                        if n == 0:
                            gates_in()
                        if n == 1:
                            gates_out()
                        if n == H - 1:
                            for h in range(2):
                                decay_steps(h)
                        conv_taps((7, 6, 4, 2)[n])
                dve.wait_ge(egc_ready, l + 1)
                st.link(dve.tensor_copy(gt["dgl"][:, 16:32], stat[:, 96:112]))
                dve.tensor_tensor(gt["dgl"][:, 0:16], stat[:, 112:128], gt["dgl"][:, 16:32],
                                  ALU.subtract).then_inc(dgl_ready, 1)

                for h in range(2, H):
                    decay_steps(h)
                conv_taps(9)
                dve.wait_ge(l2_root, l * 2 + 1)
                dve.reciprocal(gt["rk"][:, 0:16], gt["ss"][:, 0:16]).then_inc(rk_ready, 1)
                dve.wait_ge(rk_ready, l + 1)
                dve.wait_ge(ekd_ready, l + 1)
                dve.tensor_tensor(gt["kd"][:, 0:16], gt["rk"][:, 0:16], gt["ekd"][:, 0:16],
                                  ALU.mult).then_inc(kd_ready, 1)
                st.link(dve.tensor_tensor(gt["bk"][:, 0:16], gt["rk"][:, 0:16], gt["beta"][:, 0:16], ALU.mult))

                def heads(bank):
                    return res[:, bank, :].rearrange("p (c e) -> p c e", c=NC)

                for h in range(H):
                    dve.wait_ge(job_full, l * 5 * H + h + 1)
                    dve.tensor_tensor(vb[:, h], heads(h), per_token("beta", h), ALU.mult).then_inc(vt_free, 1)
                for h in range(H):
                    dve.wait_ge(job_full, l * 5 * H + H + h + 1)
                    dve.tensor_tensor(Um[:, h], heads(h), per_token("bk", h), ALU.mult).then_inc(kt_free, 1)
                for h in range(H):
                    dve.wait_ge(d_ready, l * H + h + 1)
                    dve.wait_ge(job_full, l * 5 * H + 3 * H + h + 1)
                    dve.tensor_tensor(Bm[:, h], heads(h), Dm[:, h], ALU.mult).then_inc(b_free, 1)
                dve.wait_ge(b_free, l * H + H)
                for h in range(H):
                    m = ident[:].rearrange("p (b two) -> p b two", two=2)[:, :, 0].unsqueeze(1).broadcast_to([P, NC, 64])
                    st.link(dve.tensor_tensor(pm[:, 4 * h:4 * h + 4, :],
                                              Bm[:, h].rearrange("p c (b two) -> p c b two", two=2)[:, :, :, 1], m,
                                              ALU.mult))
                    dve.wait_ge(ui_ready, l * H + h + 1)
                    odd = Um[:, h].rearrange("p c (b two) -> p c b two", two=2)[:, :, :, 1]
                    dve.tensor_tensor(odd, odd, pm[:, 4 * h:4 * h + 4, :], ALU.subtract).then_inc(u1_ready, 1)
                for h in range(H):
                    dve.wait_ge(job_full, l * 5 * H + 4 * H + h + 1)
                    dve.tensor_tensor(QK[:, h], heads(h), Dm[:, h], ALU.mult).then_inc(qk_free, 1)
                dve.wait_ge(l2_root, l * 2 + 2)
                st.link(dve.reciprocal(gt["rk"][:, 16:32], gt["ss"][:, 16:32]))
                st.link(dve.tensor_scalar(gt["rq8"][:, 0:16], gt["rk"][:, 16:32], float(DH) ** -0.5, None, ALU.mult))
                conv_taps(4)
                for n, s in enumerate(LEVELS[1:]):
                    for g in range(2):
                        dve.wait_ge(p_full, l * 12 + 2 * n + g + 1)
                        dve.tensor_tensor(pm[:, 8 * g:8 * g + 8, :], pq[:, g, :].rearrange("p (j e) -> p j e", j=8),
                                          lmask[:, n, :].unsqueeze(1).broadcast_to([P, 8, 64]),
                                          ALU.mult).then_inc(pm_ready, 1)
                        conv_taps(2)
                    if n == 5:
                        dve.wait_ge(mubc_full, l + 1)
                        for t in range(CT):
                            dve.tensor_tensor(u[:, t, :], u[:, t, :], bc[:, :], ALU.subtract).then_inc(uc_ready, 1)
                    if n == 4:
                        dve.wait_ge(usum_full, l + 1)
                        st.link(dve.tensor_scalar(rcol[:], stat[:, 0:NC], 1.0 / CW, None, ALU.mult))
                        diagonals(rcol, ldiag_h, ldiag_l, mu_ready)
                    for g in range(2):
                        dve.wait_ge(q_full, l * 12 + 2 * n + g + 1)
                        even = Tm[:, 2 * g:2 * g + 2].rearrange("p h c (b two e) -> p (h c b) two e", two=2,
                                                                e=s)[:, :, 0, :]
                        dve.tensor_tensor(even, even, pq[:, g, :].rearrange("p (b e) -> p b e", e=s),
                                          ALU.subtract).then_inc(t_upd, 1)
                        conv_taps(2)
                    if n == 3:
                        conv_taps(CT * CTAPS)
                        for t in range(CT):
                            st.need(tap_mark[t])
                        dve.sem_inc(u_ready, 1)

                def per_head(name, c):
                    return gt[name][:, 0:16].rearrange("p (h c) -> p h c", h=H)[:, :, c:c + 1].broadcast_to([P, H, P])

                def four(ap):
                    return ap.rearrange("p (h e) -> p h e", h=H)

                for c in range(NC):
                    if c == 0:
                        dve.wait_ge(vt_free, l * H + H)
                        dve.tensor_copy(Xd[:], vb[:, :, c, :]).then_inc(xd_ready, 1)
                    else:
                        dve.wait_ge(ks_full, l * (NC - 1) + c)
                        dve.wait_ge(vn_full, l * NC + c)
                        st.link(dve.tensor_tensor(Xd[:], four(pq[:, 0, :]), per_head("egc", c), ALU.mult))
                        dve.tensor_tensor(Xd[:], vb[:, :, c, :], Xd[:], ALU.subtract).then_inc(xd_ready, 1)
                        mark = st.done(dve.tensor_tensor(sd[:], St[:], per_head("egl", c), ALU.mult))
                        if c == 2:
                            dve.wait_ge(uroot, l + 1)
                            st.link(dve.reciprocal(rcol[:], rsq[:]))
                            diagonals(rcol, ldiag_h, ldiag_l, udiag)
                        if c == 3:
                            dve.wait_ge(uvbc_full, l + 1)
                            dve.wait_ge(uc_ready, l * CT + CT)
                            for t in range(CT):
                                dve.tensor_tensor(u[:, t, :], u[:, t, :], bc[:, :], ALU.mult).then_inc(un_ready, 1)
                    dve.wait_ge(su_full, l * NC + c + 1)
                    if c == 0:
                        dve.tensor_copy(St[:], four(res[:, 0, :])).then_inc(s_ready, 1)
                    else:
                        st.need(mark)
                        dve.tensor_tensor(St[:], sd[:], four(res[:, 0, :]), ALU.add).then_inc(s_ready, 1)
                    dve.wait_ge(o_full, l * NC + c + 1)
                    if c == 0:
                        dve.tensor_tensor(on[:, :, c, :], four(res[:, 3, :]), per_head("rq8", c),
                                          ALU.mult).then_inc(o_free, 1)
                    else:
                        st.link(dve.tensor_tensor(oq[:], four(res[:, 2, :]), per_head("egc", c), ALU.mult))
                        st.link(dve.tensor_tensor(oq[:], oq[:], four(res[:, 3, :]), ALU.add))
                        dve.tensor_tensor(on[:, :, c, :], oq[:], per_head("rq8", c), ALU.mult).then_inc(o_free, 1)
                for t in range(CT):
                    dve.wait_ge(uh_ready, l * CT + t + 1)
                    dve.tensor_tensor(cl[:, H + t, :], u[:, t, :], ch[:, H + t, :].bitcast(F32),
                                      ALU.subtract).then_inc(cmix_ready, 1)
                dve.wait_ge(o_free, l * NC + NC)
                for h in range(H):
                    dve.wait_ge(osq_ready, l * H + h + 1)
                    dve.tensor_reduce(gt["oss"][:, h * NC:(h + 1) * NC],
                                      osq[:, h, :].rearrange("p (c e) -> p c e", c=NC), AX_X,
                                      ALU.add).then_inc(oss_ready, 1)
                dve.wait_ge(oroot, l + 1)
                st.link(dve.reciprocal(gt["oss"][:, 0:16], gt["orr"][:, 0:16]))
                for h in range(H):
                    dve.tensor_tensor(on[:, h], on[:, h], per_token("oss", h), ALU.mult).then_inc(on_ready, 1)

                def head_low(h):
                    dve.wait_ge(gate_hi, l * H + h + 1)
                    dve.tensor_tensor(cl[:, h, :], Wm[:, h % 2].rearrange("p c t -> p (c t)"),
                                      ch[:, h, :].bitcast(F32), ALU.subtract).then_inc(gm_ready, 1)

                for h in range(H):
                    dve.wait_ge(ot_full, l * H + h + 1)
                    if h == 0:
                        dve.wait_ge(act_kvqz, l * 4 * H + 4 * H)
                    gf = Wm[:, h % 2].rearrange("p c t -> p (c t)")
                    if h >= 2:
                        dve.wait_ge(gm_ready, l * H + h - 1)
                    dve.scalar_tensor_tensor(gf, turned[h], cur[:, C_OUT:C_OUT + 1], zT[:, h, :], ALU.mult,
                                             ALU.mult).then_inc(gh_ready, 1)
                    if h >= 1:
                        head_low(h - 1)
                head_low(H - 1)
                row(3, l, rcol)
                stage_inputs(2, 3, G_F2PRE, l)
                ffn(1, l)
                dve.wait_ge(bc_full, l * NST + 7)
                for k in range(KD + 2):
                    if k < KD:
                        update(k, 2, l)
                    if k >= 2:
                        x_sum(k - 2, 3, l)
                row(6, l, rcol)
                dve.wait_ge(blk_done, l + 1)
            dve.wait_ge(bc_full, L * NST + 1)
            for k in range(KD):
                block_scale(k, L)
    return nc


_INS = ["x", "ffn1_norm_pre", "ffn1_w_in", "ffn1_w_out", "ffn1_norm_post", "mix_norm_pre", "mix_w_in",
        "gdn_conv_w", "gdn_a_log", "gdn_dt_bias", "gdn_out_norm", "cm_dw_w", "cm_dw_b", "cm_ln_g", "cm_ln_b",
        "mix_w_out", "mix_norm_post", "ffn2_norm_pre", "ffn2_w_in", "ffn2_w_out", "ffn2_norm_post", "block_norm"]


def kernel(**inputs):
    import numpy as _np
    import concourse.bacc as _bacc
    from concourse import mybir as _mybir
    from concourse.bass_utils import run_bass_kernel_spmd as _run

    nc = _bacc.Bacc("TRN2", target_bir_lowering=False, num_devices=1)
    arrays, args = {}, []
    for name in _INS:
        a = _np.ascontiguousarray(inputs[name])
        arrays[f"in_{name}"] = a
        args.append(nc.dram_tensor(f"in_{name}", a.shape, _mybir.dt.from_np(a.dtype), kind="ExternalInput").ap())
    out = nc.dram_tensor("out_dram", arrays["in_x"].shape, _mybir.dt.float32, kind="ExternalOutput").ap()
    trunk_kernel(nc, *args, out)
    r = _run(nc, [arrays], core_ids=[0])
    return r.results[0]["out_dram"]
```
